# Optimizing a Trainium2 kernel written in Bass

```python
import jax, jax.numpy as jnp
from jax import lax
import numpy as np
import math

D_MODEL = 1024
BATCH = 1
SEQ = 256
DEPTH = 2

GRID_W = 64
CTX_LEN = 256
H_M = 4
DH_M = 128
M_W = H_M * DH_M
H_A = 8
H_KV = 2
DH_A = 64
A_Q = H_A * DH_A
A_KV = H_KV * DH_A
GQA_GROUP = H_A // H_KV
WINDOW = 128
WIN_BLOCK = 128
ROPE_THETA = 10000.0
AB_WIDTHS = (M_W, M_W, M_W, M_W, 4 * H_M, A_Q, A_KV, A_KV)
MIX_W = M_W + A_Q
H_C = 4
DK_C = 128
DV_C = 256
C_K = H_C * DK_C
C_V = H_C * DV_C
GATE_RANK = 16
GATE_TAU = 16.0
C_WIDTHS = (C_K, C_K, C_V, C_V, 2 * GATE_RANK)
CHUNK = 64
N_KEYS = 128
N_EXPERTS = N_KEYS * N_KEYS
PEER_HEADS = 8
PEER_TOPK = 16
PEER_KEY_DIM = 256
PEER_HALF = PEER_KEY_DIM // 2
PEER_CHUNK = 128
N_EVEN = (DEPTH + 1) // 2
N_ODD = DEPTH // 2
DEEPNORM_ALPHA = (2 * DEPTH) ** 0.25
DEEPNORM_BETA = (8 * DEPTH) ** -0.25
LN_EPS = 1e-5


def _layernorm(x, w, b):
    xf = x.astype(jnp.float32)
    mu = xf.mean(-1, keepdims=True)
    var = jnp.mean(jnp.square(xf - mu), -1, keepdims=True)
    return ((xf - mu) * lax.rsqrt(var + LN_EPS)).astype(x.dtype) * w + b

def _split(a, widths):
    idx = np.cumsum(widths)[:-1].tolist()
    return jnp.split(a, idx, axis=-1)

def _heads(a, h):
    b, s = a.shape[:2]
    return a.reshape(b, s, h, -1).transpose(0, 2, 1, 3)

def _head_norm(h, w):
    hf = h.astype(jnp.float32)
    hf = hf * lax.rsqrt(jnp.mean(hf * hf, -1, keepdims=True) + LN_EPS)
    b, nh, s, d = h.shape
    return hf.transpose(0, 2, 1, 3).reshape(b, s, nh * d) * w

def _to_chunks(a):
    b, h, s = a.shape[:3]
    a = a.reshape((b, h, s // CHUNK, CHUNK) + a.shape[3:])
    return jnp.moveaxis(a, 2, 0)

def _from_chunks(a):
    a = jnp.moveaxis(a, 0, 2)
    return a.reshape(a.shape[:2] + (-1,) + a.shape[4:])

def _mlstm_scan(q, k, v, log_i, log_f, state):
    causal = jnp.tril(jnp.ones((CHUNK, CHUNK), bool))

    def step(carry, inp):
        c_st, n_st, m_st = carry
        qc, kc, vc, li, lf = inp
        cum = jnp.cumsum(lf, axis=-1)
        dmat = cum[..., :, None] - cum[..., None, :] + li[..., None, :]
        dmat = jnp.where(causal, dmat, -jnp.inf)
        m_inter = cum + m_st[..., None]
        m_t = jnp.maximum(m_inter, dmat.max(-1))
        w = jnp.exp(dmat - m_t[..., None]) * jnp.einsum('bhtd,bhsd->bhts', qc, kc)
        a_inter = jnp.exp(m_inter - m_t)
        num = a_inter[..., None] * jnp.einsum('bhtd,bhde->bhte', qc, c_st) + jnp.einsum('bhts,bhse->bhte', w, vc)
        den = a_inter * jnp.einsum('bhtd,bhd->bht', qc, n_st) + w.sum(-1)
        h = num / jnp.maximum(jnp.abs(den), jnp.exp(-m_t))[..., None]
        total = cum[..., -1]
        decay_s = total[..., None] - cum + li
        m_new = jnp.maximum(total + m_st, decay_s.max(-1))
        ws = jnp.exp(decay_s - m_new[..., None])
        a_st = jnp.exp(total + m_st - m_new)
        c_st = a_st[..., None, None] * c_st + jnp.einsum('bhs,bhsd,bhse->bhde', ws, kc, vc)
        n_st = a_st[..., None] * n_st + jnp.einsum('bhs,bhsd->bhd', ws, kc)
        return (c_st, n_st, m_new), h

    state, hs = lax.scan(step, state, tuple(_to_chunks(a) for a in (q, k, v, log_i, log_f)))
    return _from_chunks(hs), state

def _gla_scan(q, k, v, log_a, state):
    causal = jnp.tril(jnp.ones((CHUNK, CHUNK), bool))

    def step(st, inp):
        qc, kc, vc, la = inp
        cum = jnp.cumsum(la, axis=2)
        rel = cum[:, :, :, None, :] - cum[:, :, None, :, :]
        rel = jnp.where(causal[:, :, None], rel, -jnp.inf)
        scores = jnp.einsum('bhtk,bhsk,bhtsk->bhts', qc, kc, jnp.exp(rel))
        out = jnp.einsum('bhtk,bhkv->bhtv', qc * jnp.exp(cum), st) + jnp.einsum('bhts,bhsv->bhtv', scores, vc)
        total = cum[:, :, -1:, :]
        st = jnp.exp(total[:, :, 0, :, None]) * st + jnp.einsum('bhsk,bhsv->bhkv', kc * jnp.exp(total - cum), vc)
        return st, out

    state, outs = lax.scan(step, state, tuple(_to_chunks(a) for a in (q, k, v, log_a)))
    return _from_chunks(outs), state

def _directional(scan_fn, ctx_seq, lat_seq, init, reverse):
    if reverse:
        ctx_seq = tuple(jnp.flip(a, 2) for a in ctx_seq)
        lat_seq = tuple(jnp.flip(a, 2) for a in lat_seq)
    h_ctx, state = scan_fn(*ctx_seq, init)
    h_lat, _ = scan_fn(*lat_seq, state)
    if reverse:
        h_ctx, h_lat = jnp.flip(h_ctx, 2), jnp.flip(h_lat, 2)
    return h_ctx, h_lat

def _axial_rope(s):
    rows = s // GRID_W
    row = jnp.repeat(jnp.arange(rows), GRID_W).astype(jnp.float32)
    col = jnp.tile(jnp.arange(GRID_W), rows).astype(jnp.float32)
    n_freq = DH_A // 4
    inv = ROPE_THETA ** (-jnp.arange(n_freq, dtype=jnp.float32) / n_freq)
    ang = jnp.concatenate([row[:, None] * inv, col[:, None] * inv], -1)
    return jnp.cos(ang), jnp.sin(ang)

def _rope(x, cos, sin):
    xf = x.astype(jnp.float32)
    x1, x2 = xf[..., 0::2], xf[..., 1::2]
    c = cos[None, :, None, :]
    sn = sin[None, :, None, :]
    return jnp.stack([x1 * c - x2 * sn, x1 * sn + x2 * c], -1).reshape(x.shape).astype(x.dtype)

def _window_attention(q, k, v, k_ctx, v_ctx, sink):
    b, s = q.shape[:2]
    nb = s // WIN_BLOCK
    lc = k_ctx.shape[1]
    qb = jnp.moveaxis(q.reshape(b, nb, WIN_BLOCK, H_KV, GQA_GROUP, DH_A), 1, 0)

    def bands(a):
        ap = jnp.pad(a, ((0, 0), (WIN_BLOCK, WIN_BLOCK), (0, 0), (0, 0))).reshape(b, nb + 2, WIN_BLOCK, H_KV, DH_A)
        return jnp.moveaxis(jnp.concatenate([ap[:, :-2], ap[:, 1:-1], ap[:, 2:]], 2), 1, 0)

    kw, vw = bands(k), bands(v)
    qi = jnp.arange(WIN_BLOCK)[:, None]
    kj = jnp.arange(3 * WIN_BLOCK)[None, :]
    key_pos = jnp.arange(nb)[:, None, None] * WIN_BLOCK + kj - WIN_BLOCK
    valid = (jnp.abs(kj - WIN_BLOCK - qi) <= WINDOW) & (key_pos >= 0) & (key_pos < s)
    scale = DH_A ** -0.5
    sink_l = sink.reshape(H_KV, GQA_GROUP).astype(jnp.float32)

    def block(args):
        qn, kn, vn, mask = args
        s_ctx = jnp.einsum('bqhgd,bchd->bhgqc', qn, k_ctx).astype(jnp.float32) * scale
        s_win = jnp.einsum('bqhgd,bkhd->bhgqk', qn, kn).astype(jnp.float32) * scale
        s_win = jnp.where(mask, s_win, -jnp.inf)
        sink_col = jnp.broadcast_to(sink_l[None, :, :, None, None], s_ctx.shape[:-1] + (1,))
        p = jax.nn.softmax(jnp.concatenate([sink_col, s_ctx, s_win], -1), -1).astype(qn.dtype)
        return (jnp.einsum('bhgqc,bchd->bqhgd', p[..., 1:1 + lc], v_ctx)
                + jnp.einsum('bhgqk,bkhd->bqhgd', p[..., 1 + lc:], vn))

    out = lax.map(block, (qb, kw, vw, valid))
    return jnp.moveaxis(out, 0, 1).reshape(b, s, H_A, DH_A)

def _context_attention(q, k, v, sink):
    b, lc = q.shape[:2]
    qg = q.reshape(b, lc, H_KV, GQA_GROUP, DH_A)
    sc = jnp.einsum('bqhgd,bkhd->bhgqk', qg, k).astype(jnp.float32) * DH_A ** -0.5
    sink_col = jnp.broadcast_to(sink.reshape(H_KV, GQA_GROUP).astype(jnp.float32)[None, :, :, None, None],
                                sc.shape[:-1] + (1,))
    p = jax.nn.softmax(jnp.concatenate([sink_col, sc], -1), -1)[..., 1:].astype(q.dtype)
    return jnp.einsum('bhgqk,bkhd->bqhgd', p, v).reshape(b, lc, H_A, DH_A)

def _ab_streams(h, w_in, gate_b):
    q_m, k_m, v_m, o_m, g_m, q_a, k_a, v_a = _split(h @ w_in, AB_WIDTHS)
    b, s = h.shape[:2]
    g = g_m.reshape(b, s, 2, 2, H_M).astype(jnp.float32) + gate_b.astype(jnp.float32)
    mlstm = (_heads(q_m, H_M).astype(jnp.float32),
             _heads(k_m, H_M).astype(jnp.float32) * DH_M ** -0.5,
             _heads(v_m, H_M).astype(jnp.float32))
    gates = [(g[:, :, d, 0].transpose(0, 2, 1), jax.nn.log_sigmoid(g[:, :, d, 1]).transpose(0, 2, 1))
             for d in range(2)]
    attn = (q_a.reshape(b, s, H_A, DH_A), k_a.reshape(b, s, H_KV, DH_A), v_a.reshape(b, s, H_KV, DH_A))
    return mlstm, gates, o_m, attn

def _merge_ab(m, o, a, norm_w, w_out):
    hm = _head_norm(m, norm_w).astype(o.dtype) * jax.nn.sigmoid(o)
    cat = jnp.concatenate([hm, a.reshape(a.shape[0], a.shape[1], A_Q)], -1)
    return cat @ w_out

def _mixer_ab(hl, hc, w_in, gate_b, norm_w, sink, w_out, ctx_out):
    ml, gl, ol, (ql, kl, vl) = _ab_streams(hl, w_in, gate_b)
    mc, gc, oc, (qc, kc, vc) = _ab_streams(hc, w_in, gate_b)
    b = hl.shape[0]
    init = (jnp.zeros((b, H_M, DH_M, DH_M), jnp.float32), jnp.zeros((b, H_M, DH_M), jnp.float32),
            jnp.zeros((b, H_M), jnp.float32))
    outs = [_directional(_mlstm_scan, mc + gc[d], ml + gl[d], init, d == 1) for d in range(2)]
    cos, sin = _axial_rope(hl.shape[1])
    a_lat = _window_attention(_rope(ql, cos, sin), _rope(kl, cos, sin), vl, kc, vc, sink)
    y_lat = _merge_ab(outs[0][1] + outs[1][1], ol, a_lat, norm_w, w_out)
    if not ctx_out:
        return y_lat, None
    y_ctx = _merge_ab(outs[0][0] + outs[1][0], oc, _context_attention(qc, kc, vc, sink), norm_w, w_out)
    return y_lat, y_ctx

def _c_streams(h, w_in, gate_up, gate_b):
    q, k, v, g, low = _split(h @ w_in, C_WIDTHS)
    b, s = h.shape[:2]
    qkv = (_heads(q, H_C).astype(jnp.float32) * DK_C ** -0.5,
           _heads(k, H_C).astype(jnp.float32),
           _heads(v, H_C).astype(jnp.float32))
    low = low.reshape(b, s, 2, GATE_RANK)
    log_a = [_heads(jax.nn.log_sigmoid((low[:, :, d] @ gate_up[d] + gate_b[d]).astype(jnp.float32)) / GATE_TAU, H_C)
             for d in range(2)]
    return qkv, log_a, g

def _merge_c(h, g, norm_w, w_out):
    return (_head_norm(h, norm_w).astype(g.dtype) * jax.nn.silu(g)) @ w_out

def _mixer_c(hl, hc, w_in, gate_up, gate_b, norm_w, w_out, ctx_out):
    sl, al, gl = _c_streams(hl, w_in, gate_up, gate_b)
    sc, ac, gc = _c_streams(hc, w_in, gate_up, gate_b)
    init = jnp.zeros((hl.shape[0], H_C, DK_C, DV_C), jnp.float32)
    outs = [_directional(_gla_scan, sc + (ac[d],), sl + (al[d],), init, d == 1) for d in range(2)]
    y_lat = _merge_c(outs[0][1] + outs[1][1], gl, norm_w, w_out)
    if not ctx_out:
        return y_lat, None
    return y_lat, _merge_c(outs[0][0] + outs[1][0], gc, norm_w, w_out)

def _peer(h, wq, keys, u, v):
    shape = h.shape
    tokens = h.reshape(-1, PEER_CHUNK, shape[-1])

    def block(hb):
        tc = hb.shape[0]
        q = (hb @ wq).reshape(tc, PEER_HEADS, 2, PEER_HALF)
        s = jnp.einsum('thpk,hpnk->thpn', q, keys)
        s_top, i_top = lax.top_k(s, PEER_TOPK)
        cand = s_top[:, :, 0, :, None] + s_top[:, :, 1, None, :]
        cid = i_top[:, :, 0, :, None] * N_KEYS + i_top[:, :, 1, None, :]
        best, pos = lax.top_k(cand.reshape(tc, PEER_HEADS, -1), PEER_TOPK)
        eid = jnp.take_along_axis(cid.reshape(tc, PEER_HEADS, -1), pos, -1)
        g = jax.nn.softmax(best.astype(jnp.float32), -1).astype(hb.dtype)
        act = jax.nn.gelu(jnp.einsum('td,thed->the', hb, u[eid]), approximate=False)
        return jnp.einsum('the,thed->td', g * act, v[eid])

    return lax.map(block, tokens).reshape(shape)

def first_inputs(seed: int = 0) -> dict:
    key = jax.random.key(seed)
    ks = jax.random.split(key, 26)
    f32 = jnp.float32

    def nrm(k, shape, s):
        return jax.random.normal(k, shape, f32) * s

    d = D_MODEL
    f_bias = 3.0 + 3.0 * jnp.arange(H_M, dtype=f32) / (H_M - 1)
    gate_offset = jnp.stack([jnp.zeros((H_M,), f32), f_bias])[None, None]
    return {
        "x": nrm(ks[0], (BATCH, SEQ, d), 1.0),
        "c": nrm(ks[1], (BATCH, d), 1.0),
        "ctx": nrm(ks[2], (BATCH, CTX_LEN, d), 1.0),
        "c_ctx": nrm(ks[3], (d,), 1.0),
        "w_mod": nrm(ks[4], (DEPTH, d, 6 * d), 0.5 * d ** -0.5),
        "b_mod": nrm(ks[5], (DEPTH, 6 * d), 0.02),
        "ln_w": 1.0 + nrm(ks[6], (DEPTH, 2, d), 0.02),
        "ln_b": nrm(ks[7], (DEPTH, 2, d), 0.02),
        "ab_w_in": nrm(ks[8], (N_EVEN, d, sum(AB_WIDTHS)), d ** -0.5),
        "ab_gate_b": nrm(ks[9], (N_EVEN, 2, 2, H_M), 0.1) + gate_offset,
        "ab_norm_w": 1.0 + nrm(ks[10], (N_EVEN, M_W), 0.02),
        "ab_sink": nrm(ks[11], (N_EVEN, H_A), 0.5),
        "ab_w_out": nrm(ks[12], (N_EVEN, MIX_W, d), DEEPNORM_BETA * MIX_W ** -0.5),
        "gla_w_in": nrm(ks[13], (N_ODD, d, sum(C_WIDTHS)), d ** -0.5),
        "gla_gate_up": nrm(ks[14], (N_ODD, 2, GATE_RANK, C_K), GATE_RANK ** -0.5),
        "gla_gate_b": 1.0 + nrm(ks[15], (N_ODD, 2, C_K), 0.5),
        "gla_norm_w": 1.0 + nrm(ks[16], (N_ODD, C_V), 0.02),
        "gla_w_out": nrm(ks[17], (N_ODD, C_V, d), DEEPNORM_BETA * C_V ** -0.5),
        "peer_wq": nrm(ks[18], (DEPTH, d, PEER_HEADS * PEER_KEY_DIM), d ** -0.5),
        "peer_keys": nrm(ks[19], (DEPTH, PEER_HEADS, 2, N_KEYS, PEER_HALF), PEER_HALF ** -0.5),
        "peer_u": nrm(ks[20], (DEPTH, N_EXPERTS, d), d ** -0.5),
        "peer_v": nrm(ks[21], (DEPTH, N_EXPERTS, d), DEEPNORM_BETA * (PEER_HEADS * PEER_TOPK) ** -0.5),
    }

def first_block(x, c, ctx, c_ctx, w_mod, b_mod, ln_w, ln_b, ab_w_in, ab_gate_b, ab_norm_w, ab_sink, ab_w_out,
              gla_w_in, gla_gate_up, gla_gate_b, gla_norm_w, gla_w_out, peer_wq, peer_keys, peer_u, peer_v):
    for layer in range(DEPTH):
        last = layer == DEPTH - 1
        j = layer // 2
        mod_l = jax.nn.silu(c) @ w_mod[layer] + b_mod[layer]
        mod_c = jax.nn.silu(c_ctx) @ w_mod[layer] + b_mod[layer]
        sh1, sc1, g1, sh2, sc2, g2 = jnp.split(mod_l[:, None, :], 6, axis=-1)
        csh1, csc1, cg1, csh2, csc2, cg2 = jnp.split(mod_c, 6)
        hl = x * (1.0 + sc1) + sh1
        hc = ctx * (1.0 + csc1) + csh1
        if layer % 2 == 0:
            y_lat, y_ctx = _mixer_ab(hl, hc, ab_w_in[j], ab_gate_b[j], ab_norm_w[j], ab_sink[j], ab_w_out[j], not last)
        else:
            y_lat, y_ctx = _mixer_c(hl, hc, gla_w_in[j], gla_gate_up[j], gla_gate_b[j], gla_norm_w[j], gla_w_out[j],
                                    not last)
        x = _layernorm(DEEPNORM_ALPHA * x + g1 * y_lat, ln_w[layer, 0], ln_b[layer, 0])
        f_lat = _peer(x * (1.0 + sc2) + sh2, peer_wq[layer], peer_keys[layer], peer_u[layer], peer_v[layer])
        x = _layernorm(DEEPNORM_ALPHA * x + g2 * f_lat, ln_w[layer, 1], ln_b[layer, 1])
        if not last:
            ctx = _layernorm(DEEPNORM_ALPHA * ctx + cg1 * y_ctx, ln_w[layer, 0], ln_b[layer, 0])
            f_ctx = _peer(ctx * (1.0 + csc2) + csh2, peer_wq[layer], peer_keys[layer], peer_u[layer], peer_v[layer])
            ctx = _layernorm(DEEPNORM_ALPHA * ctx + cg2 * f_ctx, ln_w[layer, 1], ln_b[layer, 1])
    return x


RMS_EPS = 1e-6
DN_WIDTH = D_MODEL // 2
DN_DHEAD = 128
DN_HEADS = DN_WIDTH // DN_DHEAD
DN_CONV = 4
SA_WIDTH = D_MODEL // 4
SA_DHEAD = 64
SA_HEADS = SA_WIDTH // SA_DHEAD
SA_DKV = SA_DHEAD
IDX_HEADS = 4
IDX_DHEAD = 64
IDX_TOPK_MAX = 256
Q_BLOCK = 128
HG_WIDTH = D_MODEL // 4
HG_DHEAD = 64
HG_HEADS = HG_WIDTH // HG_DHEAD
D_MIX = DN_WIDTH + SA_WIDTH + HG_WIDTH
D_FF = 2816
FFN_CONV = 3

SPLIT_SIZES = (DN_WIDTH, DN_WIDTH, DN_WIDTH, DN_WIDTH, DN_HEADS, DN_HEADS,
               SA_WIDTH, SA_DKV, SA_DKV, IDX_HEADS * IDX_DHEAD, IDX_DHEAD, IDX_HEADS,
               HG_WIDTH, HG_WIDTH, HG_WIDTH, HG_WIDTH)
D_IN = sum(SPLIT_SIZES)
SPLIT_POINTS = tuple(int(p) for p in np.cumsum(SPLIT_SIZES)[:-1])


def rmsnorm(x, g):
    xf = x.astype(jnp.float32)
    y = xf * lax.rsqrt(jnp.mean(xf * xf, axis=-1, keepdims=True) + RMS_EPS)
    return (y * g.astype(jnp.float32)).astype(x.dtype)

def l2norm(x):
    return x * lax.rsqrt(jnp.sum(x * x, axis=-1, keepdims=True) + 1e-6)

def causal_depthwise_conv(x, w):
    K, C = w.shape
    return lax.conv_general_dilated(x, w[:, None, :].astype(x.dtype), window_strides=(1,),
                                    padding=[(K - 1, 0)],
                                    dimension_numbers=('NWC', 'WIO', 'NWC'),
                                    feature_group_count=C)

def to_chunks(t, n_heads, d_head):
    B, S = t.shape[:2]
    return t.reshape(B, S // CHUNK, CHUNK, n_heads, d_head).transpose(0, 3, 1, 2, 4)

def gate_chunks(t):
    B, S, H = t.shape
    return t.reshape(B, S // CHUNK, CHUNK, H).transpose(0, 3, 1, 2)

def from_chunks(o):
    N, B, H, C, d = o.shape
    return o.transpose(1, 0, 3, 2, 4).reshape(B, N * C, H, d)

def gated_deltanet(q, k, v, z, b, a, conv_w, a_log, dt_bias, norm_g):
    dtype = q.dtype
    Bsz, S, _ = q.shape
    qkv = jax.nn.silu(causal_depthwise_conv(jnp.concatenate([q, k, v], axis=-1), conv_w))
    q, k, v = jnp.split(qkv.astype(jnp.float32), 3, axis=-1)
    q = l2norm(to_chunks(q, DN_HEADS, DN_DHEAD)) * (DN_DHEAD ** -0.5)
    k = l2norm(to_chunks(k, DN_HEADS, DN_DHEAD))
    v = to_chunks(v, DN_HEADS, DN_DHEAD)
    beta = gate_chunks(jax.nn.sigmoid(b.astype(jnp.float32)))
    g = -jnp.exp(a_log.astype(jnp.float32)) * jax.nn.softplus(
        a.astype(jnp.float32) + dt_bias.astype(jnp.float32))
    G = jnp.cumsum(gate_chunks(g), axis=-1)
    causal = jnp.tril(jnp.ones((CHUNK, CHUNK), bool))
    strict = jnp.tril(jnp.ones((CHUNK, CHUNK), bool), k=-1)
    decay = jnp.exp(jnp.where(causal, G[..., :, None] - G[..., None, :], -jnp.inf))
    kk = jnp.einsum('bhnck,bhnsk->bhncs', k, k)
    M = jnp.where(strict, beta[..., :, None] * kk * decay, 0.0)
    eye = jnp.eye(CHUNK, dtype=jnp.float32)
    T = lax.linalg.triangular_solve(eye + M, jnp.broadcast_to(eye, M.shape),
                                    left_side=True, lower=True, unit_diagonal=True)
    u0 = jnp.einsum('bhncs,bhnsv->bhncv', T, beta[..., None] * v)
    wk = jnp.einsum('bhncs,bhnsk->bhnck', T, (beta * jnp.exp(G))[..., None] * k)
    qk = jnp.einsum('bhnck,bhnsk->bhncs', q, k) * decay
    q_dec = q * jnp.exp(G)[..., None]
    k_dec = k * jnp.exp(G[..., -1:] - G)[..., None]
    g_last = jnp.exp(G[..., -1])

    def step(state, inp):
        u0_c, w_c, qk_c, qd_c, kd_c, gl_c = inp
        u = u0_c - jnp.einsum('bhck,bhkv->bhcv', w_c, state)
        o = jnp.einsum('bhck,bhkv->bhcv', qd_c, state) + jnp.einsum('bhcs,bhsv->bhcv', qk_c, u)
        state = state * gl_c[..., None, None] + jnp.einsum('bhck,bhcv->bhkv', kd_c, u)
        return state, o

    xs = tuple(jnp.moveaxis(t, 2, 0) for t in (u0, wk, qk, q_dec, k_dec, g_last))
    s0 = jnp.zeros((Bsz, DN_HEADS, DN_DHEAD, DN_DHEAD), jnp.float32)
    _, o = lax.scan(step, s0, xs)
    o = rmsnorm(from_chunks(o), norm_g)
    o = o * jax.nn.silu(z.astype(jnp.float32).reshape(Bsz, S, DN_HEADS, DN_DHEAD))
    return o.reshape(Bsz, S, DN_WIDTH).astype(dtype)

def dsa_attention(q, k, v, qi, ki, wi):
    dtype = q.dtype
    Bsz, S, _ = q.shape
    nb = S // Q_BLOCK
    topk = min(IDX_TOPK_MAX, S // 4)
    f32 = jnp.float32
    qb_all = q.astype(f32).reshape(Bsz, nb, Q_BLOCK, SA_HEADS, SA_DHEAD).transpose(1, 0, 2, 3, 4)
    qib_all = qi.astype(f32).reshape(Bsz, nb, Q_BLOCK, IDX_HEADS, IDX_DHEAD).transpose(1, 0, 2, 3, 4)
    wib_all = (wi.astype(f32) * (IDX_HEADS ** -0.5 * IDX_DHEAD ** -0.5)).reshape(
        Bsz, nb, Q_BLOCK, IDX_HEADS).transpose(1, 0, 2, 3)
    k = k.astype(f32)
    v = v.astype(f32)
    ki = ki.astype(f32)
    key_chunk = jnp.arange(S) // CHUNK
    gather = jax.vmap(lambda t, idx: t[idx])

    def block(args):
        qb, qib, wib, blk = args
        q_chunk = (blk * Q_BLOCK + jnp.arange(Q_BLOCK)) // CHUNK
        score = jnp.einsum('bqhs,bqh->bqs',
                           jax.nn.relu(jnp.einsum('bqhd,bsd->bqhs', qib, ki)), wib)
        admissible = key_chunk[None, :] <= q_chunk[:, None]
        score = jnp.where(admissible[None], score, -jnp.inf)
        _, idx = lax.top_k(score, topk)
        k_sel = gather(k, idx)
        v_sel = gather(v, idx)
        valid = key_chunk[idx] <= q_chunk[None, :, None]
        logits = jnp.einsum('bqhd,bqkd->bqhk', qb, k_sel) * (SA_DHEAD ** -0.5)
        logits = jnp.where(valid[:, :, None, :], logits, -jnp.inf)
        p = jax.nn.softmax(logits, axis=-1)
        return jnp.einsum('bqhk,bqkd->bqhd', p, v_sel)

    o = lax.map(block, (qb_all, qib_all, wib_all, jnp.arange(nb)))
    return o.transpose(1, 0, 2, 3, 4).reshape(Bsz, S, SA_WIDTH).astype(dtype)

def hgrn2(q, f, i, g, lb, norm_g):
    dtype = q.dtype
    Bsz, S, _ = q.shape
    f32 = jnp.float32
    fg = lb + (1.0 - lb) * jax.nn.sigmoid(f.astype(f32))
    qc = to_chunks(jax.nn.silu(q.astype(f32)), HG_HEADS, HG_DHEAD)
    kc = to_chunks(1.0 - fg, HG_HEADS, HG_DHEAD)
    vc = to_chunks(i.astype(f32), HG_HEADS, HG_DHEAD)
    Bc = jnp.cumsum(to_chunks(jnp.log(fg), HG_HEADS, HG_DHEAD), axis=-2)
    q_dec = qc * jnp.exp(Bc)
    k_dec = kc * jnp.exp(Bc[..., -1:, :] - Bc)
    g_last = jnp.exp(Bc[..., -1, :])
    causal = jnp.tril(jnp.ones((CHUNK, CHUNK), bool))[..., None]

    def step(state, inp):
        q_c, k_c, v_c, b_c, qd_c, kd_c, gl_c = inp
        dec = jnp.exp(jnp.where(causal, b_c[..., :, None, :] - b_c[..., None, :, :], -jnp.inf))
        A = jnp.einsum('bhck,bhsk,bhcsk->bhcs', q_c, k_c, dec)
        o = jnp.einsum('bhck,bhkv->bhcv', qd_c, state) + jnp.einsum('bhcs,bhsv->bhcv', A, v_c)
        state = gl_c[..., :, None] * state + jnp.einsum('bhck,bhcv->bhkv', kd_c, v_c)
        return state, o

    xs = tuple(jnp.moveaxis(t, 2, 0) for t in (qc, kc, vc, Bc, q_dec, k_dec, g_last))
    s0 = jnp.zeros((Bsz, HG_HEADS, HG_DHEAD, HG_DHEAD), f32)
    _, o = lax.scan(step, s0, xs)
    o = rmsnorm(from_chunks(o), norm_g)
    o = o * jax.nn.silu(g.astype(f32).reshape(Bsz, S, HG_HEADS, HG_DHEAD))
    return o.reshape(Bsz, S, HG_WIDTH).astype(dtype)

def conv_geglu_ffn(h, w_up, conv_w, w_down):
    up = causal_depthwise_conv(h @ w_up, conv_w)
    gate, val = jnp.split(up, 2, axis=-1)
    return (jax.nn.gelu(gate, approximate=True) * val) @ w_down

def second_inputs(seed: int = 0) -> dict:
    key = jax.random.key(seed)
    ks = jax.random.split(key, 16)
    f32 = jnp.float32
    nrm = lambda k, s: jax.random.normal(k, s, f32)
    x = nrm(ks[0], (BATCH, SEQ, D_MODEL))
    w_in = nrm(ks[1], (DEPTH, D_MODEL, D_IN)) * D_MODEL ** -0.5
    dn_conv = nrm(ks[2], (DEPTH, DN_CONV, 3 * DN_WIDTH)) * DN_CONV ** -0.5
    dn_a_log = jnp.log(jax.random.uniform(ks[3], (DEPTH, DN_HEADS), f32, 1.0, 16.0))
    dt = jnp.exp(jax.random.uniform(ks[4], (DEPTH, DN_HEADS), f32,
                                    math.log(1e-3), math.log(1e-1)))
    dn_dt_bias = dt + jnp.log(-jnp.expm1(-dt))
    dn_norm = 1.0 + 0.02 * nrm(ks[5], (DEPTH, DN_DHEAD))
    hg_lb = 0.1 * nrm(ks[6], (DEPTH, HG_WIDTH))
    hg_norm = 1.0 + 0.02 * nrm(ks[7], (DEPTH, HG_DHEAD))
    w_out = nrm(ks[8], (DEPTH, D_MIX, D_MODEL)) * D_MIX ** -0.5
    g_mix_pre = 1.0 + 0.02 * nrm(ks[9], (DEPTH, D_MODEL))
    g_mix_post = 1.0 + 0.02 * nrm(ks[10], (DEPTH, D_MODEL))
    g_ffn_pre = 1.0 + 0.02 * nrm(ks[11], (DEPTH, D_MODEL))
    g_ffn_post = 1.0 + 0.02 * nrm(ks[12], (DEPTH, D_MODEL))
    ffn_w_up = nrm(ks[13], (DEPTH, D_MODEL, 2 * D_FF)) * D_MODEL ** -0.5
    ffn_conv = nrm(ks[14], (DEPTH, FFN_CONV, 2 * D_FF)) * FFN_CONV ** -0.5
    ffn_w_down = nrm(ks[15], (DEPTH, D_FF, D_MODEL)) * D_FF ** -0.5
    return {'x': x, 'w_in': w_in, 'dn_conv': dn_conv, 'dn_a_log': dn_a_log,
            'dn_dt_bias': dn_dt_bias, 'dn_norm': dn_norm, 'hg_lb': hg_lb, 'hg_norm': hg_norm,
            'w_out': w_out, 'g_mix_pre': g_mix_pre, 'g_mix_post': g_mix_post,
            'g_ffn_pre': g_ffn_pre, 'g_ffn_post': g_ffn_post, 'ffn_w_up': ffn_w_up,
            'ffn_conv': ffn_conv, 'ffn_w_down': ffn_w_down}

def second_block(x, w_in, dn_conv, dn_a_log, dn_dt_bias, dn_norm, hg_lb, hg_norm, w_out,
              g_mix_pre, g_mix_post, g_ffn_pre, g_ffn_post, ffn_w_up, ffn_conv, ffn_w_down):
    cs = jnp.cumsum(jax.nn.softmax(hg_lb.astype(jnp.float32), axis=0), axis=0)
    lower_bounds = cs - cs[0:1]
    for l in range(DEPTH):
        h = rmsnorm(x, g_mix_pre[l])
        (a_q, a_k, a_v, a_z, a_b, a_a,
         b_q, b_k, b_v, b_qi, b_ki, b_wi,
         c_q, c_f, c_i, c_g) = jnp.split(h @ w_in[l], SPLIT_POINTS, axis=-1)
        o_a = gated_deltanet(a_q, a_k, a_v, a_z, a_b, a_a, dn_conv[l], dn_a_log[l],
                             dn_dt_bias[l], dn_norm[l])
        o_b = dsa_attention(b_q, b_k, b_v, b_qi, b_ki, b_wi)
        o_c = hgrn2(c_q, c_f, c_i, c_g, lower_bounds[l], hg_norm[l])
        mix = jnp.concatenate([o_a, o_b, o_c], axis=-1) @ w_out[l]
        x = x + rmsnorm(mix, g_mix_post[l])
        h = rmsnorm(x, g_ffn_pre[l])
        x = x + rmsnorm(conv_geglu_ffn(h, ffn_w_up[l], ffn_conv[l], ffn_w_down[l]), g_ffn_post[l])
    return x


def setup_inputs(seed=0):
    out = dict(first_inputs(seed))
    for name, value in second_inputs(seed + 1).items():
        if name != "x":
            out[name + "_2"] = value
    return out


def reference(
    x, c, ctx, c_ctx, w_mod, b_mod, ln_w, ln_b, ab_w_in, ab_gate_b, ab_norm_w, ab_sink,
    ab_w_out, gla_w_in, gla_gate_up, gla_gate_b, gla_norm_w, gla_w_out, peer_wq, peer_keys,
    peer_u, peer_v, w_in_2, dn_conv_2, dn_a_log_2, dn_dt_bias_2, dn_norm_2, hg_lb_2, hg_norm_2,
    w_out_2, g_mix_pre_2, g_mix_post_2, g_ffn_pre_2, g_ffn_post_2, ffn_w_up_2, ffn_conv_2,
    ffn_w_down_2,
):
    x = first_block(
        x, c, ctx, c_ctx, w_mod, b_mod, ln_w, ln_b, ab_w_in, ab_gate_b, ab_norm_w, ab_sink,
        ab_w_out, gla_w_in, gla_gate_up, gla_gate_b, gla_norm_w, gla_w_out, peer_wq, peer_keys,
        peer_u, peer_v,
    )
    return second_block(
        x, w_in_2, dn_conv_2, dn_a_log_2, dn_dt_bias_2, dn_norm_2, hg_lb_2, hg_norm_2, w_out_2,
        g_mix_pre_2, g_mix_post_2, g_ffn_pre_2, g_ffn_post_2, ffn_w_up_2, ffn_conv_2,
        ffn_w_down_2,
    )


_drawn_inputs = setup_inputs


def setup_inputs(seed=0):
    import zlib

    import numpy as np

    out = dict(_drawn_inputs(seed))
    spreads = {}
    factors = {'ab_norm_w': 20.214,
     'ab_sink': 38.369,
     'gla_norm_w': 17.533,
     'hg_lb_2': 8.0,
     'hg_norm_2': 9.694,
     'peer_wq': 3.079,
     'peer_keys': 3.026,
     'peer_u': 3.301,
     'peer_v': 3.001,
     'dn_norm_2': 5.348,
     'g_ffn_post_2': 2.974}
    for name, (base, spread) in spreads.items():
        noise = np.random.default_rng([zlib.crc32(name.encode()), seed]).standard_normal(out[name].shape)
        drawn = base * np.exp(spread * noise) if base else spread * noise
        out[name] = __import__('jax').numpy.asarray(drawn.astype(out[name].dtype))
    for name, factor in factors.items():
        out[name] = (out[name] * factor).astype(out[name].dtype)
    return out
```

```python
from collections import namedtuple
from contextlib import ExitStack, contextmanager
from itertools import count

import concourse.bass as bass
import numpy as np
from concourse import mybir

F32 = mybir.dt.float32
F32R = mybir.dt.float32r
U32 = mybir.dt.uint32
ALU = mybir.AluOpType
ACT = mybir.ActivationFunctionType
AX = mybir.AxisListType
ds = bass.ds

P = 128
D = 1024
DC = D // P
SEQ = 256
CTX = 256
TOK = SEQ + CTX
DEPTH = 2
CHUNK = 64
H_M, DH_M = 4, 128
H_A, H_KV, DH_A = 8, 2, 64
WINDOW = 128
H_C, DK_C, DV_C = 4, 128, 256
GATE_RANK, GATE_TAU = 16, 16.0
N_KEYS = 128
PEER_HEADS, PEER_TOPK = 8, 16
ALPHA = (2 * DEPTH) ** 0.25
LN_EPS = 1e-5
RMS_EPS = 1e-6
DN_HEADS, DN_DHEAD, DN_CONV = 4, 128, 4
SA_HEADS, SA_DHEAD = 4, 64
HG_HEADS, HG_DHEAD = 4, 64
IDX_HEADS = 4
TOPK = 64
D_FF, FFN_CONV = 2816, 3
NF = D_FF // P
NEG = -1e30
TAKEN = -3e38

SLOTS = 3
UNIT = 4096


NUMBER = count()
SCOPES = []
STAGE_SEMS = 14


@contextmanager
def scope():
    with ExitStack() as held:
        SCOPES.append(held)
        yield
        SCOPES.pop()


def sbuf(nc, name, shape, dtype):
    return SCOPES[-1].enter_context(nc.sbuf_tensor(f"{name}_{next(NUMBER)}", shape, dtype))


class Sems:
    sets, turn = [], 0


@contextmanager
def stage(nc, *names):
    own, other = Sems.sets[Sems.turn % 2], Sems.sets[(Sems.turn + 1) % 2]
    Sems.turn += 1
    with nc.Block() as block:
        @block.gpsimd
        def _(pool):
            pool.sem_clear(range(other[0].num, other[-1].num + 1))
        yield (block, *own[:len(names)])


class Steps:

    def __init__(self, eng, sem):
        self.eng, self.sem, self.n = eng, sem, 0

    def __call__(self, ins):
        ins.then_inc(self.sem, 1)
        self.n += 1
        return self.n

    def wait(self):
        self.eng.wait_ge(self.sem, self.n)


class Weights:

    def __init__(self, nc):
        self.ring = sbuf(nc, "weight_ring", [P, SLOTS, UNIT], F32)
        self.landed = [nc.alloc_semaphore(f"slot{s}_landed") for s in range(SLOTS)]
        self.src, self.first = [], {}
        self.issued = 0
        self.used = 0
        self.release = {}

    def plan(self, name, srcs):
        self.first[name] = len(self.src)
        self.src += srcs

    def slot(self, n):
        return self.ring[:, n % SLOTS, :]

    def wait_landed(self, pe, n):
        pe.wait_ge(self.landed[n % SLOTS], 16 * (n // SLOTS + 1))

    def done(self, n, sem, value):
        self.release[n] = (sem, value)
        self.used = max(self.used, n + 1)

    def load(self, sp, n):
        src = self.src[n]
        sp.dma_start(self.slot(n)[0:src.shape[0], 0:src.shape[1]], src).then_inc(self.landed[n % SLOTS], 16)

    def run_ahead(self, sp):
        while self.issued < min(self.used + SLOTS, len(self.src)):
            n = self.issued
            if n - SLOTS in self.release:
                sp.wait_ge(*self.release[n - SLOTS])
            self.load(sp, n)
            self.issued += 1

    def stage_over(self):
        self.release = {}



Job = namedtuple("Job", "unit nk lhsT rhs m n eng dst func scale view", defaults=(None, 1.0, None))


def project(nc, G, name, jobs):
    ps, ws = G.ps, G.ws
    lanes = {"v": [j for j in jobs if j.eng == "v"], "s": [j for j in jobs if j.eng == "s"]}
    with stage(nc, f"{name}_v_ready", f"{name}_s_ready", f"{name}_v_out", f"{name}_s_out") as (
            block, v_ready, s_ready, v_out, s_out):
        ready, out = {"v": v_ready, "s": s_ready}, {"v": v_out, "s": s_out}
        bank = {"v": 0, "s": 4}

        def tile(j, k):
            o = ps[0:j.m, bank[j.eng] + k % 4, 0:j.n]
            return o

        @block.tensor
        def _(pe):
            count = {"v": 0, "s": 0}
            seen = -1
            for n, j in enumerate(jobs):
                k = count[j.eng]
                if j.unit is not None and j.unit > seen:
                    ws.wait_landed(pe, j.unit)
                    seen = j.unit
                if k >= 4:
                    pe.wait_ge(out[j.eng], k - 3)
                for c in range(j.nk):
                    mm = pe.matmul(tile(j, k), j.lhsT(c), j.rhs(c), start=(c == 0), stop=(c == j.nk - 1))
                mm.then_inc(ready[j.eng], 1)
                count[j.eng] = k + 1
                if j.unit is not None:
                    ws.done(j.unit, ready[j.eng], k + 1)

        @block.vector
        def _(dve):
            for k, j in enumerate(lanes["v"]):
                dve.wait_ge(v_ready, k + 1)
                src = tile(j, k)
                src = j.view(src) if j.view else src
                if j.scale == 1.0:
                    dve.tensor_copy(j.dst, src).then_inc(v_out, 1)
                else:
                    dve.tensor_scalar(j.dst, src, j.scale, None, ALU.mult).then_inc(v_out, 1)

        @block.scalar
        def _(act):
            for k, j in enumerate(lanes["s"]):
                act.wait_ge(s_ready, k + 1)
                src = tile(j, k)
                src = j.view(src) if j.view else src
                act.activation(j.dst, src, j.func or ACT.Identity, scale=j.scale).then_inc(s_out, 1)

        @block.sync
        def _(sp):
            ws.run_ahead(sp)
    ws.stage_over()


def transpose_in(nc, G, name, src, tiles, dst, scale=None, shift=None):
    ps, ws = G.ps, G.ws
    with stage(nc, f"{name}_turned", f"{name}_v_out", f"{name}_s_out") as (block, turned, v_out, s_out):
        @block.tensor
        def _(pe):
            for c in range(DC):
                for k, t in enumerate(tiles):
                    mm = pe.transpose(ps[:, c, k * P:(k + 1) * P], src(t, c), G.ident[:, :])
                mm.then_inc(turned, 1)

        @block.vector
        def _(dve):
            for c in range(0, DC, 2):
                dve.wait_ge(turned, c + 1)
                for q in range(len(tiles) // 2):
                    o, i = dst[:, c, q * SEQ:(q + 1) * SEQ], ps[:, c, q * SEQ:(q + 1) * SEQ]
                    if scale is None:
                        dve.tensor_copy(o, i).then_inc(v_out, 1)
                    elif shift is None:
                        dve.tensor_scalar(o, i, scale(c, q), None, ALU.mult).then_inc(v_out, 1)
                    else:
                        dve.tensor_scalar(o, i, scale(c, q), shift(c, q), ALU.mult, ALU.add).then_inc(v_out, 1)

        @block.scalar
        def _(act):
            for c in range(1, DC, 2):
                act.wait_ge(turned, c + 1)
                for q in range(len(tiles) // 2):
                    o, i = dst[:, c, q * SEQ:(q + 1) * SEQ], ps[:, c, q * SEQ:(q + 1) * SEQ]
                    if scale is None:
                        act.activation(o, i, ACT.Identity).then_inc(s_out, 1)
                    elif shift is None:
                        act.activation(o, i, ACT.Identity, scale=scale(c, q)).then_inc(s_out, 1)
                    else:
                        act.activation(o, i, ACT.Identity, scale=scale(c, q), bias=shift(c, q)).then_inc(s_out, 1)

        @block.sync
        def _(sp):
            ws.run_ahead(sp)


def modulation(nc, G, layer):
    ps, ws, mod = G.ps, G.ws, G.mod
    u0 = ws.first[f"mod{layer}"]
    UNITS, GROUPS, M = 12, 4, 32
    with scope():
        cc = sbuf(nc, "c_cols", [P, 2, DC], F32)
        sc = sbuf(nc, "silu_c", [P, DC, M], F32)
        bm = sbuf(nc, "b_mod", [P, 6 * DC], F32)
        part = sbuf(nc, "mod_parts", [P, 2, 512], F32)
        pick = sbuf(nc, "row_picker", [P, 2], F32)
        with stage(nc, "c_landed", "sc_zeroed", "silu_done", "picker_ready", "parts_ready", "parts_v_out", "parts_s_out",
                   "mod_ready", "mod_raw") as (
                block, c_landed, sc_zeroed, silu_done, picker_ready, parts_ready, v_out, s_out, mod_ready, mod_raw):
            @block.tensor
            def _(pe):
                def parts(u):
                    ws.wait_landed(pe, u0 + u)
                    if u >= 2:
                        pe.wait_ge((v_out, s_out)[u % 2], u // 2)
                    w = ws.slot(u0 + u).rearrange("p (c n) -> p c n", c=DC)
                    for c in range(DC):
                        g = c % GROUPS
                        mm = pe.matmul(ps[g * M:(g + 1) * M, 1 + u % 2, :], sc[:, c, :], w[:, c, :], start=(c < GROUPS),
                                       stop=(c >= GROUPS), tile_position=(0, g * M))
                    mm.then_inc(parts_ready, 1)
                    ws.done(u0 + u, parts_ready, u + 1)

                def sums(u):
                    pe.wait_ge((v_out, s_out)[u % 2], u // 2 + 1)
                    for q in range(4):
                        n = 4 * u + q
                        mm = pe.matmul(ps[:, 0, 2 * n:2 * n + 2], part[:, u % 2, q * P:(q + 1) * P], pick[:, :],
                                       start=True, stop=True)
                    mm.then_inc(mod_ready, 1)

                pe.wait_ge(silu_done, 1)
                pe.wait_ge(picker_ready, 1)
                parts(0)
                for u in range(1, UNITS):
                    parts(u)
                    sums(u - 1)
                sums(UNITS - 1)

            @block.sync
            def _(sp):
                sp.dma_start(cc[:, 0, :], G.d["c"]).then_inc(c_landed, 16)
                sp.dma_start(cc[:, 1, :], G.d["c_ctx"]).then_inc(c_landed, 16)
                sp.dma_start(bm[:, :], G.d[f"b_mod{layer}"]).then_inc(c_landed, 16)
                ws.run_ahead(sp)

            @block.scalar
            def _(act):
                act.wait_ge(c_landed, 48)
                act.wait_ge(sc_zeroed, 1)
                act.activation(sc[:, :, 0:2].rearrange("p c k -> p k c"), cc[:, :, :], ACT.Silu).then_inc(silu_done, 1)
                for u in range(1, UNITS, 2):
                    act.wait_ge(parts_ready, u + 1)
                    if u >= 3:
                        act.wait_ge(mod_ready, u - 1)
                    act.activation(part[:, 1, :], ps[:, 2, :], ACT.Identity).then_inc(s_out, 1)

            @block.vector
            def _(dve):
                dve.memset(sc[:, :, :], 0.0).then_inc(sc_zeroed, 1)
                diag = G.ident[:, :].rearrange("p (g m) -> p m g", m=M)
                dve.tensor_reduce(pick[:, :], diag[:, 0:2, :], AX.X, ALU.add).then_inc(picker_ready, 1)
                for u in range(0, UNITS, 2):
                    dve.wait_ge(parts_ready, u + 1)
                    if u >= 2:
                        dve.wait_ge(mod_ready, u - 1)
                    dve.tensor_copy(part[:, 0, :], ps[:, 1, :]).then_inc(v_out, 1)
                dve.wait_ge(c_landed, 48)
                dve.wait_ge(mod_ready, UNITS)
                dve.tensor_tensor(mod[:, :, :], ps[:, 0, 0:96].rearrange("p (n b) -> p n b", b=2),
                                  bm[:, :].unsqueeze(2).broadcast_to([P, 6 * DC, 2]), ALU.add).then_inc(mod_raw, 1)
                dve.wait_ge(mod_raw, 1)
                for k in (1, 4):
                    v = mod[:, k * DC:(k + 1) * DC, :]
                    dve.tensor_scalar(v, v, 1.0, None, ALU.add).then_inc(mod_raw, 1)
    ws.stage_over()


def gate_rows(nc, G, part, cols, out, banks=8):
    ps, mod = G.ps, G.mod
    with scope():
        diag = sbuf(nc, "gate_diag", [P, 4, P], F32)
        with stage(nc, "diag_ready", "rows_ready", "rows_out") as (block, diag_ready, rows_ready, rows_out):
            work = [(col, c) for col in cols for c in range(DC)]

            @block.vector
            def _(dve):
                for n, (col, c) in enumerate(work):
                    if n >= 4:
                        dve.wait_ge(rows_ready, n - 3)
                    dve.tensor_scalar(diag[:, n % 4, :], G.ident[:, :], mod[:, part * DC + c, col:col + 1], None,
                                      ALU.mult).then_inc(diag_ready, 1)

            @block.tensor
            def _(pe):
                for n, (col, c) in enumerate(work):
                    pe.wait_ge(diag_ready, n + 1)
                    if n >= banks:
                        pe.wait_ge(rows_out, n - banks + 1)
                    pe.matmul(ps[:, n % banks, 0:P], G.ones[:, :], diag[:, n % 4, :], start=True,
                              stop=True).then_inc(rows_ready, 1)

            @block.scalar
            def _(act):
                for n, (col, c) in enumerate(work):
                    act.wait_ge(rows_ready, n + 1)
                    act.activation(out[:, col, c * P:(c + 1) * P], ps[:, n % banks, 0:P], ACT.Identity).then_inc(rows_out, 1)

            @block.sync
            def _(sp):
                G.ws.run_ahead(sp)


def residual_norm(nc, G, name, tiles, banks, rows, cols, form, pre=None):
    ps, x = G.ps, G.x
    eps = LN_EPS if form == "ln" else RMS_EPS
    with scope():
        z = sbuf(nc, "norm_z", [P, 2, D], F32)
        q = sbuf(nc, "norm_q", [P, 2, D], F32)
        st = sbuf(nc, "norm_stats", [P, 2, 16], F32)
        with stage(nc, "y_ready", "y_out", "var_ready", "std_ready", "norm_step", "part_done") as (
                block, y_ready, y_out, var_ready, std_ready, step_sem, part_done):
            if pre is not None:
                @block.tensor
                def _(pe):
                    pre(pe, y_ready, part_done)

            @block.scalar
            def _(act):
                for n, t in enumerate(tiles):
                    act.wait_ge(var_ready, n + 1)
                    act.activation(st[:, n % 2, 14:15], st[:, n % 2, 13:14], ACT.Sqrt).then_inc(std_ready, 1)

            @block.vector
            def _(dve):
                step = Steps(dve, step_sem)
                for n, t in enumerate(tiles):
                    b = n % 2
                    zt, qt, s = z[:, b, :], q[:, b, :], st[:, b, :]
                    y = ps[:, banks(n):banks(n) + 2, :].rearrange("p a b -> p (a b)")
                    if pre is not None:
                        dve.wait_ge(y_ready, n + 1)
                    if form == "ln":
                        dve.tensor_tensor(zt, y, rows(cols[n]), ALU.mult).then_inc(y_out, 1)
                        dve.wait_ge(y_out, n + 1)
                        step(dve.scalar_tensor_tensor(zt, x[:, t, :], ALPHA, zt, ALU.mult, ALU.add))
                        step.wait()
                        for h in range(2):
                            step(dve.bn_stats(s[:, 6 * h:6 * h + 6], zt[:, h * 512:(h + 1) * 512]))
                        step.wait()
                        step(dve.bn_aggr(s[:, 12:14], s[:, 0:12]))
                        step.wait()
                        step(dve.tensor_copy(s[:, 15:16], s[:, 12:13]))
                        step.wait()
                        dve.tensor_scalar(s[:, 13:14], s[:, 13:14], eps, None, ALU.add).then_inc(var_ready, 1)
                        dve.wait_ge(std_ready, n + 1)
                        step(dve.reciprocal(s[:, 12:13], s[:, 14:15]))
                        step.wait()
                        step(dve.tensor_scalar(qt, zt, s[:, 15:16], s[:, 12:13], ALU.subtract, ALU.mult))
                        step.wait()
                        step(dve.tensor_tensor(zt, qt, rows("w"), ALU.mult))
                        step.wait()
                        step(dve.tensor_tensor(x[:, t, :], zt, rows("b"), ALU.add))
                    else:
                        dve.tensor_copy(zt, y).then_inc(y_out, 1)
                        dve.wait_ge(y_out, n + 1)
                        step(dve.tensor_tensor(qt, zt, zt, ALU.mult))
                        step.wait()
                        step(dve.tensor_reduce(s[:, 0:1], qt, AX.X, ALU.add))
                        step.wait()
                        dve.tensor_scalar(s[:, 13:14], s[:, 0:1], 1.0 / D, eps, ALU.mult, ALU.add).then_inc(var_ready, 1)
                        dve.wait_ge(std_ready, n + 1)
                        step(dve.reciprocal(s[:, 12:13], s[:, 14:15]))
                        step.wait()
                        step(dve.scalar_tensor_tensor(qt, zt, s[:, 12:13], rows("w"), ALU.mult, ALU.mult))
                        step.wait()
                        step(dve.tensor_tensor(x[:, t, :], qt, x[:, t, :], ALU.add))
                    step.wait()

            @block.sync
            def _(sp):
                G.ws.run_ahead(sp)
    G.ws.stage_over()


def out_project(G, u0, tiles, catT):
    ws, ps = G.ws, G.ps

    def pre(pe, y_ready, part_done):
        for h in range(2):
            ws.wait_landed(pe, u0 + h)
        for n, t in enumerate(tiles):
            for h in range(2):
                w = ws.slot(u0 + h).rearrange("p (c n) -> p c n", c=DC)
                for c in range(DC):
                    mm = pe.matmul(ps[:, 2 * n + h, :], catT[:, c, n * P:(n + 1) * P], w[:, c, :],
                                   start=(c == 0), stop=(c == DC - 1))
            mm.then_inc(y_ready, 1)
        for h in range(2):
            ws.done(u0 + h, y_ready, len(tiles))
    return pre


def attend(nc, G, items):
    ps = G.ps
    with scope():
        sm = sbuf(nc, "scores", [P, 2, 512], F32)
        pr = sbuf(nc, "probs", [P, 2, 512], F32)
        pT = sbuf(nc, "probsT", [P, 2, 512], F32)
        st = sbuf(nc, "soft_stats", [P, 2, 8], F32)
        N = len(items)
        with stage(nc, "s_ready", "masked", "maxed", "negmax_ready", "probs_ready", "sum_ready", "turned", "pT_ready",
                   "pv_ready", "den_step", "rden_ready", "att_out") as (
                block, s_ready, masked, maxed, negmax_ready, probs_ready, sum_ready, turned, pT_ready, pv_ready,
                den_step, rden_ready, att_out):
            summed = probs_ready if items[0].sink is None else sum_ready

            @block.tensor
            def _(pe):
                for i in range(N + 2):
                    if i < N:
                        it = items[i]
                        if i >= 2:
                            pe.wait_ge(masked, i - 1)
                        pe.matmul(ps[:, i % 2, 0:it.nk], it.q, it.k, start=True, stop=True).then_inc(s_ready, 1)
                    if 1 <= i <= N:
                        n = i - 1
                        it = items[n]
                        pe.wait_ge(probs_ready, n + 1)
                        if n >= 2:
                            pe.wait_ge(pT_ready, n - 1)
                        for k in range(it.nk // P):
                            mm = pe.transpose(ps[:, 2 + n % 2, k * P:(k + 1) * P], pr[:, n % 2, k * P:(k + 1) * P],
                                              G.ident[:, :])
                        mm.then_inc(turned, 1)
                    if 2 <= i:
                        n = i - 2
                        it = items[n]
                        pe.wait_ge(pT_ready, n + 1)
                        if n >= 2:
                            pe.wait_ge(att_out, n - 1)
                        for k in range(it.nk // P):
                            mm = pe.matmul(ps[:, 4 + n % 2, 0:DH_A], pT[:, n % 2, k * P:(k + 1) * P], it.v[k],
                                           start=(k == 0), stop=(k == it.nk // P - 1))
                        mm.then_inc(pv_ready, 1)

            @block.vector
            def _(dve):
                for i in range(N + 2):
                    if i < N:
                        it, b = items[i], i % 2
                        dve.wait_ge(s_ready, i + 1)
                        if i >= 2:
                            dve.wait_ge(probs_ready, i - 1)
                        s, src = sm[:, b, 0:it.nk], ps[:, b, 0:it.nk]
                        if it.mask is None:
                            dve.tensor_scalar(s, src, DH_A ** -0.5, None, ALU.mult).then_inc(masked, 1)
                        else:
                            dve.scalar_tensor_tensor(s, src, DH_A ** -0.5, it.mask, ALU.mult, ALU.add).then_inc(masked, 1)
                        dve.wait_ge(masked, i + 1)
                        if i >= 2:
                            dve.wait_ge(summed, i - 1)
                            dve.wait_ge(rden_ready, i - 1)
                        dve.tensor_reduce(st[:, b, 0:1], s, AX.X, ALU.max).then_inc(maxed, 1)
                        dve.wait_ge(maxed, i + 1)
                        if it.sink is None:
                            dve.tensor_scalar(st[:, b, 1:2], st[:, b, 0:1], -1.0, None, ALU.mult).then_inc(negmax_ready, 1)
                        else:
                            dve.tensor_scalar(st[:, b, 1:2], st[:, b, 0:1], it.sink, -1.0, ALU.max,
                                              ALU.mult).then_inc(negmax_ready, 1)
                    if 1 <= i <= N:
                        n = i - 1
                        it, b = items[n], n % 2
                        dve.wait_ge(summed, n + 1)
                        if it.sink is None:
                            dve.tensor_copy(st[:, b, 4:5], st[:, b, 2:3]).then_inc(den_step, 1)
                        else:
                            dve.tensor_tensor(st[:, b, 4:5], st[:, b, 2:3], st[:, b, 3:4], ALU.add).then_inc(den_step, 1)
                        dve.wait_ge(den_step, n + 1)
                        if n >= 2:
                            dve.wait_ge(att_out, n - 1)
                        dve.reciprocal(st[:, b, 5:6], st[:, b, 4:5]).then_inc(rden_ready, 1)
                    if 2 <= i:
                        n = i - 2
                        it, b = items[n], n % 2
                        dve.wait_ge(pv_ready, n + 1)
                        dve.wait_ge(rden_ready, n + 1)
                        dve.tensor_scalar(it.out, ps[:, 4 + b, 0:DH_A], st[:, b, 5:6], None, ALU.mult).then_inc(att_out, 1)

            @block.scalar
            def _(act):
                for i in range(N + 1):
                    if i < N:
                        it, b = items[i], i % 2
                        act.wait_ge(negmax_ready, i + 1)
                        if i >= 2:
                            act.wait_ge(turned, i - 1)
                            act.wait_ge(den_step, i - 1)
                        act.activation(pr[:, b, 0:it.nk], sm[:, b, 0:it.nk], ACT.Exp, bias=st[:, b, 1:2],
                                       accum_out=st[:, b, 2:3]).then_inc(probs_ready, 1)
                        if it.sink is not None:
                            act.activation(st[:, b, 3:4], it.sink, ACT.Exp, bias=st[:, b, 1:2]).then_inc(sum_ready, 1)
                    if 1 <= i:
                        n = i - 1
                        it = items[n]
                        act.wait_ge(turned, n + 1)
                        if n >= 2:
                            act.wait_ge(pv_ready, n - 1)
                        act.activation(pT[:, n % 2, 0:it.nk], ps[:, 2 + n % 2, 0:it.nk], ACT.Identity).then_inc(pT_ready, 1)

            @block.sync
            def _(sp):
                G.ws.run_ahead(sp)


Item = namedtuple("Item", "q k nk mask sink v out")



def mlstm_gates(nc, G, gi, gf, gcol, negM):
    ps = G.ps
    with scope():
        gb = sbuf(nc, "gate_b", [H_M, 4], F32)
        xi = sbuf(nc, "gate_i", [H_M, 2, TOK], F32)
        xf = sbuf(nc, "gate_f", [H_M, 2, TOK], F32)
        t1 = sbuf(nc, "gate_t1", [H_M, 2, TOK], F32)
        t2 = sbuf(nc, "gate_t2", [H_M, 2, TOK], F32)
        one = sbuf(nc, "gate_one", [H_M, TOK], F32)
        zero = sbuf(nc, "gate_zero", [H_M, TOK], F32)
        nat = sbuf(nc, "gate_nat", [H_M, 2, 2, TOK], F32)
        with stage(nc, "gb_landed", "gate_step", "abs_ready", "log1p_ready", "exp_step", "m_ready", "em_ready",
                   "nat_ready", "cols_ready") as (
                block, gb_landed, step_sem, abs_ready, log1p_ready, exp_step, m_ready, em_ready, nat_ready, cols_ready):
            @block.sync
            def _(sp):
                sp.dma_start(gb[:, :], G.d["ab_gate_b"]).then_inc(gb_landed, 16)
                G.ws.run_ahead(sp)

            def in_scan_order(d, dst, src):
                a = (dst[:, d, 0:CTX], src[:, d, SEQ:TOK] if d == 0 else src[:, d, TOK - 1:SEQ - 1:-1])
                b = (dst[:, d, CTX:TOK], src[:, d, 0:SEQ] if d == 0 else src[:, d, SEQ - 1::-1])
                return a, b

            def in_token_order(d, dst, src):
                a = (dst[:, d, SEQ:TOK], src[:, d, 0:CTX] if d == 0 else src[:, d, CTX - 1::-1])
                b = (dst[:, d, 0:SEQ], src[:, d, CTX:TOK] if d == 0 else src[:, d, TOK - 1:CTX - 1:-1])
                return a, b

            @block.vector
            def _(dve):
                step = Steps(dve, step_sem)
                step(dve.memset(one[:, :], 1.0))
                step(dve.memset(zero[:, :], 0.0))
                dve.wait_ge(gb_landed, 16)
                for d in range(2):
                    for o, i in in_scan_order(d, xi, gi):
                        step(dve.tensor_scalar(o, i, gb[:, d:d + 1], None, ALU.add))
                    for o, i in in_scan_order(d, xf, gf):
                        step(dve.tensor_scalar(o, i, gb[:, 2 + d:3 + d], None, ALU.add))
                step.wait()
                dve.scalar_tensor_tensor(t1[:, :, :], xf[:, :, :], -1.0, xf[:, :, :], ALU.mult, ALU.max).then_inc(abs_ready, 1)
                dve.wait_ge(log1p_ready, 1)
                step(dve.scalar_tensor_tensor(xf[:, :, :], xf[:, :, :], 0.0, t1[:, :, :], ALU.min, ALU.subtract))
                step.wait()
                for d in range(2):
                    step(dve.tensor_tensor_scan(t1[:, d, :], one[:, :], xf[:, d, :], 0.0, ALU.mult, ALU.add))
                step.wait()
                step(dve.tensor_tensor(t2[:, :, :], xi[:, :, :], t1[:, :, :], ALU.subtract))
                step.wait()
                for d in range(2):
                    step(dve.tensor_tensor_scan(xi[:, d, :], zero[:, :], t2[:, d, :], 0.0, ALU.max, ALU.max))
                step.wait()
                dve.tensor_tensor(xf[:, :, :], xi[:, :, :], t1[:, :, :], ALU.add).then_inc(m_ready, 1)
                for d in range(2):
                    for o, i in in_token_order(d, negM, xi):
                        step(dve.tensor_scalar(o, i, -1.0, None, ALU.mult))
                    for o, i in in_token_order(d, nat[:, 0], t2):
                        step(dve.tensor_copy(o, i))
                dve.wait_ge(em_ready, 1)
                for d in range(2):
                    for o, i in in_token_order(d, nat[:, 1], t1):
                        last = dve.tensor_copy(o, i)
                        if d == 0:
                            step(last)
                        elif o is not None:
                            last.then_inc(nat_ready, 1)
                dve.wait_ge(cols_ready, 1)
                step(dve.tensor_copy(gcol[:, :, :, :, :].rearrange("p k d t h -> p (k d t h)"), ps[:, 0, 0:64]))
                step.wait()

            @block.scalar
            def _(act):
                act.wait_ge(abs_ready, 1)
                act.activation(t2[:, :, :], t1[:, :, :], ACT.Exp, scale=-1.0).then_inc(exp_step, 1)
                act.wait_ge(exp_step, 1)
                act.activation(t1[:, :, :], t2[:, :, :], ACT.Ln, bias=1.0).then_inc(log1p_ready, 1)
                act.wait_ge(m_ready, 1)
                act.activation(t1[:, :, :], xf[:, :, :], ACT.Exp, scale=-1.0).then_inc(em_ready, 1)

            @block.tensor
            def _(pe):
                pe.wait_ge(nat_ready, 2)
                for kind in range(2):
                    for d in range(2):
                        for t in range(4):
                            n = (kind * 2 + d) * 4 + t
                            mm = pe.transpose(ps[:, 0, 4 * n:4 * n + 4], nat[:, kind, d, t * P:(t + 1) * P],
                                              G.ident[0:H_M, 0:H_M])
                mm.then_inc(cols_ready, 1)


QK_PARTS = [(0, 0, SEQ, 0), (1, 0, SEQ, SEQ), (2, 0, TOK, 2 * SEQ), (3, 0, TOK, 2 * SEQ + TOK)]
QK_WIDTH = 2 * SEQ + 2 * TOK


def mlstm(nc, G, qT, kT, v1, gcol, negM, hm):
    ps = G.ps
    with scope():
        mask = sbuf(nc, "scan_mask", [P, 2, QK_WIDTH], F32)
        sel = sbuf(nc, "row_select", [H_M, H_M, P], F32)
        qk = sbuf(nc, "qk", [P, 2, QK_WIDTH], F32)
        w = sbuf(nc, "mlstm_w", [P, 2, QK_WIDTH], F32)
        dt_ = sbuf(nc, "mlstm_d", [P, 2, TOK], F32)
        de = sbuf(nc, "mlstm_den", [P, 2, 8], F32)
        combos = [(h, d) for h in range(H_M) for d in range(2)]
        with stage(nc, "mask_landed", "qk_ready", "qk_out", "mb_ready", "d_ready", "exp_ready", "w_ready", "num_ready",
                   "den_step", "h_out") as (
                block, mask_landed, qk_ready, qk_out, mb_ready, d_ready, exp_ready, w_ready, num_ready, den_step, h_out):
            @block.sync
            def _(sp):
                sp.dma_start(mask[:, :, :], G.d["scan_mask"]).then_inc(mask_landed, 16)
                sp.dma_start(sel[:, :, :], G.d["row_select"]).then_inc(mask_landed, 16)
                G.ws.run_ahead(sp)

            @block.tensor
            def _(pe):
                pe.wait_ge(mask_landed, 32)

                def products(h):
                    for n, (s, q0, nq, _) in enumerate(QK_PARTS):
                        k = 4 * h + n
                        if k >= 2:
                            pe.wait_ge(qk_out, k - 1)
                        pe.matmul(ps[:, k % 2, 0:nq], kT[:, h, s * P:(s + 1) * P], qT[:, h, q0:q0 + nq], start=True,
                                  stop=True).then_inc(qk_ready, 1)

                def weighted(n):
                    h, d = combos[n]
                    pe.wait_ge(w_ready, 4 * (n + 1))
                    if n >= 2:
                        pe.wait_ge(h_out, n - 1)
                    for t in range(4):
                        keys = [0, 1, 2, 3] if t < 2 else [2, 3]
                        bank = 4 + 2 * (n % 2) + t // 2
                        for i, s in enumerate(keys):
                            _, _, _, at = QK_PARTS[s]
                            mm = pe.matmul(ps[:, bank, (t % 2) * 129:(t % 2) * 129 + 129],
                                           w[:, n % 2, at + t * P:at + (t + 1) * P], v1[:, s, h, :],
                                           start=(i == 0), stop=(i == len(keys) - 1))
                    mm.then_inc(num_ready, 1)

                products(0)
                for n, (h, d) in enumerate(combos):
                    if n >= 2:
                        pe.wait_ge(d_ready, 4 * (n - 1))
                    pe.matmul(ps[:, 2 + n % 2, :], sel[:, h, :], negM[:, d, :], start=True, stop=True).then_inc(mb_ready, 1)
                    if d == 1 and h + 1 < H_M:
                        products(h + 1)
                    if n >= 1:
                        weighted(n - 1)
                weighted(len(combos) - 1)

            @block.vector
            def _(dve):
                def finish(n):
                    h, d = combos[n]
                    dve.wait_ge(num_ready, n + 1)
                    e = de[:, n % 2, :]
                    src = ps[:, 4 + 2 * (n % 2):6 + 2 * (n % 2), 0:258].rearrange("p b (t c) -> p b t c", c=129)
                    e2 = e[:, 0:4].rearrange("p (b t) -> p b t", b=2)
                    dve.tensor_tensor(e2, src[:, :, :, 128], gcol[:, 1, d, :, h].rearrange("p (b t) -> p b t", b=2),
                                      ALU.max).then_inc(den_step, 1)
                    dve.wait_ge(den_step, 3 * n + 1)
                    dve.scalar_tensor_tensor(e2, src[:, :, :, 128], -1.0, e2, ALU.mult, ALU.max).then_inc(den_step, 1)
                    dve.wait_ge(den_step, 3 * n + 2)
                    dve.reciprocal(e[:, 4:8], e[:, 0:4]).then_inc(den_step, 1)
                    dve.wait_ge(den_step, 3 * n + 3)
                    if d == 1:
                        dve.wait_ge(h_out, n)
                    for t in range(4):
                        o = hm[:, t, h * DH_M:(h + 1) * DH_M]
                        i = ps[:, 4 + 2 * (n % 2) + t // 2, (t % 2) * 129:(t % 2) * 129 + 128]
                        if d == 0:
                            last = dve.tensor_scalar(o, i, e[:, 4 + t:5 + t], None, ALU.mult)
                        else:
                            last = dve.scalar_tensor_tensor(o, i, e[:, 4 + t:5 + t], o, ALU.mult, ALU.add)
                    last.then_inc(h_out, 1)

                dve.wait_ge(mask_landed, 32)
                for n, (h, d) in enumerate(combos):
                    dve.wait_ge(mb_ready, n + 1)
                    for i in range(5):
                        if i < 4:
                            k = 4 * n + i
                            s, q0, nq, at = QK_PARTS[i]
                            if k >= 2:
                                dve.wait_ge(w_ready, k - 1)
                            dve.scalar_tensor_tensor(dt_[:, k % 2, 0:nq], ps[:, 2 + n % 2, q0:q0 + nq],
                                                     gcol[:, 0, d, s, h:h + 1], mask[:, d, at:at + nq], ALU.add,
                                                     ALU.min).then_inc(d_ready, 1)
                        if i >= 1:
                            k = 4 * n + i - 1
                            s, q0, nq, at = QK_PARTS[i - 1]
                            dve.wait_ge(exp_ready, k + 1)
                            dve.wait_ge(qk_out, 4 * h + i)
                            if n >= 2:
                                dve.wait_ge(num_ready, n - 1)
                            dve.tensor_tensor(w[:, n % 2, at:at + nq], dt_[:, k % 2, 0:nq], qk[:, h % 2, at:at + nq],
                                              ALU.mult).then_inc(w_ready, 1)
                    if n >= 1:
                        finish(n - 1)
                finish(len(combos) - 1)

            @block.scalar
            def _(act):
                def products_out(h):
                    for n, (s, q0, nq, at) in enumerate(QK_PARTS):
                        act.wait_ge(qk_ready, 4 * h + n + 1)
                        if h >= 2:
                            act.wait_ge(w_ready, 8 * (h - 1))
                        act.activation(qk[:, h % 2, at:at + nq], ps[:, (4 * h + n) % 2, 0:nq],
                                       ACT.Identity).then_inc(qk_out, 1)

                products_out(0)
                for n, (h, d) in enumerate(combos):
                    for i, (s, q0, nq, at) in enumerate(QK_PARTS):
                        k = 4 * n + i
                        act.wait_ge(d_ready, k + 1)
                        act.activation(dt_[:, k % 2, 0:nq], dt_[:, k % 2, 0:nq], ACT.Exp).then_inc(exp_ready, 1)
                    if d == 1 and h + 1 < H_M:
                        products_out(h + 1)


def head_norm(nc, G, name, src, tiles, heads, width, wrow, gate, dst, eps):
    with scope():
        w = sbuf(nc, "head_w", [P, heads * width], F32)
        sq = sbuf(nc, "head_sq", [P, heads * width], F32)
        ms = sbuf(nc, "head_ms", [P, tiles, heads, 2], F32)
        with stage(nc, "w_landed", "hn_step", "ms_ready", "rms_ready") as (block, w_landed, step_sem, ms_ready, rms_ready):
            @block.sync
            def _(sp):
                sp.dma_start(w[:, :], wrow.partition_broadcast(P)).then_inc(w_landed, 16)
                G.ws.run_ahead(sp)

            @block.scalar
            def _(act):
                act.wait_ge(ms_ready, tiles)
                act.activation(ms[:, :, :, 1], ms[:, :, :, 0], ACT.Sqrt).then_inc(rms_ready, 1)

            @block.vector
            def _(dve):
                step = Steps(dve, step_sem)
                for n in range(tiles):
                    h3 = src(n)
                    s3 = sq[:, :].rearrange("p (h c) -> p h c", h=heads)
                    step(dve.tensor_tensor(s3, h3, h3, ALU.mult))
                    step.wait()
                    step(dve.tensor_reduce(ms[:, n, :, 0], s3, AX.X, ALU.add))
                    step.wait()
                    dve.tensor_scalar(ms[:, n, :, 0], ms[:, n, :, 0], 1.0 / width, eps, ALU.mult, ALU.add).then_inc(ms_ready, 1)
                dve.wait_ge(rms_ready, 1)
                step(dve.reciprocal(ms[:, :, :, 0], ms[:, :, :, 1]))
                step.wait()
                dve.wait_ge(w_landed, 16)
                w3 = w[:, :].rearrange("p (h c) -> p h c", h=heads)
                for n in range(tiles):
                    r = ms[:, n, :, 0:1].broadcast_to([P, heads, width])
                    step(dve.tensor_tensor(dst(n), src(n), r, ALU.mult))
                    step.wait()
                    step(dve.tensor_tensor(dst(n), dst(n), w3, ALU.mult))
                    step.wait()
                    step(dve.tensor_tensor(dst(n), dst(n), gate(n), ALU.mult))
                    step.wait()


def rope(nc, G, qa, ka):
    ps = G.ps
    with scope():
        cos = sbuf(nc, "rope_cos", [P, SEQ], F32)
        sin = sbuf(nc, "rope_sin", [P, SEQ], F32)
        swap = sbuf(nc, "rope_swap", [P, P], F32)
        t = sbuf(nc, "rope_t", [P, 6, SEQ], F32)
        rows = [qa[:, n, 0:SEQ] for n in range(4)] + [ka[:, n, 0:SEQ] for n in range(2)]
        with stage(nc, "rope_landed", "swapped", "rope_step") as (block, rope_landed, swapped, step_sem):
            @block.sync
            def _(sp):
                sp.dma_start(cos[:, :], G.d["rope_cos"]).then_inc(rope_landed, 16)
                sp.dma_start(sin[:, :], G.d["rope_sin"]).then_inc(rope_landed, 16)
                sp.dma_start(swap[:, :], G.d["rope_swap"]).then_inc(rope_landed, 16)
                G.ws.run_ahead(sp)

            @block.tensor
            def _(pe):
                pe.wait_ge(rope_landed, 48)
                for n, r in enumerate(rows):
                    pe.matmul(ps[:, n, 0:SEQ], swap[:, :], r, start=True, stop=True).then_inc(swapped, 1)

            @block.vector
            def _(dve):
                step = Steps(dve, step_sem)
                dve.wait_ge(rope_landed, 48)
                for n, r in enumerate(rows):
                    dve.wait_ge(swapped, n + 1)
                    step(dve.tensor_tensor(t[:, n, :], ps[:, n, 0:SEQ], sin[:, :], ALU.mult))
                    step(dve.tensor_tensor(r, r, cos[:, :], ALU.mult))
                    step.wait()
                    step(dve.tensor_tensor(r, r, t[:, n, :], ALU.add))
                step.wait()


def mixer_ab(nc, G):
    ws = G.ws
    u0 = ws.first["ab_in"]
    with scope():
        cat = sbuf(nc, "cat", [P, 4, D], F32)
        with scope():
            hm = sbuf(nc, "hm", [P, 4, 512], F32)
            so = sbuf(nc, "sig_o", [P, 4, 512], F32)
            qa = sbuf(nc, "qa", [P, 4, TOK], F32)
            ka = sbuf(nc, "ka", [P, 2, TOK], F32)
            va = sbuf(nc, "va", [P, 4, P], F32)
            with scope():
                qT = sbuf(nc, "qT", [P, H_M, TOK], F32)
                kT = sbuf(nc, "kT", [P, H_M, TOK], F32)
                v1 = sbuf(nc, "v1", [P, 4, H_M, 129], F32)
                gcol = sbuf(nc, "gcol", [P, 2, 2, 4, H_M], F32)
                negM = sbuf(nc, "negM", [H_M, 2, TOK], F32)
                with scope():
                    gi = sbuf(nc, "gi", [H_M, 2, TOK], F32)
                    gf = sbuf(nc, "gf", [H_M, 2, TOK], F32)
                    with scope():
                        hT = sbuf(nc, "hT", [P, DC, TOK], F32)
                        with stage(nc, "ones_set") as (block, ones_set):
                            @block.gpsimd
                            def _(pool):
                                pool.memset(v1[:, :, :, 128:129], 1.0).then_inc(ones_set, 1)
                                pool.wait_ge(ones_set, 1)
                        transpose_in(nc, G, "h1", lambda t, c: G.x[:, t, c * P:(c + 1) * P], [0, 1, 2, 3], hT,
                                     scale=lambda c, q: G.mod[:, DC + c, q:q + 1], shift=lambda c, q: G.mod[:, c, q:q + 1])

                        def unit(k, n=512):
                            return ws.slot(u0 + k)[:, 0:DC * n].rearrange("p (c n) -> p c n", c=DC)

                        def cols(k, off, m, eng, dst, n=512, scale=1.0):
                            return Job(u0 + k, DC, lambda c: unit(k, n)[:, c, off:off + m], lambda c: hT[:, c, :], m, TOK,
                                       eng, dst, scale=scale)

                        def rows(k, t, off, m, eng, dst, n=512, func=None, view=None):
                            return Job(u0 + k, DC, lambda c: hT[:, c, t * P:(t + 1) * P],
                                       lambda c: unit(k, n)[:, c, off:off + m], P, m, eng, dst, func=func, view=view)
                        jobs = []
                        for h in range(4):
                            jobs.append(cols(0, h * P, P, "vs"[h % 2], qT[:, h, :]))
                        for h in range(4):
                            jobs.append(cols(1, h * P, P, "vs"[h % 2], kT[:, h, :], scale=DH_M ** -0.5))
                        for t in range(4):
                            jobs.append(rows(2, t, 0, 512, "v", v1[:, t, :, 0:128],
                                             view=lambda a: a.rearrange("p (h c) -> p h c", h=4)))
                        for t in range(4):
                            jobs.append(rows(3, t, 0, 512, "s", so[:, t, :], func=ACT.Sigmoid))
                        for h in range(4):
                            jobs.append(cols(4, h * P, P, "vs"[h % 2], qa[:, h, :]))
                        for g in range(2):
                            jobs.append(cols(5, g * P, P, "vs"[g % 2], ka[:, g, :], n=400))
                        for t in range(4):
                            jobs.append(rows(5, t, 256, P, "vs"[t % 2], va[:, t, :], n=400))
                        for d in range(2):
                            jobs.append(cols(5, 384 + 4 * d, 4, "v", gi[:, d, :], n=400))
                            jobs.append(cols(5, 392 + 4 * d, 4, "s", gf[:, d, :], n=400))
                        project(nc, G, "ab_in", jobs)
                    mlstm_gates(nc, G, gi, gf, gcol, negM)
                mlstm(nc, G, qT, kT, v1, gcol, negM, hm)
            head_norm(nc, G, "ab", lambda n: hm[:, n, :].rearrange("p (h c) -> p h c", h=H_M), 4, H_M, DH_M,
                      G.d["ab_norm_w"], lambda n: so[:, n, :].rearrange("p (h c) -> p h c", h=H_M),
                      lambda n: cat[:, n, 0:512].rearrange("p (h c) -> p h c", h=H_M), LN_EPS)
            rope(nc, G, qa, ka)
            with scope():
                wm = sbuf(nc, "window_mask", [P, 2, TOK], F32)
                sink = sbuf(nc, "sink", [P, H_A], F32)
                with stage(nc, "wm_landed") as (block, wm_landed):
                    @block.sync
                    def _(sp):
                        sp.dma_start(wm[:, :, :], G.d["window_mask"]).then_inc(wm_landed, 16)
                        sp.dma_start(sink[:, :], G.d["ab_sink"].partition_broadcast(P)).then_inc(wm_landed, 16)
                        sp.wait_ge(wm_landed, 32)
                items = []
                for t in range(4):
                    for h in range(H_A):
                        o, g = (h % 2) * DH_A, h // (H_A // H_KV)
                        keys = range(4) if t < 2 else (2, 3)
                        k0 = 0 if t < 2 else SEQ
                        items.append(Item(qa[o:o + DH_A, h // 2, t * P:(t + 1) * P], ka[o:o + DH_A, g, k0:TOK],
                                          TOK - k0, wm[:, t, :] if t < 2 else None, sink[:, h:h + 1],
                                          [va[:, k, g * DH_A:(g + 1) * DH_A] for k in keys],
                                          cat[:, t, 512 + h * DH_A:512 + (h + 1) * DH_A]))
                attend(nc, G, items)
        with scope():
            catT = sbuf(nc, "catT", [P, DC, TOK], F32)
            grow = sbuf(nc, "gate_row", [P, 2, D], F32)
            transpose_in(nc, G, "cat", lambda t, c: cat[:, t, c * P:(c + 1) * P], [0, 1, 2, 3], catT)
            gate_rows(nc, G, 2, [0, 1], grow)
            with_rows(nc, G, 0, 0, [0, 1, 2, 3], out_project(G, ws.first["ab_out"], [0, 1, 2, 3], catT), grow)


def with_rows(nc, G, layer, which, tiles, pre, grow, banks=lambda n: 2 * n):
    with scope():
        wr = sbuf(nc, "ln_w_row", [P, D], F32)
        br = sbuf(nc, "ln_b_row", [P, D], F32)
        with stage(nc, "ln_landed") as (block, ln_landed):
            @block.sync
            def _(sp):
                sp.dma_start(wr[:, :], G.d["ln_w"][layer * 2 + which].partition_broadcast(P)).then_inc(ln_landed, 16)
                sp.dma_start(br[:, :], G.d["ln_b"][layer * 2 + which].partition_broadcast(P)).then_inc(ln_landed, 16)
                sp.wait_ge(ln_landed, 32)
        rows = {"w": wr[:, :], "b": br[:, :], 0: grow[:, 0, :], 1: grow[:, 1, :]}
        residual_norm(nc, G, "ln", tiles, banks, lambda k: rows[k], [t // 2 for t in tiles], "ln", pre)



PAIRS = PEER_HEADS * PEER_TOPK
PT = 2
NJ = N_KEYS // 2


def top16(dve, step, lanes):
    for vals, idx, src, work in lanes:
        step(dve.max(vals[:, 0:8], src))
    step.wait()
    for vals, idx, src, work in lanes:
        step(dve.max_index(idx[:, 0:8], vals[:, 0:8], src))
        step(dve.match_replace(work, vals[:, 0:8], src, TAKEN))
    step.wait()
    for vals, idx, src, work in lanes:
        step(dve.max(vals[:, 8:16], work))
    step.wait()
    for vals, idx, src, work in lanes:
        step(dve.max_index(idx[:, 8:16], vals[:, 8:16], work))
    step.wait()


def peer_select(nc, G, layer, scores, table):
    ps = G.ps
    LANES = 4
    with scope():
        work = sbuf(nc, "top_work", [P, LANES, 256], F32)
        cand = sbuf(nc, "cand", [P, LANES, 256], F32)
        top = sbuf(nc, "top_vals", [P, 2 * PEER_HEADS, 16], F32)
        ti = sbuf(nc, "top_idx", [P, 2 * PEER_HEADS, 16], U32)
        tif = sbuf(nc, "top_idx_f", [P, 2 * PEER_HEADS, 16], F32)
        best = sbuf(nc, "best", [P, PT, PEER_HEADS, 16], F32)
        pos = sbuf(nc, "best_pos", [P, PEER_HEADS, 16], U32)
        half = sbuf(nc, "pos_half", [P, 2, PAIRS], U32)
        halff = sbuf(nc, "pos_half_f", [P, 2, PAIRS], F32)
        hot = sbuf(nc, "one_hot", [P, 2, PAIRS, 16], F32)
        keyed = sbuf(nc, "one_hot_key", [P, 2, PAIRS, 16], F32)
        sel = sbuf(nc, "selected", [P, PT, 3, PAIRS], F32)
        shift = sbuf(nc, "best_shift", [P, PT, PEER_HEADS, 16], F32)
        ex = sbuf(nc, "best_exp", [P, PT, PEER_HEADS, 16], F32)
        sm = sbuf(nc, "best_sum", [P, PEER_HEADS, 2], F32)
        with stage(nc, "sel_step", "shift_ready", "best_exp_ready", "hot_ready", "keyed_ready", "sel_ready",
                   "sel_turned") as (
                block, step_sem, shift_ready, exp_ready, hot_ready, keyed_ready, sel_ready, sel_turned):
            @block.vector
            def _(dve):
                step = Steps(dve, step_sem)
                for t in range(PT):
                    for n0 in range(0, 2 * PEER_HEADS, LANES):
                        top16(dve, step, [(top[:, n, :], ti[:, n, :], scores[:, t, n, :], work[:, n - n0, 0:N_KEYS])
                                          for n in range(n0, n0 + LANES)])
                    if t > 0:
                        dve.wait_ge(keyed_ready, 2 * t)
                    step(dve.tensor_copy(tif[:, :, :], ti[:, :, :]))
                    for h0 in range(0, PEER_HEADS, LANES):
                        for h in range(h0, h0 + LANES):
                            c3 = cand[:, h - h0, :].rearrange("p (a b) -> p a b", a=16)
                            step(dve.tensor_tensor(c3, top[:, 2 * h, :].unsqueeze(2).broadcast_to([P, 16, 16]),
                                                   top[:, 2 * h + 1, :].unsqueeze(1).broadcast_to([P, 16, 16]), ALU.add))
                        step.wait()
                        top16(dve, step, [(best[:, t, h, :], pos[:, h, :], cand[:, h - h0, :], work[:, h - h0, :])
                                          for h in range(h0, h0 + LANES)])
                    dve.tensor_tensor(shift[:, t, :, :], best[:, t, :, :],
                                      best[:, t, :, 0:1].broadcast_to([P, PEER_HEADS, 16]),
                                      ALU.subtract).then_inc(shift_ready, 1)
                    pflat = pos[:, :, :].rearrange("p h m -> p (h m)")
                    step(dve.tensor_scalar(half[:, 0, :], pflat, 4, None, ALU.logical_shift_right))
                    step(dve.tensor_scalar(half[:, 1, :], pflat, 15, None, ALU.bitwise_and))
                    step.wait()
                    step(dve.tensor_copy(halff[:, :, :], half[:, :, :]))
                    step.wait()
                    for which in range(2):
                        dve.tensor_tensor(hot[:, which, :, :],
                                          halff[:, which, :].unsqueeze(2).broadcast_to([P, PAIRS, 16]),
                                          G.iota[:, 0:16].unsqueeze(1).broadcast_to([P, PAIRS, 16]),
                                          ALU.is_equal).then_inc(hot_ready, 1)
                    dve.wait_ge(exp_ready, t + 1)
                    step(dve.tensor_reduce(sm[:, :, 0], ex[:, t, :, :], AX.X, ALU.add))
                    step.wait()
                    step(dve.reciprocal(sm[:, :, 1], sm[:, :, 0]))
                    step.wait()
                    dve.tensor_tensor(sel[:, t, 2, :].rearrange("p (h m) -> p h m", h=PEER_HEADS), ex[:, t, :, :],
                                      sm[:, :, 1:2].broadcast_to([P, PEER_HEADS, 16]), ALU.mult).then_inc(sel_ready, 1)
                    for which in range(2):
                        dve.wait_ge(keyed_ready, 2 * t + which + 1)
                        dve.tensor_reduce(sel[:, t, which, :], keyed[:, which, :, :], AX.X, ALU.add).then_inc(sel_ready, 1)
                    dve.wait_ge(sel_ready, 3 * (t + 1))
                for t in range(PT):
                    dve.wait_ge(sel_turned, t + 1)
                    step(dve.tensor_copy(table[:, :, t * P:(t + 1) * P],
                                         ps[:, t, 0:3 * P].rearrange("p (k c) -> p k c", k=3)))
                step.wait()

            @block.gpsimd
            def _(pool):
                for t in range(PT):
                    for which in range(2):
                        pool.wait_ge(hot_ready, 2 * t + which + 1)
                        if t > 0:
                            pool.wait_ge(sel_ready, 3 * t)
                        k = keyed[:, which, :, :].rearrange("p (h m) c -> p h m c", h=PEER_HEADS)
                        o = hot[:, which, :, :].rearrange("p (h m) c -> p h m c", h=PEER_HEADS)
                        ids = tif[:, which::2, :].unsqueeze(2).broadcast_to([P, PEER_HEADS, 16, 16])
                        pool.tensor_tensor(k, o, ids, ALU.mult).then_inc(keyed_ready, 1)

            @block.scalar
            def _(act):
                for t in range(PT):
                    act.wait_ge(shift_ready, t + 1)
                    act.activation(ex[:, t, :, :], shift[:, t, :, :], ACT.Exp).then_inc(exp_ready, 1)

            @block.tensor
            def _(pe):
                for t in range(PT):
                    pe.wait_ge(sel_ready, 3 * (t + 1))
                    for k in range(3):
                        mm = pe.transpose(ps[:, t, k * P:(k + 1) * P], sel[:, t, k, :], G.ident[:, :])
                    mm.then_inc(sel_turned, 1)


def peer_table(nc, G, table, wt, spill):
    ps = G.ps
    GRP = 4
    BUFS = 2
    with scope():
        second = sbuf(nc, "second_half", [P, NJ, PT * P], F32)
        hi = sbuf(nc, "hot_i", [P, BUFS, GRP, P], F32)
        hj = sbuf(nc, "hot_j", [P, BUFS, GRP, P], F32)
        steps = PT * P // GRP
        with stage(nc, "i_ready", "j_ready", "weighted", "w_ready", "w_out", "spilled") as (
                block, i_ready, j_ready, weighted, w_ready, w_out, spilled):
            @block.vector
            def _(dve):
                def step(g, b, free):
                    if free is not None:
                        dve.wait_ge(w_ready, free)
                    dve.tensor_tensor(hj[:, b, :, :], G.iota[:, :].unsqueeze(1).broadcast_to([P, GRP, P]),
                                      table[:, 1, ds(g * GRP, GRP)].unsqueeze(2).broadcast_to([P, GRP, P]),
                                      ALU.is_equal).then_inc(j_ready, 1)
                    dve.tensor_tensor(hi[:, b, :, :], G.iota[:, :].unsqueeze(1).broadcast_to([P, GRP, P]),
                                      table[:, 0, ds(g * GRP, GRP)].unsqueeze(2).broadcast_to([P, GRP, P]),
                                      ALU.is_equal).then_inc(i_ready, 1)

                step(0, 0, None)
                step(1, 1, None)
                with dve.Fori(1, steps // 2) as it:
                    step(it * 2, 0, it * 2 - 1)
                    step(it * 2 + 1, 1, it * 2)

            @block.gpsimd
            def _(pool):
                def step(g, b, ready):
                    pool.wait_ge(j_ready, ready)
                    pool.tensor_tensor(hj[:, b, :, :], hj[:, b, :, :],
                                       table[:, 2, ds(g * GRP, GRP)].unsqueeze(2).broadcast_to([P, GRP, P]),
                                       ALU.mult).then_inc(weighted, 1)

                with pool.Fori(0, steps // 2) as it:
                    step(it * 2, 0, it * 2 + 1)
                    step(it * 2 + 1, 1, it * 2 + 2)

            @block.tensor
            def _(pe):
                def step(b, bank, ready, free):
                    pe.wait_ge(i_ready, ready)
                    pe.wait_ge(weighted, ready)
                    if free is not None:
                        pe.wait_ge(w_out, free)
                    for k in range(GRP):
                        mm = pe.matmul(ps[:, bank, k * P:(k + 1) * P], hi[:, b, k, :], hj[:, b, k, :], start=True, stop=True)
                    mm.then_inc(w_ready, 1)

                for g in range(4):
                    step(g % 2, g, g + 1, None)
                with pe.Fori(1, steps // 4) as it:
                    for g in range(4):
                        step(g % 2, g, it * 4 + (g + 1), it * 4 + (g - 3))

            @block.scalar
            def _(act):
                with act.Fori(0, steps // 4) as it:
                    for g in range(4):
                        act.wait_ge(w_ready, it * 4 + (g + 1))
                        w = ps[:, g, :].rearrange("p (t j) -> p j t", t=GRP)
                        at = ds(it * (4 * GRP) + g * GRP, GRP)
                        act.activation(wt[:, :, at], w[:, 0:NJ, :], ACT.Identity)
                        act.activation(second[:, :, at], w[:, NJ:, :], ACT.Identity).then_inc(w_out, 1)

            @block.sync
            def _(sp):
                G.ws.run_ahead(sp)
                for t in range(PT):
                    sp.wait_ge(w_out, (t + 1) * P // GRP)
                    sp.dma_start(spill[:, :, t * P:(t + 1) * P], second[:, :, t * P:(t + 1) * P]).then_inc(spilled, 16)
                sp.wait_ge(spilled, 16 * PT)


def peer_experts(nc, G, u0, hs, wt, first, spill):
    ps, ws = G.ps, G.ws
    UJ = 2
    BODY = UJ * SLOTS
    TURNS = NJ // BODY
    REST = NJ - TURNS * BODY
    SKEW = 2
    W = PT * P
    hT_h, hT_l = hs
    with scope():
        uh = sbuf(nc, "u_high", [P, 2, D], F32R)
        ul = sbuf(nc, "u_low", [P, 2, D], F32R)
        vh = sbuf(nc, "v_high", [P, 2, D], F32R)
        vl = sbuf(nc, "v_low", [P, 2, D], F32R)
        ge = sbuf(nc, "activated", [P, 2, W], F32)
        aw = sbuf(nc, "weighted", [P, W], F32)
        ah = sbuf(nc, "weighted_high", [P, 2, W], F32R)
        al = sbuf(nc, "weighted_low", [P, 2, W], F32R)
        zz = sbuf(nc, "zeros", [P, P], F32)
        with stage(nc, "zeros_set", "u_high_done", "u_split", "v_high_done", "v_split", "scored", "gelu_done", "aw_done",
                   "aw_high_done", "aw_split", "pv_done", "w_landed") as (
                block, zeros_set, uh_done, u_split, vh_done, v_split, scored, gelu_done, aw_done, ah_done, aw_split,
                pv_done, w_landed):
            def u_of(r):
                return ws.slot(u0 + r // UJ)[:, (r % UJ) * D:(r % UJ + 1) * D]

            def v_of(r):
                return ws.slot(u0 + r // UJ)[:, (UJ + r % UJ) * D:(UJ + r % UJ + 1) * D]

            def turns(eng, body):
                for r in range(BODY):
                    body(r, 0, True, False)
                with eng.Fori(1, TURNS) as it:
                    for r in range(BODY):
                        body(r, it * BODY, False, False)
                for r in range(REST):
                    body(r, TURNS * BODY, False, True)

            @block.tensor
            def _(pe):
                def scores(r, base, early):
                    pe.wait_ge(u_split, base + (r + 1))
                    if not (early and r < 3):
                        pe.wait_ge(gelu_done, base + (r - 2))
                    b, o = r % 2, ps[:, r % 3, 0:W]
                    for c in range(DC):
                        s = slice(c * P, (c + 1) * P)
                        pe.matmul(o, uh[:, b, s], hT_h[:, c, :], start=(c == 0), stop=False)
                        pe.matmul(o, uh[:, b, s], hT_l[:, c, :], start=False, stop=False)
                        mm = pe.matmul(o, ul[:, b, s], hT_h[:, c, :], start=False, stop=(c == DC - 1))
                    mm.then_inc(scored, 1)

                def products(r, base):
                    pe.wait_ge(aw_split, base + (r + 1))
                    pe.wait_ge(v_split, base + (r + 1))
                    b = r % 2
                    for t in range(PT):
                        for x, y in ((ah, vh), (ah, vl), (al, vh)):
                            for h in range(2):
                                mm = pe.matmul(ps[:, 4 + 2 * t + h, :], x[:, b, t * P:(t + 1) * P],
                                               y[:, b, h * 512:(h + 1) * 512], start=False, stop=False,
                                               skip_group_check=True)
                    mm.then_inc(pv_done, 1)

                def body(r, base, early, late):
                    if not (late and r + SKEW >= REST):
                        scores(r + SKEW, base, early)
                    products(r, base)

                if first:
                    pe.wait_ge(zeros_set, 1)
                    for b in range(4):
                        pe.matmul(ps[:, 4 + b, :], zz[:, :], wt[:, 0:2, :].rearrange("p j t -> p (j t)"), start=True,
                                  stop=False, skip_group_check=True)
                for r in range(SKEW):
                    scores(r, 0, True)
                turns(pe, body)
            for n in range(NJ // UJ):
                ws.done(u0 + n, v_split, (n + 1) * UJ)

            @block.scalar
            def _(act):
                def u_high(r, base, early):
                    if r % UJ == 0:
                        n = u0 + r // UJ
                        act.wait_ge(ws.landed[n % SLOTS], landed(n, base))
                    if not (early and r < 2):
                        act.wait_ge(scored, base + (r - 1))
                    act.activation(uh[:, r % 2, :], u_of(r), ACT.Identity).then_inc(uh_done, 1)

                def landed(n, base):
                    value = 16 * (n // SLOTS + 1)
                    if isinstance(base, int):
                        return value + base // BODY * 16
                    return base // BODY * 16 + value

                def body(r, base, early, late):
                    act.wait_ge(scored, base + (r + 1))
                    if not (early and r < 2):
                        act.wait_ge(aw_done, base + (r - 1))
                    act.activation(ge[:, r % 2, :], ps[:, r % 3, 0:W], ACT.Gelu).then_inc(gelu_done, 1)
                    if not (late and r + SKEW >= REST):
                        u_high(r + SKEW, base, early)
                    if not (early and r < 2):
                        act.wait_ge(pv_done, base + (r - 1))
                    act.activation(vh[:, r % 2, :], v_of(r), ACT.Identity).then_inc(vh_done, 1)

                for r in range(SKEW):
                    u_high(r, 0, True)
                turns(act, body)

            @block.vector
            def _(dve):
                def u_low(r, base, early):
                    dve.wait_ge(uh_done, base + (r + 1))
                    if not (early and r < 2):
                        dve.wait_ge(scored, base + (r - 1))
                    dve.tensor_tensor(ul[:, r % 2, :], u_of(r), uh[:, r % 2, :].bitcast(F32),
                                      ALU.subtract).then_inc(u_split, 1)

                def body(r, base, early, late):
                    j = base + r
                    w = wt[:, j, :] if isinstance(j, int) else wt[:, ds(j, 1), :].squeeze(1)
                    b = r % 2
                    dve.wait_ge(gelu_done, base + (r + 1))
                    if not (early and r < 1):
                        dve.wait_ge(aw_split, base + r)
                    dve.tensor_tensor(aw[:, :], ge[:, b, :], w, ALU.mult).then_inc(aw_done, 1)
                    if not (late and r + SKEW >= REST):
                        u_low(r + SKEW, base, early)
                    dve.wait_ge(aw_done, base + (r + 1))
                    if not (early and r < 2):
                        dve.wait_ge(pv_done, base + (r - 1))
                    dve.tensor_copy(ah[:, b, :], aw[:, :]).then_inc(ah_done, 1)
                    dve.wait_ge(ah_done, base + (r + 1))
                    dve.tensor_tensor(al[:, b, :], aw[:, :], ah[:, b, :].bitcast(F32), ALU.subtract).then_inc(aw_split, 1)
                    dve.wait_ge(vh_done, base + (r + 1))
                    dve.tensor_tensor(vl[:, b, :], v_of(r), vh[:, b, :].bitcast(F32), ALU.subtract).then_inc(v_split, 1)

                if first:
                    dve.memset(zz[:, :], 0.0).then_inc(zeros_set, 1)
                for r in range(SKEW):
                    u_low(r, 0, True)
                turns(dve, body)

            @block.sync
            def _(sp):
                assert ws.issued - u0 == SLOTS
                rounds = (NJ // UJ - SLOTS) // SLOTS
                src = G.d[f"peer_uv{G.layer}"]
                s0 = (SLOTS + u0 - ws.first[f"peer{G.layer}{G.col}"] - 4)
                with sp.Fori(0, rounds) as it:
                    for r in range(SLOTS):
                        n = u0 + SLOTS + r
                        sp.wait_ge(v_split, it * BODY + (r + 1) * UJ)
                        sp.dma_start(ws.slot(n), src[ds(it * SLOTS + (s0 + r), 1)].squeeze(0)).then_inc(
                            ws.landed[n % SLOTS], 16)
                    if first:
                        sp.wait_ge(aw_done, it * BODY + BODY)
                        at = ds(it * BODY, BODY)
                        sp.dma_start(wt[:, at, :], spill[:, at, :]).then_inc(w_landed, 16)
                ws.issued += rounds * SLOTS
                ws.run_ahead(sp)
                if first:
                    sp.wait_ge(aw_done, NJ)
                    sp.dma_start(wt[:, rounds * BODY:, :], spill[:, rounds * BODY:, :]).then_inc(w_landed, 16)
                    sp.wait_ge(w_landed, 16 * (rounds + 1))
    ws.stage_over()


def split_T(nc, G, hT, hs):
    with stage(nc, "high_done", "low_done") as (block, high_done, low_done):
        @block.scalar
        def _(act):
            for c in range(0, DC, 2):
                act.activation(hs[0][:, c:c + 2, :], hT[:, c:c + 2, :], ACT.Identity).then_inc(high_done, 1)

        @block.vector
        def _(dve):
            for c in range(0, DC, 2):
                dve.wait_ge(high_done, c // 2 + 1)
                dve.tensor_tensor(hs[1][:, c:c + 2, :], hT[:, c:c + 2, :], hs[0][:, c:c + 2, :].bitcast(F32),
                                  ALU.subtract).then_inc(low_done, 1)


def peer(nc, G, layer, col, tiles):
    ws = G.ws
    G.layer, G.col = layer, col
    key = f"peer{layer}{col}"
    u0 = ws.first[key]
    spill = nc.dram_tensor(f"spill_{key}", [P, NJ, PT * P], F32).ap()

    def modulated(hT):
        transpose_in(nc, G, "h2", lambda t, c: G.x[:, t, c * P:(c + 1) * P], tiles, hT,
                     scale=lambda c, _: G.mod[:, 4 * DC + c, col:col + 1], shift=lambda c, _: G.mod[:, 3 * DC + c, col:col + 1])

    with scope():
        table = sbuf(nc, "pair_table", [P, 3, PT * P], F32)
        with scope():
            scores = sbuf(nc, "key_scores", [P, PT, 2 * PEER_HEADS, N_KEYS], F32)
            with scope():
                hT = sbuf(nc, "peer_hT", [P, DC, PT * P], F32)
                keysT = sbuf(nc, "keysT", [P, 2 * PEER_HEADS, N_KEYS], F32)
                pq = sbuf(nc, "peer_q", [P, 2 * PEER_HEADS, PT * P], F32)
                modulated(hT)
                with stage(nc, "keys_landed") as (block, keys_landed):
                    @block.sync
                    def _(sp):
                        sp.dma_start(keysT[:, :, :], G.d["peer_keysT"][layer]).then_inc(keys_landed, 16)
                        sp.wait_ge(keys_landed, 16)
                jobs = []
                for n in range(2 * PEER_HEADS):
                    w = ws.slot(u0 + n // 4).rearrange("p (c n) -> p c n", c=DC)
                    jobs.append(Job(u0 + n // 4, DC, lambda c, w=w, n=n: w[:, c, (n % 4) * P:(n % 4 + 1) * P],
                                    lambda c: hT[:, c, :], P, PT * P, "vs"[n % 2], pq[:, n, :]))
                project(nc, G, "peer_q", jobs)
                jobs = []
                for t in range(PT):
                    for n in range(2 * PEER_HEADS):
                        jobs.append(Job(None, 1, lambda c, t=t, n=n: pq[:, n, t * P:(t + 1) * P],
                                        lambda c, n=n: keysT[:, n, :], P, N_KEYS, "vs"[n % 2], scores[:, t, n, :]))
                project(nc, G, "peer_s", jobs)
            peer_select(nc, G, layer, scores, table)
        with scope():
            wt = sbuf(nc, "expert_weights", [P, NJ, PT * P], F32)
            peer_table(nc, G, table, wt, spill)
            hs = [sbuf(nc, f"peer_hT_{k}", [P, DC, PT * P], F32R) for k in ("high", "low")]
            with scope():
                hT = sbuf(nc, "peer_hT", [P, DC, PT * P], F32)
                modulated(hT)
                split_T(nc, G, hT, hs)
            for half in range(2):
                peer_experts(nc, G, u0 + 4 + half * NJ // 2, hs, wt, half == 0, spill)
    with scope():
        grow = sbuf(nc, "gate_row", [P, 2, D], F32)
        gate_rows(nc, G, 5, [col], grow, banks=4)
        with_rows(nc, G, layer, 1, tiles, None, grow, banks=lambda n: 4 + 2 * n)




def chain_order(d):
    order = [(t, n) for t in range(2) for n in range(2)]
    return order if d == 0 else order[::-1]


def linear_prepare(nc, G, d, units, heads, la, qT, kT, kn, mask, qz, at, kd, etot):
    ps = G.ps
    W = units * P
    dk = P // heads
    work = [(t, u) for t in range(2) for u in range(units)]
    with scope():
        ex = sbuf(nc, "decays", [P, 2, 3 * P], F32)
        ea = sbuf(nc, "decay_after", [P, 2, W], F32)
        qr = sbuf(nc, "q_rel", [P, 2, P], F32)
        kr = sbuf(nc, "k_rel", [P, 2, P], F32)
        with stage(nc, "zeroed", "cum_ready", "after_ready", "ex_ready", "ea_ready", "rel_ready", "qz_ready", "at_ready",
                   "at_out", "kd_ready") as (
                block, zeroed, cum_ready, after_ready, ex_ready, ea_ready, rel_ready, qz_ready, at_ready, at_out, kd_ready):
            @block.tensor
            def _(pe):
                for t in range(2):
                    pe.matmul(ps[:, 2 + t, 0:W], mask[:, 2, :], la[:, t, :], start=True, stop=True).then_inc(after_ready, 1)

                def own(i):
                    pe.wait_ge(rel_ready, 2 * (i + 1))
                    if i >= 2:
                        pe.wait_ge(at_out, i - 1)
                    for a in range(heads):
                        mm = pe.matmul(ps[:, 4 + 2 * (i % 2) + a, 0:P], kr[a * dk:(a + 1) * dk, i % 2, :],
                                       qr[a * dk:(a + 1) * dk, i % 2, :], start=True, stop=True)
                    mm.then_inc(at_ready, 1)

                for i, (t, u) in enumerate(work):
                    if i >= 2:
                        pe.wait_ge(ex_ready, 2 * (i - 1))
                    pe.matmul(ps[:, i % 2, 0:2 * P], la[:, t, u * P:(u + 1) * P],
                              mask[:, 0:2, :].rearrange("p a b -> p (a b)"), start=True, stop=True).then_inc(cum_ready, 1)
                    if i >= 1:
                        own(i - 1)
                own(len(work) - 1)

            @block.scalar
            def _(act):
                for t in range(2):
                    act.wait_ge(after_ready, t + 1)
                    act.activation(ea[:, t, :], ps[:, 2 + t, 0:W], ACT.Exp).then_inc(ea_ready, 1)
                for i, (t, u) in enumerate(work):
                    act.wait_ge(cum_ready, i + 1)
                    if i >= 2:
                        act.wait_ge(qz_ready, i - 1)
                    act.activation(ex[:, i % 2, 0:2 * P], ps[:, i % 2, 0:2 * P], ACT.Exp).then_inc(ex_ready, 1)
                    act.activation(ex[:, i % 2, 2 * P:3 * P], ps[:, i % 2, P:2 * P], ACT.Exp, scale=-1.0).then_inc(ex_ready, 1)

            @block.gpsimd
            def _(pool):
                pool.memset(qz[:, :, :, :, :], 0.0).then_inc(zeroed, 1)

            @block.vector
            def _(dve):
                for t in range(2):
                    dve.wait_ge(ea_ready, t + 1)
                    dve.tensor_tensor(kd[:, t, :], kn[:, t, :], ea[:, t, :], ALU.mult).then_inc(kd_ready, 1)
                dve.wait_ge(zeroed, 1)

                def weights_out(i):
                    t, u = work[i]
                    dve.wait_ge(at_ready, i + 1)
                    for a in range(heads):
                        last = dve.tensor_tensor(at[:, t, u, a, :], ps[:, 4 + 2 * (i % 2) + a, 0:P], mask[:, 3, :], ALU.mult)
                    last.then_inc(at_out, 1)

                for i, (t, u) in enumerate(work):
                    e = ex[:, i % 2, :]
                    cols = slice(t * P, (t + 1) * P)
                    dve.wait_ge(ex_ready, 2 * (i + 1))
                    if i >= 2:
                        dve.wait_ge(at_ready, i - 1)
                    dve.tensor_tensor(qr[:, i % 2, :], qT[:, u, cols], e[:, P:2 * P], ALU.mult).then_inc(rel_ready, 1)
                    dve.tensor_tensor(kr[:, i % 2, :], kT[:, u, cols], e[:, 2 * P:3 * P], ALU.mult).then_inc(rel_ready, 1)
                    for n in range(2):
                        own = slice(n * CHUNK, (n + 1) * CHUNK)
                        dve.tensor_tensor(qz[:, t, u, n, own], qT[:, u, t * P + n * CHUNK:t * P + (n + 1) * CHUNK],
                                          e[:, own], ALU.mult)
                    end = CHUNK - 1 if d == 0 else 0
                    dve.tensor_copy(etot[:, t, u, :], e[:, end:P:CHUNK]).then_inc(qz_ready, 1)
                    if i >= 1:
                        weights_out(i - 1)
                weights_out(len(work) - 1)

            @block.sync
            def _(sp):
                G.ws.run_ahead(sp)


def linear_scan(nc, G, d, units, heads, dv, v, qz, at, kd, etot, state, pair_mask, out, add):
    ps = G.ps
    order = chain_order(d)
    work = [(t, u) for t in range(2) for u in range(units)]
    hv = dv // heads
    with scope():
        up = sbuf(nc, "update", [P, 2, dv], F32)
        with stage(nc, "update_ready", "update_masked", "state_ready", "o_ready", "o_out") as (
                block, update_ready, update_masked, state_ready, o_ready, o_out):
            @block.tensor
            def _(pe):
                k = 0
                for n, (t, c) in enumerate(order[:3]):
                    rows = slice(c * CHUNK, (c + 1) * CHUNK)
                    for u in range(units):
                        if k >= 4:
                            pe.wait_ge(update_masked if heads == 2 else state_ready, k - 3)
                        pe.matmul(ps[:, k % 4, 0:dv], kd[rows, t, u * P:(u + 1) * P], v[rows, t, u * dv:(u + 1) * dv],
                                  start=True, stop=True).then_inc(update_ready, 1)
                        k += 1
                pe.wait_ge(state_ready, 3 * units)
                for i, (t, u) in enumerate(work):
                    if i >= 4:
                        pe.wait_ge(o_out, i - 3)
                    o = ps[:, 4 + i % 4, 0:dv]
                    for c in range(2):
                        pe.matmul(o, qz[:, t, u, c, :], state[:, order.index((t, c)), u, :], start=(c == 0), stop=False,
                                  skip_group_check=True)
                    for a in range(heads):
                        mm = pe.matmul(o[:, a * hv:(a + 1) * hv], at[:, t, u, a, :],
                                       v[:, t, u * dv + a * hv:u * dv + (a + 1) * hv], start=False, stop=True,
                                       skip_group_check=True)
                    mm.then_inc(o_ready, 1)

            @block.vector
            def _(dve):
                k = 0
                for n, (t, c) in enumerate(order[:3]):
                    for u in range(units):
                        dve.wait_ge(update_ready, k + 1)
                        upd = ps[:, k % 4, 0:dv]
                        if heads == 2:
                            if k >= 2:
                                dve.wait_ge(state_ready, k - 1)
                            dve.tensor_tensor(up[:, k % 2, :], upd, pair_mask, ALU.mult).then_inc(update_masked, 1)
                            dve.wait_ge(update_masked, k + 1)
                            upd = up[:, k % 2, :]
                        if n >= 1:
                            dve.wait_ge(state_ready, k - units + 1)
                        dve.scalar_tensor_tensor(state[:, n + 1, u, :], state[:, n, u, :], etot[:, t, u, c:c + 1], upd,
                                                 ALU.mult, ALU.add).then_inc(state_ready, 1)
                        k += 1
                for i, (t, u) in enumerate(work):
                    dve.wait_ge(o_ready, i + 1)
                    o, src = out[:, t, u * dv:(u + 1) * dv], ps[:, 4 + i % 4, 0:dv]
                    if add:
                        dve.tensor_tensor(o, src, o, ALU.add).then_inc(o_out, 1)
                    else:
                        dve.tensor_copy(o, src).then_inc(o_out, 1)

            @block.sync
            def _(sp):
                G.ws.run_ahead(sp)


def log_sigmoid(nc, G, z, parts):
    with scope():
        w = sbuf(nc, "ls_work", [P, 2, 512], F32)
        with stage(nc, "abs_ready", "e_ready", "ln_ready", "ls_out") as (block, abs_ready, e_ready, ln_ready, ls_out):
            @block.vector
            def _(dve):
                for i in range(len(parts) + 1):
                    if i < len(parts):
                        if i >= 2:
                            dve.wait_ge(ls_out, i - 1)
                        p = parts[i]
                        dve.scalar_tensor_tensor(w[:, i % 2, :], p, -1.0, p, ALU.mult, ALU.max).then_inc(abs_ready, 1)
                    if i >= 1:
                        p = parts[i - 1]
                        dve.wait_ge(ln_ready, i)
                        dve.scalar_tensor_tensor(p, p, 0.0, w[:, (i - 1) % 2, :], ALU.min, ALU.subtract).then_inc(ls_out, 1)

            @block.scalar
            def _(act):
                for i in range(len(parts)):
                    act.wait_ge(abs_ready, i + 1)
                    act.activation(w[:, i % 2, :], w[:, i % 2, :], ACT.Exp, scale=-1.0).then_inc(e_ready, 1)
                    act.wait_ge(e_ready, i + 1)
                    act.activation(w[:, i % 2, :], w[:, i % 2, :], ACT.Ln, bias=1.0).then_inc(ln_ready, 1)

            @block.sync
            def _(sp):
                G.ws.run_ahead(sp)


def context_state(nc, G, d, la, kn, v, mask, state):
    ps = G.ps
    with scope():
        e = sbuf(nc, "ctx_decay", [P, 2, 512], F32)
        with stage(nc, "after_ready", "e_ready", "kd_ready", "s_ready", "s_out") as (
                block, after_ready, e_ready, kd_ready, s_ready, s_out):
            @block.tensor
            def _(pe):
                for t in range(2):
                    later = 1 - t if (t == 0) == (d == 0) else None
                    mm = pe.matmul(ps[:, t, :], mask[:, 0, :], la[:, t, :], start=True, stop=later is None)
                    if later is not None:
                        mm = pe.matmul(ps[:, t, :], mask[:, 1, :], la[:, later, :], start=False, stop=True)
                    mm.then_inc(after_ready, 1)
                pe.wait_ge(kd_ready, 2)
                for h in range(H_C):
                    for t in range(2):
                        mm = pe.matmul(ps[:, 4 + h, 0:DV_C], e[:, t, h * P:(h + 1) * P], v[:, t, h * DV_C:(h + 1) * DV_C],
                                       start=(t == 0), stop=(t == 1))
                    mm.then_inc(s_ready, 1)

            @block.scalar
            def _(act):
                for t in range(2):
                    act.wait_ge(after_ready, t + 1)
                    act.activation(e[:, t, :], ps[:, t, :], ACT.Exp).then_inc(e_ready, 1)

            @block.vector
            def _(dve):
                for t in range(2):
                    dve.wait_ge(e_ready, t + 1)
                    dve.tensor_tensor(e[:, t, :], e[:, t, :], kn[:, t, :], ALU.mult).then_inc(kd_ready, 1)
                for h in range(H_C):
                    dve.wait_ge(s_ready, h + 1)
                    dve.tensor_copy(state[:, 0, h, :], ps[:, 4 + h, 0:DV_C]).then_inc(s_out, 1)

            @block.sync
            def _(sp):
                G.ws.run_ahead(sp)


def mixer_c(nc, G):
    ws = G.ws
    u0 = ws.first["gla_in"]
    with scope():
        o = sbuf(nc, "gla_o", [P, 2, 1024], F32)
        sg = sbuf(nc, "silu_g", [P, 2, 1024], F32)
        with scope():
            la = sbuf(nc, "log_a", [P, 2, 4, 512], F32)
            qT = sbuf(nc, "gla_qT", [P, H_C, SEQ], F32)
            kT = sbuf(nc, "gla_kT", [P, H_C, SEQ], F32)
            kn = sbuf(nc, "gla_k", [P, 4, 512], F32)
            v = sbuf(nc, "gla_v", [P, 4, 1024], F32)
            with scope():
                hT = sbuf(nc, "hT", [P, DC, TOK], F32)
                low = sbuf(nc, "lowT", [GATE_RANK + 1, 2, TOK], F32)
                up = sbuf(nc, "gate_up", [GATE_RANK + 1, 2, 512], F32)
                with stage(nc, "low_set", "up_landed") as (block, low_set, up_landed):
                    @block.gpsimd
                    def _(pool):
                        pool.memset(low[:, :, :], 1.0).then_inc(low_set, 1)
                        pool.wait_ge(low_set, 1)

                    @block.sync
                    def _(sp):
                        sp.dma_start(up[:, :, :], G.d["gla_gate"]).then_inc(up_landed, 16)
                        sp.wait_ge(up_landed, 16)
                transpose_in(nc, G, "h1", lambda t, c: G.x[:, t, c * P:(c + 1) * P], [0, 1, 2, 3], hT,
                             scale=lambda c, q: G.mod[:, DC + c, q:q + 1], shift=lambda c, q: G.mod[:, c, q:q + 1])

                def unit(k, n=512):
                    return ws.slot(u0 + k)[:, 0:DC * n].rearrange("p (c n) -> p c n", c=DC)

                def cols(k, off, m, eng, dst, tok, n=512, scale=1.0):
                    return Job(u0 + k, DC, lambda c: unit(k, n)[:, c, off:off + m], lambda c: hT[:, c, 0:tok], m, tok, eng,
                               dst, scale=scale)

                def rows(k, t, eng, dst, func=None):
                    return Job(u0 + k, DC, lambda c: hT[:, c, t * P:(t + 1) * P], lambda c: unit(k)[:, c, :], P, 512, eng,
                               dst, func=func)
                jobs = [cols(0, h * P, P, "vs"[h % 2], qT[:, h, :], SEQ, scale=DK_C ** -0.5) for h in range(H_C)]
                jobs += [cols(1, h * P, P, "vs"[h % 2], kT[:, h, :], SEQ) for h in range(H_C)]
                jobs += [rows(1, t, "vs"[t % 2], kn[:, t, :]) for t in range(4)]
                for half in range(2):
                    jobs += [rows(2 + half, t, "vs"[t % 2], v[:, t, half * 512:(half + 1) * 512]) for t in range(4)]
                for half in range(2):
                    jobs += [rows(4 + half, t, "s", sg[:, t, half * 512:(half + 1) * 512], func=ACT.Silu) for t in range(2)]
                jobs += [cols(6, dr * 16, 16, "vs"[dr], low[0:16, dr, :], TOK, n=32) for dr in range(2)]
                project(nc, G, "gla_in", jobs)
                jobs = [Job(None, 1, lambda c, t=t, dr=dr: low[:, dr, t * P:(t + 1) * P], lambda c, dr=dr: up[:, dr, :], P,
                            512, "vs"[t % 2], la[:, dr, t, :]) for dr in range(2) for t in range(4)]
                project(nc, G, "gla_gates", jobs)
            log_sigmoid(nc, G, la, [la[:, dr, t, :] for dr in range(2) for t in range(4)])
            with scope():
                mask = sbuf(nc, "chunk_masks", [P, 2, 6, P], F32)
                qz = sbuf(nc, "qz", [P, 2, H_C, 2, P], F32)
                at = sbuf(nc, "at", [P, 2, H_C, 1, P], F32)
                kd = sbuf(nc, "kd", [P, 2, 512], F32)
                etot = sbuf(nc, "etot", [P, 2, H_C, 2], F32)
                state = sbuf(nc, "state", [P, 4, H_C, DV_C], F32)
                with stage(nc, "masks_landed") as (block, masks_landed):
                    @block.sync
                    def _(sp):
                        sp.dma_start(mask[:, :, :, :], G.d["gla_masks"]).then_inc(masks_landed, 16)
                        sp.wait_ge(masks_landed, 16)
                for dr in range(2):
                    context_state(nc, G, dr, la[:, dr, 2:4, :], kn[:, 2:4, :], v[:, 2:4, :], mask[:, dr, 4:6, :], state)
                    linear_prepare(nc, G, dr, H_C, 1, la[:, dr, 0:2, :], qT, kT, kn, mask[:, dr, 0:4, :], qz, at, kd, etot)
                    linear_scan(nc, G, dr, H_C, 1, DV_C, v, qz, at, kd, etot, state, None, o, dr == 1)
        with scope():
            catT = sbuf(nc, "catT", [P, DC, SEQ], F32)
            grow = sbuf(nc, "gate_row", [P, 2, D], F32)

            def by_head(a):
                return lambda n: a[:, n, :].rearrange("p (h c) -> p h c", h=H_C)
            head_norm(nc, G, "gla", by_head(o), 2, H_C, DV_C, G.d["gla_norm_w"], by_head(sg), by_head(o), LN_EPS)
            transpose_in(nc, G, "cat", lambda t, c: o[:, t, c * P:(c + 1) * P], [0, 1], catT)
            gate_rows(nc, G, 2, [0], grow)
            with_rows(nc, G, 1, 0, [0, 1], out_project(G, ws.first["gla_out"], [0, 1], catT), grow)



def rms_in(nc, G, dst):
    x = G.x
    with scope():
        sq = sbuf(nc, "rms_sq", [P, 2, D], F32)
        ms = sbuf(nc, "rms_ms", [P, 2, 2], F32)
        with stage(nc, "rms_step", "ms_ready", "rms_ready") as (block, step_sem, ms_ready, rms_ready):
            @block.vector
            def _(dve):
                step = Steps(dve, step_sem)
                step(dve.tensor_tensor(sq[:, :, :], x[:, 0:2, :], x[:, 0:2, :], ALU.mult))
                step.wait()
                step(dve.tensor_reduce(ms[:, :, 0], sq[:, :, :], AX.X, ALU.add))
                step.wait()
                dve.tensor_scalar(ms[:, :, 0], ms[:, :, 0], 1.0 / D, RMS_EPS, ALU.mult, ALU.add).then_inc(ms_ready, 1)
                dve.wait_ge(rms_ready, 1)
                step(dve.reciprocal(ms[:, :, 0], ms[:, :, 1]))
                step.wait()
                for t in range(2):
                    step(dve.tensor_scalar(dst[:, t, :], x[:, t, :], ms[:, t, 0:1], None, ALU.mult))
                step.wait()

            @block.scalar
            def _(act):
                act.wait_ge(ms_ready, 1)
                act.activation(ms[:, :, 1], ms[:, :, 0], ACT.Sqrt).then_inc(rms_ready, 1)

            @block.sync
            def _(sp):
                G.ws.run_ahead(sp)


def normed_T(nc, G, key, hT):
    with scope():
        xn = sbuf(nc, "x_normed", [P, 2, D], F32)
        g = sbuf(nc, "norm_cols", [P, DC], F32)
        rms_in(nc, G, xn)
        with stage(nc, "g_landed") as (block, g_landed):
            @block.sync
            def _(sp):
                sp.dma_start(g[:, :], G.d[key]).then_inc(g_landed, 16)
                sp.wait_ge(g_landed, 16)
        transpose_in(nc, G, "hn", lambda t, c: xn[:, t, c * P:(c + 1) * P], [0, 1], hT, scale=lambda c, q: g[:, c:c + 1])


def turn(nc, G, moves):
    ps = G.ps
    groups = [moves[i:i + 4] for i in range(0, len(moves), 4)]
    with stage(nc, "turned", "out_v", "out_s") as (block, turned, out_v, out_s):
        outs = (out_v, out_s)

        @block.tensor
        def _(pe):
            for n, g in enumerate(groups):
                if n >= 8:
                    pe.wait_ge(outs[n % 2], (n - 8) // 2 + 1)
                for k, (src, _) in enumerate(g):
                    mm = pe.transpose(ps[:, n % 8, k * P:(k + 1) * P], src, G.ident[:, :])
                mm.then_inc(turned, 1)

        @block.vector
        def _(dve):
            for n in range(0, len(groups), 2):
                dve.wait_ge(turned, n + 1)
                for k, (_, dst) in enumerate(groups[n]):
                    last = dve.tensor_copy(dst, ps[:, n % 8, k * P:(k + 1) * P])
                last.then_inc(out_v, 1)

        @block.scalar
        def _(act):
            for n in range(1, len(groups), 2):
                act.wait_ge(turned, n + 1)
                for k, (_, dst) in enumerate(groups[n]):
                    last = act.activation(dst, ps[:, n % 8, k * P:(k + 1) * P], ACT.Identity)
                last.then_inc(out_s, 1)

        @block.sync
        def _(sp):
            G.ws.run_ahead(sp)


UNITS = 2 * DN_HEADS


def conv_silu(nc, G, layer, raw, cv):
    with scope():
        cw = sbuf(nc, "conv_w", [P, 12, DN_CONV], F32)
        with stage(nc, "cw_landed", "conv_step", "silu_out") as (block, cw_landed, conv_step, silu_out):
            @block.sync
            def _(sp):
                sp.dma_start(cw[:, :, :], G.d[f"dn_conv{layer}"]).then_inc(cw_landed, 16)
                G.ws.run_ahead(sp)

            @block.vector
            def _(dve):
                dve.wait_ge(cw_landed, 16)
                for j in range(DN_CONV):
                    for n in range(12):
                        o, i, w = cv[:, n, :], raw[:, n, j:j + SEQ], cw[:, n, j:j + 1]
                        if j == 0:
                            dve.tensor_scalar(o, i, w, None, ALU.mult).then_inc(conv_step, 1)
                        else:
                            dve.wait_ge(conv_step, 12 * (j - 1) + n + 1)
                            dve.scalar_tensor_tensor(o, i, w, o, ALU.mult, ALU.add).then_inc(conv_step, 1)

            @block.scalar
            def _(act):
                for n in range(12):
                    act.wait_ge(conv_step, 12 * (DN_CONV - 1) + n + 1)
                    act.activation(cv[:, n, :], cv[:, n, :], ACT.Silu).then_inc(silu_out, 1)


def delta_gates(nc, G, layer, nat, small, rhs, m, qkd, qd, kdec, qkT):
    ps = G.ps
    with scope():
        sq = sbuf(nc, "dn_sq", [P, 2, 8, P], F32)
        ms = sbuf(nc, "dn_ms", [P, 2, 8, 2], F32)
        row = sbuf(nc, "dn_rows", [P, 2, DN_HEADS], F32)
        dm = sbuf(nc, "dn_masks", [P, 4, P], F32)
        ba = sbuf(nc, "dn_beta", [P, 2, DN_HEADS], F32)
        z = sbuf(nc, "dn_z", [P, 2, DN_HEADS], F32)
        g = sbuf(nc, "dn_g", [P, 2, DN_HEADS], F32)
        w = sbuf(nc, "dn_w", [P, 2, DN_HEADS], F32)
        ea = sbuf(nc, "dn_ea", [P, DN_HEADS], F32)
        gb = sbuf(nc, "dn_gb", [P, UNITS, P], F32)
        gc = sbuf(nc, "dn_gc", [P, 5, UNITS], F32)
        with stage(nc, "rows_landed", "dn_step", "ms_ready", "rms_ready", "z_ready", "ln_ready", "act_step", "g_ready",
                   "gc_ready", "gc_out", "eg_ready", "nat_ready") as (
                block, rows_landed, step_sem, ms_ready, rms_ready, z_ready, ln_ready, act_step, g_ready, gc_ready,
                gc_out, eg_ready, nat_ready):
            @block.sync
            def _(sp):
                sp.dma_start(row[:, 0, :], G.d["dn_a_log"][layer].partition_broadcast(P)).then_inc(rows_landed, 16)
                sp.dma_start(row[:, 1, :], G.d["dn_dt_bias"][layer].partition_broadcast(P)).then_inc(rows_landed, 16)
                sp.dma_start(dm[:, :, :], G.d["dn_masks"]).then_inc(rows_landed, 16)
                G.ws.run_ahead(sp)

            @block.scalar
            def _(act):
                act.wait_ge(rows_landed, 48)
                act.activation(ea[:, :], row[:, 0, :], ACT.Exp).then_inc(act_step, 1)
                act.activation(ba[:, :, :], small[:, :, 64:68], ACT.Sigmoid).then_inc(act_step, 1)
                act.wait_ge(z_ready, 1)
                act.activation(w[:, :, :], w[:, :, :], ACT.Exp, scale=-1.0).then_inc(act_step, 1)
                act.wait_ge(act_step, 3)
                act.activation(w[:, :, :], w[:, :, :], ACT.Ln, bias=1.0).then_inc(ln_ready, 1)
                act.wait_ge(ms_ready, 1)
                act.activation(ms[:, :, :, 1], ms[:, :, :, 0], ACT.Sqrt).then_inc(rms_ready, 1)
                act.wait_ge(gc_out, 1)
                act.activation(gc[:, 1, :], gc[:, 0, :], ACT.Exp).then_inc(eg_ready, 1)
                act.activation(gc[:, 4, :], gc[:, 3, :], ACT.Exp).then_inc(eg_ready, 1)

            @block.tensor
            def _(pe):
                pe.wait_ge(rows_landed, 48)
                pe.wait_ge(g_ready, 1)
                gf = g[:, :, :].rearrange("p t h -> p (t h)")
                pe.matmul(ps[:, 0, 0:UNITS], dm[:, 0, :], gf, start=True, stop=True)
                pe.matmul(ps[:, 1, 0:UNITS], G.ones[:, :], gf, start=True, stop=True).then_inc(gc_ready, 1)

            @block.vector
            def _(dve):
                step = Steps(dve, step_sem)
                dve.wait_ge(rows_landed, 48)
                step(dve.tensor_tensor(z[:, :, :], small[:, :, 68:72], row[:, 1:2, :].broadcast_to([P, 2, DN_HEADS]), ALU.add))
                step.wait()
                dve.scalar_tensor_tensor(w[:, :, :], z[:, :, :], -1.0, z[:, :, :], ALU.mult, ALU.max).then_inc(z_ready, 1)
                step(dve.tensor_tensor(sq[:, :, :, :], nat[:, :, 0:8, :], nat[:, :, 0:8, :], ALU.mult))
                dve.wait_ge(ln_ready, 1)
                step(dve.scalar_tensor_tensor(z[:, :, :], z[:, :, :], 0.0, w[:, :, :], ALU.max, ALU.add))
                step.wait()
                dve.wait_ge(act_step, 1)
                dve.scalar_tensor_tensor(g[:, :, :], z[:, :, :], -1.0, ea[:, :].unsqueeze(1).broadcast_to([P, 2, DN_HEADS]),
                                         ALU.mult, ALU.mult).then_inc(g_ready, 1)
                step(dve.tensor_reduce(ms[:, :, :, 0], sq[:, :, :, :], AX.X, ALU.add))
                step.wait()
                dve.tensor_scalar(ms[:, :, :, 0], ms[:, :, :, 0], 1e-6, None, ALU.add).then_inc(ms_ready, 1)
                dve.wait_ge(gc_ready, 1)
                step(dve.tensor_copy(gc[:, 0, :], ps[:, 0, 0:UNITS]))
                step.wait()
                dve.tensor_tensor(gc[:, 3, :], ps[:, 1, 0:UNITS], gc[:, 0, :], ALU.subtract).then_inc(gc_out, 1)
                dve.wait_ge(rms_ready, 1)
                step(dve.reciprocal(ms[:, :, :, 0], ms[:, :, :, 1]))
                step.wait()
                step(dve.tensor_scalar(ms[:, :, 0:4, 0], ms[:, :, 0:4, 0], DN_DHEAD ** -0.5, None, ALU.mult))
                step.wait()
                for t in range(2):
                    dve.tensor_tensor(nat[:, t, 0:8, :], nat[:, t, 0:8, :], ms[:, t, :, 0:1].broadcast_to([P, 8, P]),
                                      ALU.mult).then_inc(nat_ready, 1)
                dve.wait_ge(nat_ready, 2)
                dve.wait_ge(eg_ready, 2)
                dve.wait_ge(act_step, 2)
                step(dve.tensor_tensor(gc[:, 2, :], gc[:, 1, :], ba[:, :, :].rearrange("p t h -> p (t h)"), ALU.mult))
                step.wait()

                def col(k, t):
                    return gc[:, k, t * 4:(t + 1) * 4].unsqueeze(2).broadcast_to([P, 4, P])
                for t in range(2):
                    units = slice(t * 4, (t + 1) * 4)
                    step(dve.tensor_tensor(rhs[:, units, 0:P], nat[:, t, 8:12, :],
                                           ba[:, t, :].unsqueeze(2).broadcast_to([P, 4, P]), ALU.mult))
                    step(dve.tensor_tensor(rhs[:, units, P:2 * P], nat[:, t, 4:8, :], col(2, t), ALU.mult))
                    step(dve.tensor_tensor(qd[:, units, :], nat[:, t, 0:4, :], col(1, t), ALU.mult))
                    step(dve.tensor_tensor(kdec[:, units, :], nat[:, t, 4:8, :], col(4, t), ALU.mult))
                    step(dve.tensor_copy(gb[:, units, :], g[:, t, :].unsqueeze(2).broadcast_to([P, 4, P])))
                step.wait()
        turn(nc, G, [(nat[:, t, 4 * w_ + h, :], qkT[:, w_, h, t * P:(t + 1) * P])
                     for w_ in range(2) for h in range(4) for t in range(2)])
        with scope():
            dd = sbuf(nc, "dn_dist", [P, 2, 2 * P], F32)
            with stage(nc, "gb_ready", "kk_ready", "dist_ready", "decay_ready", "m_out") as (
                    block, gb_ready, kk_ready, dist_ready, decay_ready, m_out):
                @block.tensor
                def _(pe):
                    for i in range(UNITS):
                        t, h = divmod(i, 4)
                        q, k = (qkT[:, a, h, t * P:(t + 1) * P] for a in range(2))
                        if i >= 2:
                            pe.wait_ge(dist_ready, 2 * (i - 1))
                        pe.matmul(ps[:, i % 2, 0:P], gb[:, i, :], dm[:, 0, :], start=True, stop=True).then_inc(gb_ready, 1)
                        if i >= 2:
                            pe.wait_ge(m_out, 2 * (i - 1))
                        pe.matmul(ps[:, 2 + i % 2, 0:P], k, k, start=True, stop=True)
                        pe.matmul(ps[:, 2 + i % 2, P:2 * P], k, q, start=True, stop=True).then_inc(kk_ready, 1)

                @block.vector
                def _(dve):
                    for i in range(UNITS + 1):
                        if i < UNITS:
                            b = i % 2
                            dve.wait_ge(gb_ready, i + 1)
                            if i >= 2:
                                dve.wait_ge(m_out, 2 * (i - 1))
                            dve.scalar_tensor_tensor(dd[:, b, 0:P], ps[:, b, 0:P], gc[:, 0, i:i + 1], dm[:, 1, :],
                                                     ALU.subtract, ALU.max).then_inc(dist_ready, 1)
                            dve.scalar_tensor_tensor(dd[:, b, P:2 * P], ps[:, b, 0:P], gc[:, 0, i:i + 1], dm[:, 2, :],
                                                     ALU.subtract, ALU.min).then_inc(dist_ready, 1)
                        if i >= 1:
                            n = i - 1
                            b = n % 2
                            t, h = divmod(n, 4)
                            dve.wait_ge(decay_ready, 2 * (n + 1))
                            dve.wait_ge(kk_ready, n + 1)
                            dve.scalar_tensor_tensor(m[:, n, :], ps[:, 2 + b, 0:P], ba[:, t, h:h + 1], dd[:, b, 0:P],
                                                     ALU.mult, ALU.mult).then_inc(m_out, 1)
                            dve.tensor_tensor(qkd[:, n, :], ps[:, 2 + b, P:2 * P], dd[:, b, P:2 * P], ALU.mult).then_inc(m_out, 1)

                @block.scalar
                def _(act):
                    for i in range(UNITS):
                        b = i % 2
                        act.wait_ge(dist_ready, 2 * (i + 1))
                        act.activation(dd[:, b, 0:P], dd[:, b, 0:P], ACT.Exp, scale=-1.0).then_inc(decay_ready, 1)
                        act.activation(dd[:, b, P:2 * P], dd[:, b, P:2 * P], ACT.Exp).then_inc(decay_ready, 1)

                @block.sync
                def _(sp):
                    G.ws.run_ahead(sp)


def delta_solve(nc, G, m, blocks, rhs):
    ps = G.ps
    with scope():
        a = sbuf(nc, "solve_a", [P, UNITS, 2 * P], F32)
        b = sbuf(nc, "solve_b", [P, UNITS, 2 * P], F32)
        c = sbuf(nc, "solve_c", [P, UNITS, 2 * P], F32)
        last = sbuf(nc, "solve_last", [P, UNITS, P], F32)
        with stage(nc, "pe_done", "dve_done") as (block, pe_done, dve_done):
            def halves(x):
                return x[:, :, 0:P], x[:, :, P:2 * P]
            (d1, d1T), (d2, d2T), (d4, d4T) = halves(a), halves(b), halves(c)
            x1 = rhs[:, :, 2 * P:3 * P]
            _, x1T = halves(a)
            x2, x2T = halves(b)

            @block.tensor
            def _(pe):
                done = [0]

                def step(*products):
                    done[0] += 1
                    pe.wait_ge(dve_done, done[0])
                    for u in range(UNITS):
                        for lhsT, r, col in products:
                            if lhsT is None:
                                mm = pe.transpose(ps[:, u, col:col + P], r[:, u, :], G.ident[:, :])
                            else:
                                w = r.shape[2]
                                mm = pe.matmul(ps[:, u, col:col + w], lhsT[:, u, :], r[:, u, :], start=True, stop=True)
                    mm.then_inc(pe_done, 1)
                both, cols = rhs[:, :, 0:3 * P], rhs[:, :, 0:2 * P]
                step((None, d1, 0))
                step((d1T, d1, 0), (d1, d1T, P))
                step((d2T, d2, 0), (d2, d2T, P))
                step((d4, d4T, 0))
                for t in (last, d4T, d2T, d1T):
                    step((t, both, 0))
                step((None, x1, 0))
                step((x1T, x1, 0), (x1, x1T, P))
                step((x2, x2T, 0))
                for t in (last, x2T, x1T):
                    step((t, cols, 0))

            @block.vector
            def _(dve):
                n = [0]

                def out(dst, w, op=None):
                    n[0] += 1
                    dve.wait_ge(pe_done, n[0])
                    src = ps[:, :, 0:w]
                    if op is None:
                        ins = dve.tensor_copy(dst, src)
                    else:
                        ins = dve.tensor_tensor(dst, dst, src, op)
                    ins.then_inc(dve_done, 1)

                dve.tensor_tensor(d1, m[:, :, :], blocks.unsqueeze(1).broadcast_to([P, UNITS, P]), ALU.mult).then_inc(pe_done, 1)
                dve.wait_ge(pe_done, 1)
                n[0] = 1
                dve.tensor_tensor(x1, m[:, :, :], d1, ALU.subtract).then_inc(dve_done, 1)
                out(d1T, P)
                out(b[:, :, :], 2 * P)
                out(c[:, :, :], 2 * P)
                out(last[:, :, :], P)
                for op in (ALU.add, ALU.add, ALU.add, ALU.subtract):
                    out(rhs[:, :, :], 3 * P, op)
                out(x1T, P)
                out(b[:, :, :], 2 * P)
                out(last[:, :, :], P)
                for op in (ALU.add, ALU.add, ALU.subtract):
                    out(rhs[:, :, 0:2 * P], 2 * P, op)

            @block.sync
            def _(sp):
                G.ws.run_ahead(sp)


def delta_out(nc, G, rhs, qkd, qdT, wkT, kdec, o):
    ps = G.ps
    H = DN_HEADS
    with scope():
        s = sbuf(nc, "dn_state", [P, H, P], F32)
        u1 = sbuf(nc, "dn_u", [P, H, P], F32)
        with stage(nc, "first_ready", "first_out", "wu_ready", "u_out", "second_ready", "o_out") as (
                block, first_ready, first_out, wu_ready, u_out, second_ready, o_out):
            @block.tensor
            def _(pe):
                for h in range(H):
                    pe.matmul(ps[:, 0, h * P:(h + 1) * P], kdec[:, h, :], rhs[:, h, 0:P], start=True, stop=True)
                for h in range(H):
                    mm = pe.matmul(ps[:, 1, h * P:(h + 1) * P], qkd[:, h, :], rhs[:, h, 0:P], start=True, stop=True)
                mm.then_inc(first_ready, 1)
                pe.wait_ge(first_out, 1)
                for h in range(H):
                    mm = pe.matmul(ps[:, 2, h * P:(h + 1) * P], wkT[:, h, :], s[:, h, :], start=True, stop=True)
                mm.then_inc(wu_ready, 1)
                pe.wait_ge(u_out, 1)
                for h in range(H):
                    pe.matmul(ps[:, 3 + h, 0:P], qdT[:, h, :], s[:, h, :], start=True, stop=False)
                    mm = pe.matmul(ps[:, 3 + h, 0:P], qkd[:, H + h, :], u1[:, h, :], start=False, stop=True)
                mm.then_inc(second_ready, 1)

            @block.vector
            def _(dve):
                dve.wait_ge(first_ready, 1)
                dve.tensor_copy(s[:, :, :], ps[:, 0, :].rearrange("p (h c) -> p h c", h=H)).then_inc(first_out, 1)
                dve.tensor_copy(o[:, 0, :], ps[:, 1, :])
                dve.wait_ge(wu_ready, 1)
                dve.tensor_tensor(u1[:, :, :], rhs[:, H:2 * H, 0:P], ps[:, 2, :].rearrange("p (h c) -> p h c", h=H),
                                  ALU.subtract).then_inc(u_out, 1)
                dve.wait_ge(second_ready, 1)
                dve.tensor_copy(o[:, 1, :].rearrange("p (h c) -> p h c", h=H), ps[:, 3:7, 0:P]).then_inc(o_out, 1)

            @block.sync
            def _(sp):
                G.ws.run_ahead(sp)


def index_select(nc, G, qi, ki, small, amask):
    ps = G.ps
    with scope():
        r = sbuf(nc, "relu", [P, 2, SEQ], F32)
        acc = sbuf(nc, "index_score", [P, 2, SEQ], F32)
        wi = sbuf(nc, "index_w", [P, 2, IDX_HEADS], F32)
        top = sbuf(nc, "index_top", [P, 2, 8], F32)
        work = [(t, h) for t in range(2) for h in range(IDX_HEADS)]
        with stage(nc, "qk_ready", "relu_ready", "idx_step") as (block, qk_ready, relu_ready, step_sem):
            @block.tensor
            def _(pe):
                for i, (t, h) in enumerate(work):
                    o = (h % 2) * 64
                    pe.matmul(ps[:, i, 0:SEQ], qi[o:o + 64, h // 2, t * P:(t + 1) * P], ki[o:o + 64, :], start=True,
                              stop=True).then_inc(qk_ready, 1)

            @block.scalar
            def _(act):
                for i in range(len(work)):
                    act.wait_ge(qk_ready, i + 1)
                    if i >= 2:
                        act.wait_ge(step_sem, i)
                    act.activation(r[:, i % 2, :], ps[:, i, 0:SEQ], ACT.Relu).then_inc(relu_ready, 1)

            @block.vector
            def _(dve):
                step = Steps(dve, step_sem)
                step(dve.tensor_scalar(wi[:, :, :], small[:, :, 72:76], IDX_HEADS ** -0.5 * 64 ** -0.5, None, ALU.mult))
                for i, (t, h) in enumerate(work):
                    dve.wait_ge(relu_ready, i + 1)
                    step.wait()
                    if h == 0:
                        step(dve.tensor_scalar(acc[:, t, :], r[:, i % 2, :], wi[:, t, h:h + 1], None, ALU.mult))
                    else:
                        step(dve.scalar_tensor_tensor(acc[:, t, :], r[:, i % 2, :], wi[:, t, h:h + 1], acc[:, t, :],
                                                      ALU.mult, ALU.add))
                step.wait()
                step(dve.tensor_tensor(acc[:, :, :], acc[:, :, :], amask[:, :, :], ALU.add))
                step.wait()
                for k in range(TOPK // 8):
                    for t in range(2):
                        step(dve.max(top[:, t, :], acc[:, t, :]))
                    step.wait()
                    for t in range(2):
                        step(dve.match_replace(acc[:, t, :], top[:, t, :], acc[:, t, :], TAKEN))
                    step.wait()
                step(dve.tensor_scalar(acc[:, :, :], acc[:, :, :], TAKEN / 2, None, ALU.is_le))
                step.wait()
                step(dve.tensor_scalar(acc[:, :, :], acc[:, :, :], 1.0, -NEG, ALU.subtract, ALU.mult))
                step.wait()
                step(dve.tensor_tensor(amask[:, :, :], amask[:, :, :], acc[:, :, :], ALU.add))
                step.wait()

            @block.sync
            def _(sp):
                G.ws.run_ahead(sp)


def forget_gates(nc, G, layer, f, k):
    with scope():
        lb = sbuf(nc, "hg_lb", [P, DEPTH, SEQ], F32)
        t = sbuf(nc, "hg_t", [P, 3, SEQ], F32)
        with stage(nc, "lb_landed", "hg_step", "max_ready", "lb_exp", "sig_ready", "fg_ready", "ln_ready") as (
                block, lb_landed, step_sem, max_ready, lb_exp, sig_ready, fg_ready, ln_ready):
            @block.sync
            def _(sp):
                for n in range(DEPTH):
                    sp.dma_start(lb[:, n, :], G.d["hg_lb"][n].partition_broadcast(P)).then_inc(lb_landed, 16)
                G.ws.run_ahead(sp)

            @block.scalar
            def _(act):
                act.activation(f[:, :, :], f[:, :, :], ACT.Sigmoid).then_inc(sig_ready, 1)
                act.wait_ge(max_ready, 1)
                act.activation(lb[:, :, :], lb[:, :, :], ACT.Exp).then_inc(lb_exp, 1)
                act.wait_ge(fg_ready, 1)
                act.activation(f[:, :, :], f[:, :, :], ACT.Ln).then_inc(ln_ready, 1)

            @block.vector
            def _(dve):
                step = Steps(dve, step_sem)
                dve.wait_ge(lb_landed, 16 * DEPTH)
                step(dve.tensor_tensor(t[:, 0, :], lb[:, 0, :], lb[:, 1, :], ALU.max))
                step.wait()
                dve.tensor_tensor(lb[:, :, :], lb[:, :, :], t[:, 0:1, :].broadcast_to([P, DEPTH, SEQ]),
                                  ALU.subtract).then_inc(max_ready, 1)
                dve.wait_ge(lb_exp, 1)
                step(dve.tensor_tensor(t[:, 0, :], lb[:, 0, :], lb[:, 1, :], ALU.add))
                step.wait()
                step(dve.reciprocal(t[:, 1, :], t[:, 0, :]))
                step.wait()
                if layer == 0:
                    step(dve.memset(t[:, 0, :], 0.0))
                else:
                    step(dve.tensor_tensor(t[:, 0, :], lb[:, 1, :], t[:, 1, :], ALU.mult))
                step.wait()
                step(dve.tensor_scalar(t[:, 1, :], t[:, 0, :], -1.0, 1.0, ALU.mult, ALU.add))
                dve.wait_ge(sig_ready, 1)
                step.wait()
                step(dve.tensor_tensor(f[:, :, :], f[:, :, :], t[:, 1:2, :].broadcast_to([P, 2, SEQ]), ALU.mult))
                step.wait()
                step(dve.tensor_tensor(f[:, :, :], f[:, :, :], t[:, 0:1, :].broadcast_to([P, 2, SEQ]), ALU.add))
                step.wait()
                dve.tensor_scalar(k[:, :, :], f[:, :, :], -1.0, 1.0, ALU.mult, ALU.add).then_inc(fg_ready, 1)


def load(nc, G, *pairs):
    with stage(nc, "loaded") as (block, loaded):
        @block.sync
        def _(sp):
            for dst, src in pairs:
                sp.dma_start(dst, src).then_inc(loaded, 16)
            sp.wait_ge(loaded, 16 * len(pairs))


def mixer_2(nc, G, layer):
    ws = G.ws
    u0 = ws.first[f"in2_{layer}"]
    with scope():
        cat = sbuf(nc, "cat2", [P, 2, D], F32)
        with scope():
            sz = sbuf(nc, "silu_z", [P, 2, 512], F32)
            qbT = sbuf(nc, "sa_qT", [P, 2, SEQ], F32)
            kbT = sbuf(nc, "sa_kT", [P, SEQ], F32)
            qiT = sbuf(nc, "idx_qT", [P, 2, SEQ], F32)
            kiT = sbuf(nc, "idx_kT", [P, SEQ], F32)
            cqT = sbuf(nc, "hg_qT", [P, 2, SEQ], F32)
            cf = sbuf(nc, "hg_f", [P, 2, SEQ], F32)
            ci = sbuf(nc, "hg_i", [P, 2, SEQ], F32)
            cg = sbuf(nc, "hg_g", [P, 2, SEQ], F32)
            small = sbuf(nc, "small", [P, 2, 76], F32)
            with scope():
                cv = sbuf(nc, "dn_cv", [P, 12, SEQ], F32)
                with scope():
                    raw = sbuf(nc, "dn_raw", [P, 12, SEQ + DN_CONV - 1], F32)
                    hT = sbuf(nc, "hT", [P, DC, SEQ], F32)
                    with stage(nc, "raw_set") as (block, raw_set):
                        @block.gpsimd
                        def _(pool):
                            pool.memset(raw[:, :, 0:DN_CONV - 1], 0.0).then_inc(raw_set, 1)
                            pool.wait_ge(raw_set, 1)
                    normed_T(nc, G, f"g_mix_pre{layer}", hT)

                    def cols(k, off, eng, dst, func=None):
                        w = ws.slot(u0 + k).rearrange("p (c n) -> p c n", c=DC)
                        return Job(u0 + k, DC, lambda c: w[:, c, off:off + P], lambda c: hT[:, c, :], P, SEQ, eng, dst,
                                   func=func)

                    def rows(k, t, off, m, eng, dst, func=None, n=512):
                        w = ws.slot(u0 + k)[:, 0:DC * n].rearrange("p (c n) -> p c n", c=DC)
                        return Job(u0 + k, DC, lambda c: hT[:, c, t * P:(t + 1) * P], lambda c: w[:, c, off:off + m], P, m,
                                   eng, dst, func=func)
                    jobs = []
                    for n in range(12):
                        jobs.append(cols(n // 4, (n % 4) * P, "vs"[n % 2], raw[:, n, DN_CONV - 1:DN_CONV - 1 + SEQ]))
                    jobs += [rows(3, t, 0, 512, "s", sz[:, t, :], func=ACT.Silu) for t in range(2)]
                    jobs += [cols(4, n * P, "vs"[n % 2], (qbT, qiT)[n // 2][:, n % 2, :]) for n in range(4)]
                    jobs += [cols(5, 0, "v", kbT[:, :]), cols(5, P, "v", kiT[:, :])]
                    jobs += [cols(5, (2 + n) * P, "s", cqT[:, n, :], func=ACT.Silu) for n in range(2)]
                    for t in range(2):
                        jobs += [rows(6, t, 0, SEQ, "v", cf[:, t, :]), rows(6, t, SEQ, SEQ, "s", ci[:, t, :])]
                    for t in range(2):
                        jobs += [rows(7, t, 0, SEQ, "s", cg[:, t, :], func=ACT.Silu, n=332),
                                 rows(7, t, SEQ, 76, "v", small[:, t, :], n=332)]
                    project(nc, G, "in2", jobs)
                    conv_silu(nc, G, layer, raw, cv)
                with scope():
                    rhs = sbuf(nc, "dn_rhs", [P, UNITS, 3 * P], F32)
                    m = sbuf(nc, "dn_m", [P, UNITS, P], F32)
                    qkd = sbuf(nc, "dn_qkd", [P, UNITS, P], F32)
                    qd = sbuf(nc, "dn_qd", [P, UNITS, P], F32)
                    kdec = sbuf(nc, "dn_kdec", [P, UNITS, P], F32)
                    with scope():
                        nat = sbuf(nc, "dn_nat", [P, 2, 12, P], F32)
                        qkT = sbuf(nc, "dn_qkT", [P, 2, DN_HEADS, SEQ], F32)
                        turn(nc, G, [(cv[:, n, t * P:(t + 1) * P], nat[:, t, n, :]) for t in range(2) for n in range(12)])
                        delta_gates(nc, G, layer, nat, small, rhs, m, qkd, qd, kdec, qkT)
                    with scope():
                        blocks = sbuf(nc, "dn_blocks", [P, P], F32)
                        load(nc, G, (blocks[:, :], G.d["dn_masks"][:, 3, :]))
                        delta_solve(nc, G, m, blocks[:, :], rhs)
                    with scope():
                        qdT = sbuf(nc, "dn_qdT", [P, DN_HEADS, P], F32)
                        wkT = sbuf(nc, "dn_wkT", [P, DN_HEADS, P], F32)
                        oa = sbuf(nc, "dn_o", [P, 2, 512], F32)
                        turn(nc, G, [(qd[:, 4 + h, :], qdT[:, h, :]) for h in range(4)]
                             + [(rhs[:, 4 + h, P:2 * P], wkT[:, h, :]) for h in range(4)])
                        delta_out(nc, G, rhs, qkd, qdT, wkT, kdec, oa)

                        def by_head(a, lo=0, hi=512, h=4):
                            return lambda n: a[:, n, lo:hi].rearrange("p (h c) -> p h c", h=h)
                        head_norm(nc, G, "dn", by_head(oa), 2, DN_HEADS, DN_DHEAD, G.d["dn_norm"][layer], by_head(sz),
                                  by_head(cat), RMS_EPS)
            with scope():
                amask = sbuf(nc, "key_mask", [P, 2, SEQ], F32)
                load(nc, G, (amask[:, :, :], G.d["admissible"]))
                index_select(nc, G, qiT, kiT, small, amask)
                items = []
                for t in range(2):
                    for h in range(SA_HEADS):
                        o = (h % 2) * 64
                        items.append(Item(qbT[o:o + 64, h // 2, t * P:(t + 1) * P], kbT[o:o + 64, :], SEQ, amask[:, t, :],
                                          None, [small[:, k, 0:64] for k in range(2)],
                                          cat[:, t, 512 + h * 64:512 + (h + 1) * 64]))
                attend(nc, G, items)
            with scope():
                ck = sbuf(nc, "hg_k", [P, 2, SEQ], F32)
                ckT = sbuf(nc, "hg_kT", [P, 2, SEQ], F32)
                mask = sbuf(nc, "hg_masks", [P, 5, P], F32)
                qz = sbuf(nc, "hg_qz", [P, 2, 2, 2, P], F32)
                at = sbuf(nc, "hg_at", [P, 2, 2, 2, P], F32)
                kd = sbuf(nc, "hg_kd", [P, 2, SEQ], F32)
                etot = sbuf(nc, "hg_etot", [P, 2, 2, 2], F32)
                state = sbuf(nc, "hg_state", [P, 4, 2, P], F32)
                oc = sbuf(nc, "hg_o", [P, 2, SEQ], F32)
                forget_gates(nc, G, layer, cf, ck)
                turn(nc, G, [(ck[:, t, n * P:(n + 1) * P], ckT[:, n, t * P:(t + 1) * P]) for n in range(2) for t in range(2)])
                with stage(nc, "state_set", "masks_landed") as (block, state_set, masks_landed):
                    @block.gpsimd
                    def _(pool):
                        pool.memset(state[:, 0, :, :], 0.0).then_inc(state_set, 1)
                        pool.wait_ge(state_set, 1)

                    @block.sync
                    def _(sp):
                        sp.dma_start(mask[:, :, :], G.d["hg_masks"]).then_inc(masks_landed, 16)
                        sp.wait_ge(masks_landed, 16)
                linear_prepare(nc, G, 0, 2, 2, cf, cqT, ckT, ck, mask[:, 0:4, :], qz, at, kd, etot)
                linear_scan(nc, G, 0, 2, 2, P, ci, qz, at, kd, etot, state, mask[:, 4, :], oc, False)
                head_norm(nc, G, "hg", lambda n: oc[:, n, :].rearrange("p (h c) -> p h c", h=4), 2, HG_HEADS, HG_DHEAD,
                          G.d["hg_norm"][layer], lambda n: cg[:, n, :].rearrange("p (h c) -> p h c", h=4),
                          lambda n: cat[:, n, 768:1024].rearrange("p (h c) -> p h c", h=4), RMS_EPS)
        with scope():
            catT = sbuf(nc, "catT", [P, DC, SEQ], F32)
            transpose_in(nc, G, "cat", lambda t, c: cat[:, t, c * P:(c + 1) * P], [0, 1], catT)
            post_norm(nc, G, f"g_mix_post{layer}", out_project(G, ws.first[f"out2_{layer}"], [0, 1], catT))


def post_norm(nc, G, key, pre):
    with scope():
        row = sbuf(nc, "post_row", [P, D], F32)
        load(nc, G, (row[:, :], G.d[key].partition_broadcast(P)))
        residual_norm(nc, G, "post", [0, 1], lambda n: 2 * n, lambda k: row[:, :], None, "rms", pre)


def ffn_2(nc, G, layer):
    ws, ps = G.ws, G.ps
    u0, d0 = ws.first[f"up{layer}"], ws.first[f"down{layer}"]
    with scope():
        aT = sbuf(nc, "ffn_act", [P, NF, SEQ], F32)
        with scope():
            hT = sbuf(nc, "hT", [P, DC, SEQ], F32)
            cw = sbuf(nc, "ffn_conv", [P, 2 * NF, FFN_CONV], F32)
            acc = sbuf(nc, "ffn_acc", [P, 8, SEQ], F32)
            normed_T(nc, G, f"g_ffn_pre{layer}", hT)
            load(nc, G, (cw[:, :, :], G.d[f"ffn_conv{layer}"]))
            NU = NF // 2
            with stage(nc, "up_ready", "tap2", "tap1", "tap0", "gelu_ready", "act_out") as (
                    block, up_ready, tap2, tap1, tap0, gelu_ready, act_out):
                @block.tensor
                def _(pe):
                    for u in range(NU):
                        ws.wait_landed(pe, u0 + u)
                        w = ws.slot(u0 + u).rearrange("p (c n) -> p c n", c=DC)
                        for q in range(4):
                            k = 4 * u + q
                            if k >= 8:
                                pe.wait_ge(tap0, k - 7)
                            for c in range(DC):
                                mm = pe.matmul(ps[:, k % 8, 0:SEQ], w[:, c, q * P:(q + 1) * P], hT[:, c, :],
                                               start=(c == 0), stop=(c == DC - 1))
                            mm.then_inc(up_ready, 1)
                        ws.done(u0 + u, up_ready, 4 * (u + 1))

                @block.scalar
                def _(act):
                    def gelu(u):
                        for q in range(2):
                            k = 4 * u + q
                            act.wait_ge(tap0, k + 1)
                            act.activation(acc[:, k % 8, :], acc[:, k % 8, :], ACT.Gelu_apprx_tanh).then_inc(gelu_ready, 1)
                    for u in range(NU):
                        for q in range(4):
                            k = 4 * u + q
                            act.wait_ge(up_ready, k + 1)
                            if u >= 2:
                                act.wait_ge(act_out, 2 * (u - 1))
                            act.activation(acc[:, k % 8, :], ps[:, k % 8, 0:SEQ], ACT.Identity,
                                           scale=cw[:, k, 2:3]).then_inc(tap2, 1)
                        if u >= 1:
                            gelu(u - 1)
                    gelu(NU - 1)

                @block.vector
                def _(dve):
                    def product(u):
                        for q in range(2):
                            dve.wait_ge(gelu_ready, 2 * u + q + 1)
                            dve.wait_ge(tap0, 4 * u + q + 3)
                            dve.tensor_tensor(aT[:, 2 * u + q, :], acc[:, (4 * u + q) % 8, :], acc[:, (4 * u + q + 2) % 8, :],
                                              ALU.mult).then_inc(act_out, 1)
                    for u in range(NU):
                        for tap, before, sem in ((1, tap2, tap1), (0, tap1, tap0)):
                            for q in range(4):
                                k = 4 * u + q
                                s = 2 - tap
                                dve.wait_ge(before, k + 1)
                                dve.scalar_tensor_tensor(acc[:, k % 8, s:SEQ], ps[:, k % 8, 0:SEQ - s],
                                                         cw[:, k, tap:tap + 1], acc[:, k % 8, s:SEQ], ALU.mult,
                                                         ALU.add).then_inc(sem, 1)
                        if u >= 1:
                            product(u - 1)
                    product(NU - 1)

                @block.sync
                def _(sp):
                    ws.run_ahead(sp)
            ws.stage_over()

        def down(pe, y_ready, part_done):
            for h in range(2):
                for q in range(3):
                    n = d0 + 3 * h + q
                    ws.wait_landed(pe, n)
                    chunks = range(8 * q, min(8 * q + 8, NF))
                    w = ws.slot(n)[:, 0:len(chunks) * 512].rearrange("p (c n) -> p c n", n=512)
                    for t in range(2):
                        for c in chunks:
                            mm = pe.matmul(ps[:, 2 * t + h, :], aT[:, c, t * P:(t + 1) * P], w[:, c - 8 * q, :],
                                           start=(c == 0), stop=(c == NF - 1))
                        if (h, q) == (1, 2):
                            mm.then_inc(y_ready, 1)
                            ws.done(n, y_ready, t + 1)
                    if (h, q) != (1, 2):
                        mm.then_inc(part_done, 1)
                        ws.done(n, part_done, 3 * h + q + 1)
        post_norm(nc, G, f"g_ffn_post{layer}", down)



class Shared:
    pass


def make_shared(nc, dram):
    G = Shared()
    G.d = dram
    G.ident = sbuf(nc, "ident", [P, P], F32)
    G.ones = sbuf(nc, "ones", [P, P], F32)
    G.iota = sbuf(nc, "iota", [P, P], F32)
    G.x = sbuf(nc, "x", [P, 4, D], F32)
    G.mod = sbuf(nc, "mod", [P, 6 * DC, 2], F32)
    for b in range(2):
        Sems.sets.append([nc.alloc_semaphore(f"stage_{b}_{n}") for n in range(STAGE_SEMS)])
    G.ps = nc.alloc_psum_tensor("ps", [P, 8, 512], F32)
    G.ws = Weights(nc)
    return G


def load_x(nc, G):
    with stage(nc, "x_landed", "ones_set") as (block, x_landed, ones_set):
        @block.sync
        def _(sp):
            sp.dma_start(G.ident[:, :], G.d["ident"]).then_inc(x_landed, 16)
            sp.dma_start(G.iota[:, :], G.d["iota"]).then_inc(x_landed, 16)
            sp.dma_start(G.x[:, 0:2, :], G.d["x"]).then_inc(x_landed, 16)
            sp.dma_start(G.x[:, 2:4, :], G.d["ctx"]).then_inc(x_landed, 16)
            G.ws.run_ahead(sp)
            sp.wait_ge(x_landed, 64)

        @block.vector
        def _(dve):
            dve.memset(G.ones[:, :], 1.0).then_inc(ones_set, 1)
            dve.wait_ge(ones_set, 1)


def plan_weights(G):
    ws, d = G.ws, G.d

    def blocks(name, widths):
        a, out, at = d[name], [], 0
        for w in widths:
            out.append(a[:, at:at + w])
            at += w
        return out

    for layer in range(DEPTH):
        ws.plan(f"mod{layer}", blocks(f"w_mod{layer}", [UNIT] * 12))
        if layer == 0:
            ws.plan("ab_in", blocks("ab_w_in", [UNIT] * 5 + [DC * 400]))
            ws.plan("ab_out", blocks("ab_w_out", [UNIT] * 2))
        else:
            ws.plan("gla_in", blocks("gla_w_in", [UNIT] * 6 + [DC * 32]))
            ws.plan("gla_out", blocks("gla_w_out", [UNIT] * 2))
        for col in range(2 if layer == 0 else 1):
            ws.plan(f"peer{layer}{col}", blocks(f"peer_wq{layer}", [UNIT] * 4))
            ws.src += [d[f"peer_uv{layer}"][n] for n in range(N_KEYS // 2)]
    for layer in range(DEPTH):
        ws.plan(f"in2_{layer}", blocks(f"w_in_2{layer}", [UNIT] * 7 + [DC * 332]))
        ws.plan(f"out2_{layer}", blocks(f"w_out_2{layer}", [UNIT] * 2))
        ws.plan(f"up{layer}", blocks(f"ffn_w_up_2{layer}", [UNIT] * 11))
        ws.plan(f"down{layer}", blocks(f"ffn_w_down_2{layer}", [UNIT, UNIT, 6 * 512] * 2))


def program(nc, dram, out):
    with scope():
        G = make_shared(nc, dram)
        plan_weights(G)
        load_x(nc, G)
        modulation(nc, G, 0)
        mixer_ab(nc, G)
        peer(nc, G, 0, 0, [0, 1])
        peer(nc, G, 0, 1, [2, 3])
        modulation(nc, G, 1)
        mixer_c(nc, G)
        peer(nc, G, 1, 0, [0, 1])
        for layer in range(DEPTH):
            mixer_2(nc, G, layer)
            ffn_2(nc, G, layer)
        with stage(nc, "out_landed") as (block, out_landed):
            @block.sync
            def _(sp):
                sp.dma_start(out.rearrange("a (t p) d -> p (a t) d", p=P), G.x[:, 0:2, :]).then_inc(out_landed, 16)
                sp.wait_ge(out_landed, 16)



def tri(keep):
    s, t = np.arange(P)[:, None], np.arange(P)[None, :]
    return np.where(keep(s, t), 0.0, NEG).astype(np.float32)


def constants():
    f = np.float32
    c = {"ident": np.eye(P, dtype=f), "iota": np.tile(np.arange(P, dtype=f), (P, 1))}
    m = np.full((P, 2, QK_WIDTH), NEG, f)
    s = np.arange(P)[:, None]
    for tile, q0, nq, at in QK_PARTS:
        pos_s = (tile % 2) * P + s
        q = np.arange(q0, q0 + nq)[None, :]
        for dr in range(2):
            if tile < 2:
                ok = pos_s <= q if dr == 0 else pos_s >= q
            else:
                own = (q - SEQ >= pos_s) if dr == 0 else (q - SEQ <= pos_s)
                ok = np.where(q < SEQ, True, own)
            m[:, dr, at:at + nq] = np.where(ok, 0.0, NEG)
    c["scan_mask"] = m
    c["row_select"] = np.ascontiguousarray(np.repeat(np.eye(H_M, dtype=f)[:, :, None], P, 2))
    wm = np.zeros((P, 2, TOK), f)
    for t in range(2):
        i, j = t * P + s, np.arange(SEQ)[None, :]
        wm[:, t, 0:SEQ] = np.where(np.abs(i - j) <= WINDOW, 0.0, NEG)
    c["window_mask"] = wm
    rows = SEQ // 64
    row = np.repeat(np.arange(rows), 64).astype(f)
    col = np.tile(np.arange(64), rows).astype(f)
    n_freq = DH_A // 4
    inv = (f(10000.0) ** (-np.arange(n_freq, dtype=f) / f(n_freq))).astype(f)
    ang = np.concatenate([row[:, None] * inv, col[:, None] * inv], -1)
    at = (np.arange(P) % DH_A) // 2
    c["rope_cos"] = np.ascontiguousarray(np.cos(ang).astype(f).T[at])
    c["rope_sin"] = np.ascontiguousarray(np.sin(ang).astype(f).T[at])
    sw = np.zeros((P, P), f)
    for i in range(0, P, 2):
        sw[i + 1, i], sw[i, i + 1] = -1.0, 1.0
    c["rope_swap"] = sw
    c["gla_masks"] = np.stack([chunk_masks(dr, 1 / GATE_TAU) for dr in range(2)], 1)
    hg = chunk_masks(0, 1.0)[:, 0:5]
    hg[:, 4] = s // HG_DHEAD == s.T // HG_DHEAD
    c["hg_masks"] = hg
    t = s.T
    c["dn_masks"] = np.stack([s <= t, np.where(t < s, 0.0, -NEG), np.where(s <= t, 0.0, NEG), s // 16 == t // 16],
                             1).astype(f)
    q = np.arange(SEQ)
    ok = q[None, :] // CHUNK <= q[:, None] // CHUNK
    c["admissible"] = np.where(ok, 0.0, NEG).astype(f).reshape(2, P, SEQ).transpose(1, 0, 2)
    return c


def chunk_masks(d, unit):
    s, t = np.arange(P)[:, None], np.arange(P)[None, :]
    if d == 1:
        s, t = P - 1 - s, P - 1 - t
    same = s // CHUNK == t // CHUNK
    mid = t // CHUNK * CHUNK + CHUNK // 2 - 1
    cum = same & (s <= t)
    rel = (same & (s > mid) & (s <= t)) * 1.0 - (same & (s <= mid) & (s > t)) * 1.0
    return np.stack([cum * unit, rel * unit, (same & (s > t)) * unit, cum * 1.0, (s > t) * unit,
                     np.full((P, P), unit)], 1).astype(np.float32)


def pack_columns(w, blocks):
    k = w.shape[0] // P
    w3 = w.reshape(k, P, w.shape[1])
    return np.ascontiguousarray(np.concatenate([w3[:, :, b].transpose(1, 0, 2).reshape(P, -1) for b in blocks], 1))


def spans(n, width=512, start=0):
    return [np.arange(a, min(a + width, start + n)) for a in range(start, start + n, width)]


def layouts(i):
    g = {k: np.asarray(v) for k, v in i.items()}
    a = {"x": g["x"][0].reshape(2, P, D).transpose(1, 0, 2), "ctx": g["ctx"][0].reshape(2, P, D).transpose(1, 0, 2),
         "c": g["c"].reshape(DC, P).T, "c_ctx": g["c_ctx"].reshape(DC, P).T,
         "ln_w": g["ln_w"].reshape(2 * DEPTH, D), "ln_b": g["ln_b"].reshape(2 * DEPTH, D)}
    for n in range(DEPTH):
        a[f"w_mod{n}"] = pack_columns(g["w_mod"][n], spans(6 * D))
        a[f"b_mod{n}"] = g["b_mod"][n].reshape(6 * DC, P).T
        a[f"peer_wq{n}"] = pack_columns(g["peer_wq"][n], spans(2048))
        u = g["peer_u"][n].reshape(N_KEYS, N_KEYS // 2, 2, DC, P).transpose(1, 4, 2, 3, 0)
        v = g["peer_v"][n].reshape(N_KEYS, N_KEYS // 2, 2, D).transpose(1, 0, 2, 3)
        a[f"peer_uv{n}"] = np.concatenate([u.reshape(N_KEYS // 2, P, 2 * D), v.reshape(N_KEYS // 2, P, 2 * D)], 2)
    a["peer_keysT"] = g["peer_keys"].reshape(DEPTH, 2 * PEER_HEADS, N_KEYS, P).transpose(0, 3, 1, 2)
    w = g["ab_w_in"][0]
    base = 2064
    ka = [np.arange(2576 + h * DH_A, 2576 + (h + 1) * DH_A) for h in (0, 0, 1, 1)]
    gates = [2048 + dr * 8 + kind * 4 + np.arange(4) for kind in range(2) for dr in range(2)]
    last = np.concatenate(ka + [np.arange(2704, 2832)] + gates)
    a["ab_w_in"] = pack_columns(w, spans(2048) + [np.arange(base, base + 512), last])
    a["ab_gate_b"] = g["ab_gate_b"][0].transpose(1, 0, 2).reshape(4, H_M).T
    a["ab_norm_w"] = g["ab_norm_w"][0]
    a["ab_sink"] = g["ab_sink"][0]
    a["ab_w_out"] = pack_columns(g["ab_w_out"][0], spans(D))
    layouts_rest(g, a)
    return a



def layouts_rest(g, a):
    a["gla_w_in"] = pack_columns(g["gla_w_in"][0], spans(3072) + [np.arange(3072, 3104)])
    up = np.concatenate([g["gla_gate_up"][0], g["gla_gate_b"][0][:, None, :]], 1)
    a["gla_gate"] = up.transpose(1, 0, 2)
    a["gla_norm_w"] = g["gla_norm_w"][0]
    a["gla_w_out"] = pack_columns(g["gla_w_out"][0], spans(D))
    r = np.arange
    k, ki = r(2312, 2376), r(2696, 2760)
    cols = [r(0, 512), r(512, 1024), r(1024, 1536), r(1536, 2048),
            np.concatenate([r(2056, 2312), r(2440, 2696)]), np.concatenate([k, k, ki, ki, r(2764, 3020)]),
            r(3020, 3532), np.concatenate([r(3532, 3788), r(2376, 2440), r(2048, 2056), r(2760, 2764)])]
    for n in range(DEPTH):
        a[f"w_in_2{n}"] = pack_columns(g["w_in_2"][n], cols)
        a[f"dn_conv{n}"] = g["dn_conv_2"][n].reshape(DN_CONV, 12, P).transpose(2, 1, 0)
        a[f"w_out_2{n}"] = pack_columns(g["w_out_2"][n], spans(D))
        for name in ("g_mix_pre", "g_ffn_pre"):
            a[f"{name}{n}"] = g[f"{name}_2"][n].reshape(DC, P).T
        for name in ("g_mix_post", "g_ffn_post"):
            a[f"{name}{n}"] = g[f"{name}_2"][n]
        tiles = [r(b + (2 * u) * P, b + (2 * u + 2) * P) for u in range(NF // 2) for b in (0, D_FF)]
        units = [np.concatenate(tiles[2 * u:2 * u + 2]) for u in range(NF // 2)]
        a[f"ffn_w_up_2{n}"] = pack_columns(g["ffn_w_up_2"][n], units)
        fc = g["ffn_conv_2"][n][:, np.concatenate(units)]
        a[f"ffn_conv{n}"] = fc.reshape(FFN_CONV, 2 * NF, P).transpose(2, 1, 0)
        w3 = g["ffn_w_down_2"][n].reshape(NF, P, 2, 512)
        a[f"ffn_w_down_2{n}"] = np.concatenate(
            [w3[q:min(q + 8, NF), :, h].transpose(1, 0, 2).reshape(P, -1) for h in range(2) for q in (0, 8, 16)], 1)
    a["dn_a_log"], a["dn_dt_bias"] = g["dn_a_log_2"], g["dn_dt_bias_2"]
    a["dn_norm"] = np.tile(g["dn_norm_2"], (1, DN_HEADS))
    a["hg_lb"] = g["hg_lb_2"]
    a["hg_norm"] = np.tile(g["hg_norm_2"], (1, HG_HEADS))

_OUTS = [((1, SEQ, D), "float32")]


def kernel(**inputs):
    import concourse.bacc as _bacc
    from concourse.bass_utils import run_bass_kernel_spmd as _run

    nc = _bacc.Bacc("TRN2", target_bir_lowering=False, num_devices=1)
    arrays, dram = {}, {}
    for name, a in {**layouts(inputs), **constants()}.items():
        a = np.ascontiguousarray(a)
        arrays[f"in_{name}"] = a
        dram[name] = nc.dram_tensor(f"in_{name}", a.shape, mybir.dt.from_np(a.dtype), kind="ExternalInput").ap()
    out = nc.dram_tensor("out_0", _OUTS[0][0], F32, kind="ExternalOutput").ap()
    program(nc, dram, out)
    r = _run(nc, [arrays], core_ids=[0])
    return r.results[0]["out_0"]
```

```python
from collections import namedtuple
from contextlib import ExitStack, contextmanager
from itertools import count

import concourse.bass as bass
import numpy as np
from concourse import mybir

F32 = mybir.dt.float32
F32R = mybir.dt.float32r
U32 = mybir.dt.uint32
ALU = mybir.AluOpType
ACT = mybir.ActivationFunctionType
AX = mybir.AxisListType
ds = bass.ds

P = 128
D = 1024
DC = D // P
SEQ = 256
CTX = 256
TOK = SEQ + CTX
DEPTH = 2
CHUNK = 64
H_M, DH_M = 4, 128
H_A, H_KV, DH_A = 8, 2, 64
WINDOW = 128
H_C, DK_C, DV_C = 4, 128, 256
GATE_RANK, GATE_TAU = 16, 16.0
N_KEYS = 128
PEER_HEADS, PEER_TOPK = 8, 16
ALPHA = (2 * DEPTH) ** 0.25
LN_EPS = 1e-5
RMS_EPS = 1e-6
DN_HEADS, DN_DHEAD, DN_CONV = 4, 128, 4
SA_HEADS, SA_DHEAD = 4, 64
HG_HEADS, HG_DHEAD = 4, 64
IDX_HEADS = 4
TOPK = 64
D_FF, FFN_CONV = 2816, 3
NF = D_FF // P
NEG = -1e30
TAKEN = -3e38

PAD = 32
SLOTS = 3
UNIT = 4096
QUARTERS = 4
PASSES = ((0, 0), (0, 1), (1, 0))


NUMBER = count()
SCOPES = []
STAGE_SEMS = 14


@contextmanager
def scope():
    with ExitStack() as held:
        SCOPES.append(held)
        yield
        SCOPES.pop()


def sbuf(nc, name, shape, dtype):
    return SCOPES[-1].enter_context(nc.sbuf_tensor(f"{name}_{next(NUMBER)}", shape, dtype))


class Sems:
    sets, turn = [], 0


@contextmanager
def stage(nc, *names, beside=None, loads=()):
    own, other = Sems.sets[Sems.turn % 2], Sems.sets[(Sems.turn + 1) % 2]
    Sems.turn += 1
    with nc.Block() as block:
        @block.gpsimd
        def _(pool):
            pool.sem_clear(range(other[0].num, other[-1].num + 1))
        if beside is not None:
            beside(block, own[len(names):])
        loads_landed = own[-1]
        assert len(names) + (3 if beside is not None else 0) < len(own)

        @block.sync
        def _(sp):
            for dst, src in loads:
                sp.dma_start(dst, src).then_inc(loads_landed, 16)
        yield (block, *own[:len(names)])

        @block.sync
        def _(sp):
            if loads:
                sp.wait_ge(loads_landed, 16 * len(loads))
    if beside is not None:
        beside.ws.stage_over()


class Steps:

    def __init__(self, eng, sem):
        self.eng, self.sem, self.n = eng, sem, 0

    def __call__(self, ins):
        ins.then_inc(self.sem, 1)
        self.n += 1
        return self.n

    def wait(self):
        self.eng.wait_ge(self.sem, self.n)


class Weights:

    def __init__(self, nc):
        self.ring = sbuf(nc, "weight_ring", [P, SLOTS, UNIT], F32)
        at = nc.sbuf_base - SLOTS * UNIT * 4
        self.ring_low = nc.alloc_sbuf_tensor_at("weight_ring_low", [P, SLOTS, UNIT], F32R, offset=at)
        self.landed = [nc.alloc_semaphore(f"slot{s}_landed") for s in range(SLOTS)]
        self.src, self.first = [], {}
        self.issued = 0
        self.used = 0
        self.release = {}

    def plan(self, name, srcs):
        self.first[name] = len(self.src)
        self.src += srcs

    def slot(self, n):
        return self.ring[:, n % SLOTS, :]

    def wait_landed(self, pe, n):
        pe.wait_ge(self.landed[n % SLOTS], 16 * (n // SLOTS + 1))

    def done(self, n, sem, value):
        self.release[n] = (sem, value)
        self.used = max(self.used, n + 1)

    def load(self, sp, n):
        src = self.src[n]
        sp.dma_start(self.slot(n)[0:src.shape[0], 0:src.shape[1]], src).then_inc(self.landed[n % SLOTS], 16)

    def run_ahead(self, sp):
        while self.issued < min(self.used + SLOTS, len(self.src)):
            n = self.issued
            if n - SLOTS in self.release:
                sp.wait_ge(*self.release[n - SLOTS])
            self.load(sp, n)
            self.issued += 1

    def stage_over(self):
        self.release = {}

    def make_high(self, nc):
        self.highs = sbuf(nc, "units_high", [P, 2, UNIT], F32R)

    def parts(self, n):
        return self.highs[:, n % 2, :], self.ring_low[:, n % SLOTS, :]

    def split_high(self, act, n, i, free, high_done):
        self.wait_landed(act, n)
        if free:
            act.wait_ge(*free)
        w = self.src[n].shape[1] // QUARTERS
        for q in range(QUARTERS):
            act.activation(self.parts(n)[0][:, q * w:(q + 1) * w], self.slot(n)[:, q * w:(q + 1) * w],
                           ACT.Identity).then_inc(high_done, 1)

    def split_low(self, dve, n, i, high_done, low_done):
        w = self.src[n].shape[1] // QUARTERS
        for q in range(QUARTERS):
            s = slice(q * w, (q + 1) * w)
            dve.wait_ge(high_done, i * QUARTERS + q + 1)
            dve.tensor_tensor(self.parts(n)[1][:, s], self.slot(n)[:, s], self.parts(n)[0][:, s].bitcast(F32),
                              ALU.subtract).then_inc(low_done, 1)



Job = namedtuple("Job", "unit nk lhsT rhs m n eng dst func scale view", defaults=(None, 1.0, None))


def project(nc, G, name, jobs):
    ps, ws = G.ps, G.ws
    lanes = {"v": [j for j in jobs if j.eng == "v"], "s": [j for j in jobs if j.eng == "s"]}
    units = sorted({j.unit for j in jobs if j.unit is not None})
    with stage(nc, f"{name}_v_ready", f"{name}_s_ready", f"{name}_v_out", f"{name}_s_out", "high_done", "low_done") as (
            block, v_ready, s_ready, v_out, s_out, high_done, low_done):
        ready, out = {"v": v_ready, "s": s_ready}, {"v": v_out, "s": s_out}
        bank = {"v": 0, "s": 4}

        def tile(j, k):
            return ps[0:j.m, bank[j.eng] + k % 4, 0:j.n]

        def by_unit(lane):
            ahead = 0
            for k, j in enumerate(lanes[lane]):
                until = min(len(units), units.index(j.unit) + 2) if units else 0
                yield range(ahead, until), k, j
                ahead = max(ahead, until)

        @block.tensor
        def _(pe):
            count = {"v": 0, "s": 0}
            seen = None
            for n, j in enumerate(jobs):
                k = count[j.eng]
                if k >= 4:
                    pe.wait_ge(out[j.eng], k - 3)
                if j.unit is None:
                    for c in range(j.nk):
                        mm = pe.matmul(tile(j, k), j.lhsT(c), j.rhs(c), start=(c == 0), stop=(c == j.nk - 1))
                else:
                    for c in range(j.nk):
                        if j.unit != seen and c % (DC // QUARTERS) == 0:
                            pe.wait_ge(low_done, units.index(j.unit) * QUARTERS + c // (DC // QUARTERS) + 1)
                        for x, y in PASSES:
                            mm = pe.matmul(tile(j, k), j.lhsT(c, x), j.rhs(c, y), start=(c == 0 and (x, y) == (0, 0)),
                                           stop=(c == j.nk - 1 and (x, y) == PASSES[-1]))
                    seen = j.unit
                mm.then_inc(ready[j.eng], 1)
                count[j.eng] = k + 1
                if j.unit is not None:
                    ws.done(j.unit, ready[j.eng], k + 1)

        @block.scalar
        def _(act):
            def split(i):
                ws.split_high(act, units[i], i, ws.release[units[i - 2]] if i >= 2 else None, high_done)

            ahead = 0
            for split_now, k, j in by_unit("s"):
                for i in split_now:
                    split(i)
                    ahead = i + 1
                act.wait_ge(s_ready, k + 1)
                src = tile(j, k)
                src = j.view(src) if j.view else src
                act.activation(j.dst, src, j.func or ACT.Identity, scale=j.scale).then_inc(s_out, 1)
            assert ahead == len(units)

        @block.vector
        def _(dve):
            ahead = 0
            for split_now, k, j in by_unit("v"):
                for i in split_now:
                    ws.split_low(dve, units[i], i, high_done, low_done)
                    ahead = i + 1
                dve.wait_ge(v_ready, k + 1)
                src = tile(j, k)
                src = j.view(src) if j.view else src
                if j.scale == 1.0:
                    dve.tensor_copy(j.dst, src).then_inc(v_out, 1)
                else:
                    dve.tensor_scalar(j.dst, src, j.scale, None, ALU.mult).then_inc(v_out, 1)
            assert ahead == len(units)

        @block.sync
        def _(sp):
            ws.run_ahead(sp)
    ws.stage_over()


def two_parts(nc, name, tok):
    return [sbuf(nc, f"{name}_{k}", [P, DC, tok], F32R) for k in ("high", "low")]


def transpose_in(nc, G, name, src, tiles, dst, scale=None, shift=None, loads=()):
    ps, ws = G.ps, G.ws
    high, low = dst
    BUFS = 4
    with scope():
        whole = sbuf(nc, "turned_whole", [P, BUFS, len(tiles) * P], F32)
        with stage(nc, f"{name}_turned", f"{name}_v_out", f"{name}_s_out", "high_done", "low_done", loads=loads) as (
                block, turned, v_out, s_out, high_done, low_done):
            pairs = len(tiles) // 2

            @block.tensor
            def _(pe):
                for c in range(DC):
                    for k, t in enumerate(tiles):
                        mm = pe.transpose(ps[:, c, k * P:(k + 1) * P], src(t, c), G.ident[:, :])
                    mm.then_inc(turned, 1)

            @block.vector
            def _(dve):
                def split(c):
                    dve.wait_ge(high_done, c + 1)
                    dve.tensor_tensor(low[:, c, :], whole[:, c % BUFS, :], high[:, c, :].bitcast(F32),
                                      ALU.subtract).then_inc(low_done, 1)
                for c in range(0, DC, 2):
                    dve.wait_ge(turned, c + 1)
                    if c >= BUFS:
                        dve.wait_ge(low_done, c - BUFS + 1)
                    for q in range(pairs):
                        o, i = whole[:, c % BUFS, q * SEQ:(q + 1) * SEQ], ps[:, c, q * SEQ:(q + 1) * SEQ]
                        if scale is None:
                            dve.tensor_copy(o, i).then_inc(v_out, 1)
                        elif shift is None:
                            dve.tensor_scalar(o, i, scale(c, q), None, ALU.mult).then_inc(v_out, 1)
                        else:
                            dve.tensor_scalar(o, i, scale(c, q), shift(c, q), ALU.mult, ALU.add).then_inc(v_out, 1)
                    if c >= 2:
                        split(c - 2)
                        split(c - 1)
                split(DC - 2)
                split(DC - 1)

            @block.scalar
            def _(act):
                for c in range(1, DC, 2):
                    act.wait_ge(turned, c + 1)
                    if c >= BUFS:
                        act.wait_ge(low_done, c - BUFS + 1)
                    for q in range(pairs):
                        o, i = whole[:, c % BUFS, q * SEQ:(q + 1) * SEQ], ps[:, c, q * SEQ:(q + 1) * SEQ]
                        if scale is None:
                            act.activation(o, i, ACT.Identity).then_inc(s_out, 1)
                        elif shift is None:
                            act.activation(o, i, ACT.Identity, scale=scale(c, q)).then_inc(s_out, 1)
                        else:
                            act.activation(o, i, ACT.Identity, scale=scale(c, q), bias=shift(c, q)).then_inc(s_out, 1)
                    for k, out in ((c - 1, v_out), (c, s_out)):
                        act.wait_ge(out, (k // 2 + 1) * pairs)
                        act.activation(high[:, k, :], whole[:, k % BUFS, :], ACT.Identity).then_inc(high_done, 1)

            @block.sync
            def _(sp):
                ws.run_ahead(sp)


class Modulation:

    def __init__(self, nc, G, name, layer, lo, hi, mod):
        self.G, self.ws, self.layer, self.lo, self.hi, self.mod = G, G.ws, layer, lo, hi, mod
        self.u0 = G.ws.first[name]
        self.part = sbuf(nc, "mod_parts", [P, 2, 512], F32)

    def __call__(self, block, sems):
        G, ws, ps, part, N = self.G, self.ws, self.G.ps, self.part, self.hi - self.lo
        parts_ready, parts_out, mod_ready = sems[:3]
        GROUPS, SUMS, PARTS = 4, 5, 6
        n0, n1 = 4 * self.lo, 4 * self.hi
        sums_of = ps[:, SUMS, 0:2 * (n1 - n0)]

        @block.tensor
        def _(pe):
            def parts(u):
                ws.wait_landed(pe, self.u0 + u)
                if u >= 2:
                    pe.wait_ge(parts_out, u - 1)
                w = ws.slot(self.u0 + u).rearrange("p (c n) -> p c n", c=DC)
                for c in range(DC):
                    g = c % GROUPS
                    mm = pe.matmul(ps[g * PAD:(g + 1) * PAD, PARTS + u % 2, :], G.sc[:, c, :], w[:, c, :],
                                   start=(c < GROUPS), stop=(c >= GROUPS), tile_position=(0, g * PAD))
                mm.then_inc(parts_ready, 1)
                ws.done(self.u0 + u, parts_ready, u + 1)

            def sums(u):
                pe.wait_ge(parts_out, u + 1)
                for q in range(4):
                    n = 4 * u + q
                    mm = pe.matmul(sums_of[:, 2 * n:2 * n + 2], part[:, u % 2, q * P:(q + 1) * P], G.pick[:, :],
                                   start=False, stop=True, skip_group_check=True)
                mm.then_inc(mod_ready, 1)

            pe.matmul(sums_of, G.ident[:, :], G.bias[:, self.layer, n0:n1, :].rearrange("p n k -> p (n k)"),
                      start=True, stop=False, skip_group_check=True)
            parts(0)
            for u in range(1, N):
                parts(u)
                sums(u - 1)
            sums(N - 1)

        @block.scalar
        def _(act):
            for u in range(N):
                act.wait_ge(parts_ready, u + 1)
                if u >= 2:
                    act.wait_ge(mod_ready, u - 1)
                act.activation(part[:, u % 2, :], ps[:, PARTS + u % 2, :], ACT.Identity).then_inc(parts_out, 1)
            act.wait_ge(mod_ready, N)
            act.activation(self.mod[:, n0:n1, :].rearrange("p n k -> p (n k)"), sums_of, ACT.Identity)


def gate_rows(nc, G, part, cols, out, banks=8):
    ps, mod = G.ps, G.mod
    with scope():
        diag = sbuf(nc, "gate_diag", [P, 4, P], F32)
        with stage(nc, "diag_ready", "rows_ready", "rows_out") as (block, diag_ready, rows_ready, rows_out):
            work = [(col, c) for col in cols for c in range(DC)]

            @block.vector
            def _(dve):
                for n, (col, c) in enumerate(work):
                    if n >= 4:
                        dve.wait_ge(rows_ready, n - 3)
                    dve.tensor_scalar(diag[:, n % 4, :], G.ident[:, :], mod[:, part * DC + c, col:col + 1], None,
                                      ALU.mult).then_inc(diag_ready, 1)

            @block.tensor
            def _(pe):
                for n, (col, c) in enumerate(work):
                    pe.wait_ge(diag_ready, n + 1)
                    if n >= banks:
                        pe.wait_ge(rows_out, n - banks + 1)
                    pe.matmul(ps[:, n % banks, 0:P], G.ones[:, :], diag[:, n % 4, :], start=True,
                              stop=True).then_inc(rows_ready, 1)

            @block.scalar
            def _(act):
                for n, (col, c) in enumerate(work):
                    act.wait_ge(rows_ready, n + 1)
                    act.activation(out[:, col, c * P:(c + 1) * P], ps[:, n % banks, 0:P], ACT.Identity).then_inc(rows_out, 1)

            @block.sync
            def _(sp):
                G.ws.run_ahead(sp)


def residual_norm(nc, G, name, tiles, banks, rows, cols, form, pre=None, units=(), loads=()):
    ps, x, ws = G.ps, G.x, G.ws
    eps = LN_EPS if form == "ln" else RMS_EPS
    with scope():
        z = sbuf(nc, "norm_z", [P, 2, D], F32)
        q = sbuf(nc, "norm_q", [P, 2, D], F32)
        st = sbuf(nc, "norm_stats", [P, 2, 16], F32)
        with stage(nc, "y_ready", "y_out", "var_ready", "std_ready", "norm_step", "part_done",
                   "high_done", "low_done", "squared", "rows_landed") as (
                block, y_ready, y_out, var_ready, std_ready, step_sem, part_done, high_done, low_done, squared,
                rows_landed):
            if pre is not None:
                @block.tensor
                def _(pe):
                    pre(pe, y_ready, part_done, low_done)

            @block.scalar
            def _(act):
                for i, n in enumerate(units):
                    ws.split_high(act, n, i, ws.release[units[i - 2]] if i >= 2 else None, high_done)
                for n, t in enumerate(tiles):
                    if form == "rms":
                        act.wait_ge(y_ready, n + 1)
                        if n >= 2:
                            act.wait_ge(step_sem, 3 * (n - 1))
                        act.activation(z[:, n % 2, :], ps[:, banks(n):banks(n) + 2, :].rearrange("p a b -> p (a b)"),
                                       ACT.Square, accum_out=st[:, n % 2, 0:1]).then_inc(squared, 1)
                    act.wait_ge(var_ready, n + 1)
                    act.activation(st[:, n % 2, 14:15], st[:, n % 2, 13:14], ACT.Sqrt).then_inc(std_ready, 1)

            @block.vector
            def _(dve):
                step = Steps(dve, step_sem)
                for i, n in enumerate(units):
                    ws.split_low(dve, n, i, high_done, low_done)
                dve.wait_ge(rows_landed, 16 * len(loads))
                for n, t in enumerate(tiles):
                    b = n % 2
                    zt, qt, s = z[:, b, :], q[:, b, :], st[:, b, :]
                    y = ps[:, banks(n):banks(n) + 2, :].rearrange("p a b -> p (a b)")
                    if pre is not None:
                        dve.wait_ge(y_ready, n + 1)
                    if form == "ln":
                        dve.tensor_tensor(zt, y, rows(cols[n]), ALU.mult).then_inc(y_out, 1)
                        dve.wait_ge(y_out, n + 1)
                        step(dve.scalar_tensor_tensor(zt, x[:, t, :], ALPHA, zt, ALU.mult, ALU.add))
                        step.wait()
                        for h in range(2):
                            step(dve.bn_stats(s[:, 6 * h:6 * h + 6], zt[:, h * 512:(h + 1) * 512]))
                        step.wait()
                        step(dve.bn_aggr(s[:, 12:14], s[:, 0:12]))
                        step.wait()
                        step(dve.tensor_copy(s[:, 15:16], s[:, 12:13]))
                        step.wait()
                        dve.tensor_scalar(s[:, 13:14], s[:, 13:14], eps, None, ALU.add).then_inc(var_ready, 1)
                        dve.wait_ge(std_ready, n + 1)
                        step(dve.reciprocal(s[:, 12:13], s[:, 14:15]))
                        step.wait()
                        step(dve.tensor_scalar(qt, zt, s[:, 15:16], s[:, 12:13], ALU.subtract, ALU.mult))
                        step.wait()
                        step(dve.tensor_tensor(zt, qt, rows("w"), ALU.mult))
                        step.wait()
                        step(dve.tensor_tensor(x[:, t, :], zt, rows("b"), ALU.add))
                    else:
                        dve.wait_ge(squared, n + 1)
                        dve.tensor_scalar(s[:, 13:14], s[:, 0:1], 1.0 / D, eps, ALU.mult, ALU.add).then_inc(var_ready, 1)
                        dve.wait_ge(std_ready, n + 1)
                        step(dve.reciprocal(s[:, 12:13], s[:, 14:15]))
                        step.wait()
                        step(dve.scalar_tensor_tensor(qt, y, s[:, 12:13], rows("w"), ALU.mult, ALU.mult))
                        step.wait()
                        step(dve.tensor_tensor(x[:, t, :], qt, x[:, t, :], ALU.add))
                    step.wait()

            @block.sync
            def _(sp):
                for dst, src in loads:
                    sp.dma_start(dst, src).then_inc(rows_landed, 16)
                G.ws.run_ahead(sp)
    G.ws.stage_over()


def part_products(pe, out, low_done, i, c, chunks, lhsT, rhs, first, last, wait):
    if wait:
        pe.wait_ge(low_done, i * QUARTERS + -(-(c + 1) * QUARTERS // chunks))
    for x, y in PASSES:
        mm = pe.matmul(out, lhsT(x), rhs(y), start=(first and (x, y) == PASSES[0]), stop=(last and (x, y) == PASSES[-1]))
    return mm


def out_project(G, u0, tiles, catT):
    ws, ps = G.ws, G.ps

    def pre(pe, y_ready, part_done, low_done):
        for n, t in enumerate(tiles):
            for h in range(2):
                w = [a.rearrange("p (c n) -> p c n", c=DC) for a in ws.parts(u0 + h)]
                for c in range(DC):
                    mm = part_products(pe, ps[:, 2 * n + h, :], low_done, h, c, DC,
                                       lambda x: catT[x][:, c, n * P:(n + 1) * P], lambda x: w[x][:, c, :],
                                       c == 0, c == DC - 1, n == 0)
            mm.then_inc(y_ready, 1)
        for h in range(2):
            ws.done(u0 + h, y_ready, len(tiles))
    return pre


def attend(nc, G, items):
    ps = G.ps
    R = 3
    TURN, OUT = 2, 3
    with scope():
        sm = sbuf(nc, "scores", [P, R, 512], F32)
        pr = sbuf(nc, "probs", [P, R, 512], F32)
        pT = sbuf(nc, "probsT", [P, 2, 512], F32)
        st = sbuf(nc, "soft_stats", [P, R, 8], F32)
        N = len(items)
        with stage(nc, "s_ready", "masked", "maxed", "negmax_ready", "probs_ready", "sum_ready", "turned", "pT_ready",
                   "pv_ready", "den_step", "rden_ready", "att_out") as (
                block, s_ready, masked, maxed, negmax_ready, probs_ready, sum_ready, turned, pT_ready, pv_ready,
                den_step, rden_ready, att_out):
            summed = probs_ready if items[0].sink is None else sum_ready

            @block.tensor
            def _(pe):
                for i in range(N + OUT):
                    if i < N:
                        it = items[i]
                        if i >= 2:
                            pe.wait_ge(masked, i - 1)
                        pe.matmul(ps[:, i % 2, 0:it.nk], it.q, it.k, start=True, stop=True).then_inc(s_ready, 1)
                    if TURN <= i < N + TURN:
                        n = i - TURN
                        it = items[n]
                        pe.wait_ge(probs_ready, n + 1)
                        if n >= 2:
                            pe.wait_ge(pT_ready, n - 1)
                        for k in range(it.nk // P):
                            mm = pe.transpose(ps[:, 2 + n % 2, k * P:(k + 1) * P], pr[:, n % R, k * P:(k + 1) * P],
                                              G.ident[:, :])
                        mm.then_inc(turned, 1)
                    if OUT <= i:
                        n = i - OUT
                        it = items[n]
                        pe.wait_ge(pT_ready, n + 1)
                        if n >= 2:
                            pe.wait_ge(att_out, n - 1)
                        for k in range(it.nk // P):
                            mm = pe.matmul(ps[:, 4 + n % 2, 0:DH_A], pT[:, n % 2, k * P:(k + 1) * P], it.v[k],
                                           start=(k == 0), stop=(k == it.nk // P - 1))
                        mm.then_inc(pv_ready, 1)

            @block.vector
            def _(dve):
                for i in range(N + OUT):
                    if i < N:
                        it, b = items[i], i % R
                        dve.wait_ge(s_ready, i + 1)
                        if i >= R:
                            dve.wait_ge(probs_ready, i - R + 1)
                        s, src = sm[:, b, 0:it.nk], ps[:, i % 2, 0:it.nk]
                        if it.mask is None:
                            dve.tensor_scalar(s, src, DH_A ** -0.5, None, ALU.mult).then_inc(masked, 1)
                        else:
                            dve.scalar_tensor_tensor(s, src, DH_A ** -0.5, it.mask, ALU.mult, ALU.add).then_inc(masked, 1)
                        dve.wait_ge(masked, i + 1)
                        if i >= R:
                            dve.wait_ge(summed, i - R + 1)
                            dve.wait_ge(rden_ready, i - R + 1)
                        dve.tensor_reduce(st[:, b, 0:1], s, AX.X, ALU.max).then_inc(maxed, 1)
                        dve.wait_ge(maxed, i + 1)
                        if it.sink is None:
                            dve.tensor_scalar(st[:, b, 1:2], st[:, b, 0:1], -1.0, None, ALU.mult).then_inc(negmax_ready, 1)
                        else:
                            dve.tensor_scalar(st[:, b, 1:2], st[:, b, 0:1], it.sink, -1.0, ALU.max,
                                              ALU.mult).then_inc(negmax_ready, 1)
                    if TURN <= i < N + TURN:
                        n = i - TURN
                        it, b = items[n], n % R
                        dve.wait_ge(summed, n + 1)
                        if it.sink is None:
                            dve.tensor_copy(st[:, b, 4:5], st[:, b, 2:3]).then_inc(den_step, 1)
                        else:
                            dve.tensor_tensor(st[:, b, 4:5], st[:, b, 2:3], st[:, b, 3:4], ALU.add).then_inc(den_step, 1)
                        dve.wait_ge(den_step, n + 1)
                        if n >= R:
                            dve.wait_ge(att_out, n - R + 1)
                        dve.reciprocal(st[:, b, 5:6], st[:, b, 4:5]).then_inc(rden_ready, 1)
                    if OUT <= i:
                        n = i - OUT
                        it, b = items[n], n % R
                        dve.wait_ge(pv_ready, n + 1)
                        dve.wait_ge(rden_ready, n + 1)
                        dve.tensor_scalar(it.out, ps[:, 4 + n % 2, 0:DH_A], st[:, b, 5:6], None, ALU.mult).then_inc(att_out, 1)

            @block.scalar
            def _(act):
                for i in range(N + TURN):
                    if i < N:
                        it, b = items[i], i % R
                        act.wait_ge(negmax_ready, i + 1)
                        if i >= R:
                            act.wait_ge(turned, i - R + 1)
                            act.wait_ge(den_step, i - R + 1)
                        act.activation(pr[:, b, 0:it.nk], sm[:, b, 0:it.nk], ACT.Exp, bias=st[:, b, 1:2],
                                       accum_out=st[:, b, 2:3]).then_inc(probs_ready, 1)
                        if it.sink is not None:
                            act.activation(st[:, b, 3:4], it.sink, ACT.Exp, bias=st[:, b, 1:2]).then_inc(sum_ready, 1)
                    if TURN <= i:
                        n = i - TURN
                        it = items[n]
                        act.wait_ge(turned, n + 1)
                        if n >= 2:
                            act.wait_ge(pv_ready, n - 1)
                        act.activation(pT[:, n % 2, 0:it.nk], ps[:, 2 + n % 2, 0:it.nk], ACT.Identity).then_inc(pT_ready, 1)

            @block.sync
            def _(sp):
                G.ws.run_ahead(sp)


Item = namedtuple("Item", "q k nk mask sink v out")



def mlstm_gates(nc, G, gi, gf, gcol, negM, beside):
    ps = G.ps
    with scope():
        gb = sbuf(nc, "gate_b", [H_M, 4], F32)
        xi = sbuf(nc, "gate_i", [H_M, 2, TOK], F32)
        xf = sbuf(nc, "gate_f", [H_M, 2, TOK], F32)
        t1 = sbuf(nc, "gate_t1", [H_M, 2, TOK], F32)
        t2 = sbuf(nc, "gate_t2", [H_M, 2, TOK], F32)
        one = sbuf(nc, "gate_one", [H_M, TOK], F32)
        zero = sbuf(nc, "gate_zero", [H_M, TOK], F32)
        nat = sbuf(nc, "gate_nat", [H_M, 2, 2, TOK], F32)
        with stage(nc, "gb_landed", "gate_step", "abs_ready", "log1p_ready", "exp_step", "m_ready", "em_ready",
                   "nat_ready", "cols_ready", beside=beside) as (
                block, gb_landed, step_sem, abs_ready, log1p_ready, exp_step, m_ready, em_ready, nat_ready, cols_ready):
            @block.sync
            def _(sp):
                sp.dma_start(gb[:, :], G.d["ab_gate_b"]).then_inc(gb_landed, 16)
                G.ws.run_ahead(sp)

            def in_scan_order(d, dst, src):
                a = (dst[:, d, 0:CTX], src[:, d, SEQ:TOK] if d == 0 else src[:, d, TOK - 1:SEQ - 1:-1])
                b = (dst[:, d, CTX:TOK], src[:, d, 0:SEQ] if d == 0 else src[:, d, SEQ - 1::-1])
                return a, b

            def in_token_order(d, dst, src):
                a = (dst[:, d, SEQ:TOK], src[:, d, 0:CTX] if d == 0 else src[:, d, CTX - 1::-1])
                b = (dst[:, d, 0:SEQ], src[:, d, CTX:TOK] if d == 0 else src[:, d, TOK - 1:CTX - 1:-1])
                return a, b

            @block.vector
            def _(dve):
                step = Steps(dve, step_sem)
                step(dve.memset(one[:, :], 1.0))
                step(dve.memset(zero[:, :], 0.0))
                dve.wait_ge(gb_landed, 16)
                for d in range(2):
                    for o, i in in_scan_order(d, xi, gi):
                        step(dve.tensor_scalar(o, i, gb[:, d:d + 1], None, ALU.add))
                    for o, i in in_scan_order(d, xf, gf):
                        step(dve.tensor_scalar(o, i, gb[:, 2 + d:3 + d], None, ALU.add))
                step.wait()
                dve.scalar_tensor_tensor(t1[:, :, :], xf[:, :, :], -1.0, xf[:, :, :], ALU.mult, ALU.max).then_inc(abs_ready, 1)
                dve.wait_ge(log1p_ready, 1)
                step(dve.scalar_tensor_tensor(xf[:, :, :], xf[:, :, :], 0.0, t1[:, :, :], ALU.min, ALU.subtract))
                step.wait()
                for d in range(2):
                    step(dve.tensor_tensor_scan(t1[:, d, :], one[:, :], xf[:, d, :], 0.0, ALU.mult, ALU.add))
                step.wait()
                step(dve.tensor_tensor(t2[:, :, :], xi[:, :, :], t1[:, :, :], ALU.subtract))
                step.wait()
                for d in range(2):
                    step(dve.tensor_tensor_scan(xi[:, d, :], zero[:, :], t2[:, d, :], 0.0, ALU.max, ALU.max))
                step.wait()
                dve.tensor_tensor(xf[:, :, :], xi[:, :, :], t1[:, :, :], ALU.add).then_inc(m_ready, 1)
                for d in range(2):
                    for o, i in in_token_order(d, negM, xi):
                        step(dve.tensor_scalar(o, i, -1.0, None, ALU.mult))
                    for o, i in in_token_order(d, nat[:, 0], t2):
                        step(dve.tensor_copy(o, i))
                dve.wait_ge(em_ready, 1)
                for d in range(2):
                    for o, i in in_token_order(d, nat[:, 1], t1):
                        last = dve.tensor_copy(o, i)
                        if d == 0:
                            step(last)
                        elif o is not None:
                            last.then_inc(nat_ready, 1)
                dve.wait_ge(cols_ready, 1)
                step(dve.tensor_copy(gcol[:, :, :, :, :].rearrange("p k d t h -> p (k d t h)"), ps[:, 0, 0:64]))
                step.wait()

            @block.scalar
            def _(act):
                act.wait_ge(abs_ready, 1)
                act.activation(t2[:, :, :], t1[:, :, :], ACT.Exp, scale=-1.0).then_inc(exp_step, 1)
                act.wait_ge(exp_step, 1)
                act.activation(t1[:, :, :], t2[:, :, :], ACT.Ln, bias=1.0).then_inc(log1p_ready, 1)
                act.wait_ge(m_ready, 1)
                act.activation(t1[:, :, :], xf[:, :, :], ACT.Exp, scale=-1.0).then_inc(em_ready, 1)

            @block.tensor
            def _(pe):
                pe.wait_ge(nat_ready, 2)
                for kind in range(2):
                    for d in range(2):
                        for t in range(4):
                            n = (kind * 2 + d) * 4 + t
                            mm = pe.transpose(ps[:, 0, 4 * n:4 * n + 4], nat[:, kind, d, t * P:(t + 1) * P],
                                              G.ident[0:H_M, 0:H_M])
                mm.then_inc(cols_ready, 1)


QK_PARTS = [(0, 0, SEQ, 0), (1, 0, SEQ, SEQ), (2, 0, TOK, 2 * SEQ), (3, 0, TOK, 2 * SEQ + TOK)]
QK_WIDTH = 2 * SEQ + 2 * TOK


def mlstm(nc, G, qT, kT, v1, gcol, negM, hm):
    ps = G.ps
    with scope():
        mask = sbuf(nc, "scan_mask", [P, 2, QK_WIDTH], F32)
        sel = sbuf(nc, "row_select", [H_M, H_M, P], F32)
        qk = sbuf(nc, "qk", [P, 2, QK_WIDTH], F32)
        w = sbuf(nc, "mlstm_w", [P, 2, QK_WIDTH], F32)
        dt_ = sbuf(nc, "mlstm_d", [P, 2, TOK], F32)
        de = sbuf(nc, "mlstm_den", [P, 2, 8], F32)
        combos = [(h, d) for h in range(H_M) for d in range(2)]
        with stage(nc, "mask_landed", "qk_ready", "qk_out", "mb_ready", "d_ready", "exp_ready", "w_ready", "num_ready",
                   "den_step", "h_out") as (
                block, mask_landed, qk_ready, qk_out, mb_ready, d_ready, exp_ready, w_ready, num_ready, den_step, h_out):
            @block.sync
            def _(sp):
                sp.dma_start(mask[:, :, :], G.d["scan_mask"]).then_inc(mask_landed, 16)
                sp.dma_start(sel[:, :, :], G.d["row_select"]).then_inc(mask_landed, 16)
                G.ws.run_ahead(sp)

            @block.tensor
            def _(pe):
                pe.wait_ge(mask_landed, 32)

                def products(h):
                    for n, (s, q0, nq, _) in enumerate(QK_PARTS):
                        k = 4 * h + n
                        if k >= 2:
                            pe.wait_ge(qk_out, k - 1)
                        pe.matmul(ps[:, k % 2, 0:nq], kT[:, h, s * P:(s + 1) * P], qT[:, h, q0:q0 + nq], start=True,
                                  stop=True).then_inc(qk_ready, 1)

                def weighted(n):
                    h, d = combos[n]
                    pe.wait_ge(w_ready, 4 * (n + 1))
                    if n >= 2:
                        pe.wait_ge(h_out, n - 1)
                    for t in range(4):
                        keys = [0, 1, 2, 3] if t < 2 else [2, 3]
                        bank = 4 + 2 * (n % 2) + t // 2
                        for i, s in enumerate(keys):
                            _, _, _, at = QK_PARTS[s]
                            mm = pe.matmul(ps[:, bank, (t % 2) * 129:(t % 2) * 129 + 129],
                                           w[:, n % 2, at + t * P:at + (t + 1) * P], v1[:, s, h, :],
                                           start=(i == 0), stop=(i == len(keys) - 1))
                    mm.then_inc(num_ready, 1)

                products(0)
                for n, (h, d) in enumerate(combos):
                    if n >= 2:
                        pe.wait_ge(d_ready, 4 * (n - 1))
                    pe.matmul(ps[:, 2 + n % 2, :], sel[:, h, :], negM[:, d, :], start=True, stop=True).then_inc(mb_ready, 1)
                    if d == 1 and h + 1 < H_M:
                        products(h + 1)
                    if n >= 1:
                        weighted(n - 1)
                weighted(len(combos) - 1)

            @block.vector
            def _(dve):
                def finish(n):
                    h, d = combos[n]
                    dve.wait_ge(num_ready, n + 1)
                    e = de[:, n % 2, :]
                    src = ps[:, 4 + 2 * (n % 2):6 + 2 * (n % 2), 0:258].rearrange("p b (t c) -> p b t c", c=129)
                    e2 = e[:, 0:4].rearrange("p (b t) -> p b t", b=2)
                    dve.tensor_tensor(e2, src[:, :, :, 128], gcol[:, 1, d, :, h].rearrange("p (b t) -> p b t", b=2),
                                      ALU.max).then_inc(den_step, 1)
                    dve.wait_ge(den_step, 3 * n + 1)
                    dve.scalar_tensor_tensor(e2, src[:, :, :, 128], -1.0, e2, ALU.mult, ALU.max).then_inc(den_step, 1)
                    dve.wait_ge(den_step, 3 * n + 2)
                    dve.reciprocal(e[:, 4:8], e[:, 0:4]).then_inc(den_step, 1)
                    dve.wait_ge(den_step, 3 * n + 3)
                    if d == 1:
                        dve.wait_ge(h_out, n)
                    for t in range(4):
                        o = hm[:, t, h * DH_M:(h + 1) * DH_M]
                        i = ps[:, 4 + 2 * (n % 2) + t // 2, (t % 2) * 129:(t % 2) * 129 + 128]
                        if d == 0:
                            last = dve.tensor_scalar(o, i, e[:, 4 + t:5 + t], None, ALU.mult)
                        else:
                            last = dve.scalar_tensor_tensor(o, i, e[:, 4 + t:5 + t], o, ALU.mult, ALU.add)
                    last.then_inc(h_out, 1)

                dve.wait_ge(mask_landed, 32)
                for n, (h, d) in enumerate(combos):
                    dve.wait_ge(mb_ready, n + 1)
                    for i in range(5):
                        if i < 4:
                            k = 4 * n + i
                            s, q0, nq, at = QK_PARTS[i]
                            if k >= 2:
                                dve.wait_ge(w_ready, k - 1)
                            dve.scalar_tensor_tensor(dt_[:, k % 2, 0:nq], ps[:, 2 + n % 2, q0:q0 + nq],
                                                     gcol[:, 0, d, s, h:h + 1], mask[:, d, at:at + nq], ALU.add,
                                                     ALU.min).then_inc(d_ready, 1)
                        if i >= 1:
                            k = 4 * n + i - 1
                            s, q0, nq, at = QK_PARTS[i - 1]
                            dve.wait_ge(exp_ready, k + 1)
                            dve.wait_ge(qk_out, 4 * h + i)
                            if n >= 2:
                                dve.wait_ge(num_ready, n - 1)
                            dve.tensor_tensor(w[:, n % 2, at:at + nq], dt_[:, k % 2, 0:nq], qk[:, h % 2, at:at + nq],
                                              ALU.mult).then_inc(w_ready, 1)
                    if n >= 1:
                        finish(n - 1)
                finish(len(combos) - 1)

            @block.scalar
            def _(act):
                def products_out(h):
                    for n, (s, q0, nq, at) in enumerate(QK_PARTS):
                        act.wait_ge(qk_ready, 4 * h + n + 1)
                        if h >= 2:
                            act.wait_ge(w_ready, 8 * (h - 1))
                        act.activation(qk[:, h % 2, at:at + nq], ps[:, (4 * h + n) % 2, 0:nq],
                                       ACT.Identity).then_inc(qk_out, 1)

                products_out(0)
                for n, (h, d) in enumerate(combos):
                    for i, (s, q0, nq, at) in enumerate(QK_PARTS):
                        k = 4 * n + i
                        act.wait_ge(d_ready, k + 1)
                        act.activation(dt_[:, k % 2, 0:nq], dt_[:, k % 2, 0:nq], ACT.Exp).then_inc(exp_ready, 1)
                    if d == 1 and h + 1 < H_M:
                        products_out(h + 1)


def head_norm(nc, G, name, src, tiles, heads, width, wrow, gate, dst, eps, beside=None):
    with scope():
        w = sbuf(nc, "head_w", [P, heads * width], F32)
        sq = sbuf(nc, "head_sq", [P, heads * width], F32)
        ms = sbuf(nc, "head_ms", [P, tiles, heads, 2], F32)
        with stage(nc, "w_landed", "hn_step", "ms_ready", "rms_ready", beside=beside) as (
                block, w_landed, step_sem, ms_ready, rms_ready):
            @block.sync
            def _(sp):
                sp.dma_start(w[:, :], wrow.partition_broadcast(P)).then_inc(w_landed, 16)
                G.ws.run_ahead(sp)

            @block.scalar
            def _(act):
                act.wait_ge(ms_ready, tiles)
                act.activation(ms[:, :, :, 1], ms[:, :, :, 0], ACT.Sqrt).then_inc(rms_ready, 1)

            @block.vector
            def _(dve):
                step = Steps(dve, step_sem)
                for n in range(tiles):
                    h3 = src(n)
                    s3 = sq[:, :].rearrange("p (h c) -> p h c", h=heads)
                    step(dve.tensor_tensor(s3, h3, h3, ALU.mult))
                    step.wait()
                    step(dve.tensor_reduce(ms[:, n, :, 0], s3, AX.X, ALU.add))
                    step.wait()
                    dve.tensor_scalar(ms[:, n, :, 0], ms[:, n, :, 0], 1.0 / width, eps, ALU.mult, ALU.add).then_inc(ms_ready, 1)
                dve.wait_ge(rms_ready, 1)
                step(dve.reciprocal(ms[:, :, :, 0], ms[:, :, :, 1]))
                step.wait()
                dve.wait_ge(w_landed, 16)
                w3 = w[:, :].rearrange("p (h c) -> p h c", h=heads)
                for n in range(tiles):
                    r = ms[:, n, :, 0:1].broadcast_to([P, heads, width])
                    step(dve.tensor_tensor(dst(n), src(n), r, ALU.mult))
                    step.wait()
                    step(dve.tensor_tensor(dst(n), dst(n), w3, ALU.mult))
                    step.wait()
                    step(dve.tensor_tensor(dst(n), dst(n), gate(n), ALU.mult))
                    step.wait()


def rope(nc, G, qa, ka):
    ps = G.ps
    with scope():
        cos = sbuf(nc, "rope_cos", [P, SEQ], F32)
        sin = sbuf(nc, "rope_sin", [P, SEQ], F32)
        swap = sbuf(nc, "rope_swap", [P, P], F32)
        t = sbuf(nc, "rope_t", [P, 6, SEQ], F32)
        rows = [qa[:, n, 0:SEQ] for n in range(4)] + [ka[:, n, 0:SEQ] for n in range(2)]
        with stage(nc, "rope_landed", "swapped", "rope_step") as (block, rope_landed, swapped, step_sem):
            @block.sync
            def _(sp):
                sp.dma_start(cos[:, :], G.d["rope_cos"]).then_inc(rope_landed, 16)
                sp.dma_start(sin[:, :], G.d["rope_sin"]).then_inc(rope_landed, 16)
                sp.dma_start(swap[:, :], G.d["rope_swap"]).then_inc(rope_landed, 16)
                G.ws.run_ahead(sp)

            @block.tensor
            def _(pe):
                pe.wait_ge(rope_landed, 48)
                for n, r in enumerate(rows):
                    pe.matmul(ps[:, n, 0:SEQ], swap[:, :], r, start=True, stop=True).then_inc(swapped, 1)

            @block.vector
            def _(dve):
                step = Steps(dve, step_sem)
                dve.wait_ge(rope_landed, 48)
                for n, r in enumerate(rows):
                    dve.wait_ge(swapped, n + 1)
                    step(dve.tensor_tensor(t[:, n, :], ps[:, n, 0:SEQ], sin[:, :], ALU.mult))
                    step(dve.tensor_tensor(r, r, cos[:, :], ALU.mult))
                    step.wait()
                    step(dve.tensor_tensor(r, r, t[:, n, :], ALU.add))
                step.wait()


def mixer_ab(nc, G):
    ws = G.ws
    u0 = ws.first["ab_in"]
    with scope():
        cat = sbuf(nc, "cat", [P, 4, D], F32)
        with scope():
            hm = cat[:, :, 512:1024]
            so = sbuf(nc, "sig_o", [P, 4, 512], F32)
            qa = sbuf(nc, "qa", [P, 4, TOK], F32)
            ka = sbuf(nc, "ka", [P, 2, TOK], F32)
            va = sbuf(nc, "va", [P, 4, P], F32)
            with scope():
                qT = sbuf(nc, "qT", [P, H_M, TOK], F32)
                kT = sbuf(nc, "kT", [P, H_M, TOK], F32)
                v1 = sbuf(nc, "v1", [P, 4, H_M, 129], F32)
                gcol = sbuf(nc, "gcol", [P, 2, 2, 4, H_M], F32)
                negM = sbuf(nc, "negM", [H_M, 2, TOK], F32)
                with scope():
                    gi = sbuf(nc, "gi", [H_M, 2, TOK], F32)
                    gf = sbuf(nc, "gf", [H_M, 2, TOK], F32)
                    with scope():
                        hT = two_parts(nc, "hT", TOK)
                        with stage(nc, "ones_set") as (block, ones_set):
                            @block.gpsimd
                            def _(pool):
                                pool.memset(v1[:, :, :, 128:129], 1.0).then_inc(ones_set, 1)
                                pool.wait_ge(ones_set, 1)
                        transpose_in(nc, G, "h1", lambda t, c: G.x[:, t, c * P:(c + 1) * P], [0, 1, 2, 3], hT,
                                     scale=lambda c, q: G.mod[:, DC + c, q:q + 1], shift=lambda c, q: G.mod[:, c, q:q + 1])

                        ws.make_high(nc)

                        def unit(k, n=512):
                            return [w[:, 0:DC * n].rearrange("p (c n) -> p c n", c=DC) for w in ws.parts(u0 + k)]

                        def cols(k, off, m, eng, dst, n=512, scale=1.0):
                            return Job(u0 + k, DC, lambda c, x: unit(k, n)[x][:, c, off:off + m], lambda c, x: hT[x][:, c, :], m, TOK,
                                       eng, dst, scale=scale)

                        def rows(k, t, off, m, eng, dst, n=512, func=None, view=None):
                            return Job(u0 + k, DC, lambda c, x: hT[x][:, c, t * P:(t + 1) * P],
                                       lambda c, x: unit(k, n)[x][:, c, off:off + m], P, m, eng, dst, func=func, view=view)
                        jobs = []
                        for h in range(4):
                            jobs.append(cols(0, h * P, P, "vs"[h % 2], qT[:, h, :]))
                        for h in range(4):
                            jobs.append(cols(1, h * P, P, "vs"[h % 2], kT[:, h, :], scale=DH_M ** -0.5))
                        for t in range(4):
                            jobs.append(rows(2, t, 0, 512, "v", v1[:, t, :, 0:128],
                                             view=lambda a: a.rearrange("p (h c) -> p h c", h=4)))
                        for t in range(4):
                            jobs.append(rows(3, t, 0, 512, "s", so[:, t, :], func=ACT.Sigmoid))
                        for h in range(4):
                            jobs.append(cols(4, h * P, P, "vs"[h % 2], qa[:, h, :]))
                        for g in range(2):
                            jobs.append(cols(5, g * P, P, "vs"[g % 2], ka[:, g, :], n=400))
                        for t in range(4):
                            jobs.append(rows(5, t, 256, P, "vs"[t % 2], va[:, t, :], n=400))
                        for d in range(2):
                            jobs.append(cols(5, 384 + 4 * d, 4, "v", gi[:, d, :], n=400))
                            jobs.append(cols(5, 392 + 4 * d, 4, "s", gf[:, d, :], n=400))
                        project(nc, G, "ab_in", jobs)
                    mlstm_gates(nc, G, gi, gf, gcol, negM, Modulation(nc, G, "mod_b", 0, 4, 8, G.mod))
                mlstm(nc, G, qT, kT, v1, gcol, negM, hm)
            with scope():
                head_norm(nc, G, "ab", lambda n: hm[:, n, :].rearrange("p (h c) -> p h c", h=H_M), 4, H_M, DH_M,
                          G.d["ab_norm_w"], lambda n: so[:, n, :].rearrange("p (h c) -> p h c", h=H_M),
                          lambda n: cat[:, n, 0:512].rearrange("p (h c) -> p h c", h=H_M), LN_EPS,
                          beside=Modulation(nc, G, "mod_c", 0, 8, 12, G.mod))
            rope(nc, G, qa, ka)
            with scope():
                wm = sbuf(nc, "window_mask", [P, 2, TOK], F32)
                sink = sbuf(nc, "sink", [P, H_A], F32)
                with stage(nc, "wm_landed") as (block, wm_landed):
                    @block.sync
                    def _(sp):
                        sp.dma_start(wm[:, :, :], G.d["window_mask"]).then_inc(wm_landed, 16)
                        sp.dma_start(sink[:, :], G.d["ab_sink"].partition_broadcast(P)).then_inc(wm_landed, 16)
                        sp.wait_ge(wm_landed, 32)
                items = []
                for t in range(4):
                    for h in range(H_A):
                        o, g = (h % 2) * DH_A, h // (H_A // H_KV)
                        keys = range(4) if t < 2 else (2, 3)
                        k0 = 0 if t < 2 else SEQ
                        items.append(Item(qa[o:o + DH_A, h // 2, t * P:(t + 1) * P], ka[o:o + DH_A, g, k0:TOK],
                                          TOK - k0, wm[:, t, :] if t < 2 else None, sink[:, h:h + 1],
                                          [va[:, k, g * DH_A:(g + 1) * DH_A] for k in keys],
                                          cat[:, t, 512 + h * DH_A:512 + (h + 1) * DH_A]))
                attend(nc, G, items)
        with scope():
            catT = two_parts(nc, "catT", TOK)
            grow = sbuf(nc, "gate_row", [P, 2, D], F32)
            transpose_in(nc, G, "cat", lambda t, c: cat[:, t, c * P:(c + 1) * P], [0, 1, 2, 3], catT)
            gate_rows(nc, G, 2, [0, 1], grow)
            ws.make_high(nc)
            with_rows(nc, G, 0, 0, [0, 1, 2, 3], out_project(G, ws.first["ab_out"], [0, 1, 2, 3], catT), grow,
                      units=[ws.first["ab_out"] + h for h in range(2)])


def with_rows(nc, G, layer, which, tiles, pre, grow, banks=lambda n: 2 * n, units=()):
    with scope():
        wr = sbuf(nc, "ln_w_row", [P, D], F32)
        br = sbuf(nc, "ln_b_row", [P, D], F32)
        n = layer * 2 + which
        loads = [(wr[:, :], G.d["ln_w"][n].partition_broadcast(P)), (br[:, :], G.d["ln_b"][n].partition_broadcast(P))]
        rows = {"w": wr[:, :], "b": br[:, :], 0: grow[:, 0, :], 1: grow[:, 1, :]}
        residual_norm(nc, G, "ln", tiles, banks, lambda k: rows[k], [t // 2 for t in tiles], "ln", pre, units, loads)



PAIRS = PEER_HEADS * PEER_TOPK
PT = 2
UJ = 2
BODY = UJ * SLOTS
TURNS = N_KEYS // BODY
REST = N_KEYS - TURNS * BODY
FIRST_TURNS = (TURNS + 1) // 2
NJ = FIRST_TURNS * BODY


def top16(dve, step, lanes):
    for vals, idx, src, work in lanes:
        step(dve.max(vals[:, 0:8], src))
    step.wait()
    for vals, idx, src, work in lanes:
        step(dve.max_index(idx[:, 0:8], vals[:, 0:8], src))
        step(dve.match_replace(work, vals[:, 0:8], src, TAKEN))
    step.wait()
    for vals, idx, src, work in lanes:
        step(dve.max(vals[:, 8:16], work))
    step.wait()
    for vals, idx, src, work in lanes:
        step(dve.max_index(idx[:, 8:16], vals[:, 8:16], work))
    step.wait()


def peer_select(nc, G, layer, scores, table, beside):
    ps = G.ps
    LANES = 4
    JS = 8
    CANDS = 16 + 15 * JS
    with scope():
        work = sbuf(nc, "top_work", [P, LANES, CANDS], F32)
        cand = sbuf(nc, "cand", [P, LANES, CANDS], F32)
        top = sbuf(nc, "top_vals", [P, 2 * PEER_HEADS, 16], F32)
        ti = sbuf(nc, "top_idx", [P, 2 * PEER_HEADS, 16], U32)
        tif = sbuf(nc, "top_idx_f", [P, PT, 2 * PEER_HEADS, 16], F32)
        best = sbuf(nc, "best", [P, PT, PEER_HEADS, 16], F32)
        pos = sbuf(nc, "best_pos", [P, PEER_HEADS, 16], U32)
        row = sbuf(nc, "pos_row", [P, PAIRS], U32)
        posf = sbuf(nc, "pos_f", [P, 3, PAIRS], F32)
        ij = sbuf(nc, "pos_ij", [P, 2, PAIRS], F32)
        hot = sbuf(nc, "one_hot", [P, PT, 2, PAIRS, 16], F32)
        sel = sbuf(nc, "selected", [P, PT, 3, PAIRS], F32)
        shift = sbuf(nc, "best_shift", [P, PT, PEER_HEADS, 16], F32)
        ex = sbuf(nc, "best_exp", [P, PT, PEER_HEADS, 16], F32)
        sm = sbuf(nc, "best_sum", [P, PT, PEER_HEADS, 2], F32)
        with stage(nc, "sel_step", "shift_ready", "best_exp_ready", "hot_ready", "keyed_ready", "sel_ready",
                   "sel_turned", beside=beside) as (
                block, step_sem, shift_ready, exp_ready, hot_ready, keyed_ready, sel_ready, sel_turned):
            @block.vector
            def _(dve):
                step = Steps(dve, step_sem)
                for t in range(PT):
                    for n0 in range(0, 2 * PEER_HEADS, LANES):
                        top16(dve, step, [(top[:, n, :], ti[:, n, :], scores[:, t, n, :], work[:, n - n0, 0:N_KEYS])
                                          for n in range(n0, n0 + LANES)])
                    step(dve.tensor_copy(tif[:, t, :, :], ti[:, :, :]))
                    for h0 in range(0, PEER_HEADS, LANES):
                        pairs = top[:, 2 * h0:2 * (h0 + LANES), :].rearrange("p (h k) c -> p h k c", k=2)
                        first, second = pairs[:, :, 0, :], pairs[:, :, 1, :]
                        step(dve.tensor_tensor(cand[:, :, 0:16], first[:, :, 0:1].broadcast_to([P, LANES, 16]), second,
                                               ALU.add))
                        step(dve.tensor_tensor(cand[:, :, 16:].rearrange("p h (a b) -> p h a b", b=JS),
                                               first[:, :, 1:16].unsqueeze(3).broadcast_to([P, LANES, 15, JS]),
                                               second[:, :, 0:JS].unsqueeze(2).broadcast_to([P, LANES, 15, JS]), ALU.add))
                        step.wait()
                        top16(dve, step, [(best[:, t, h, :], pos[:, h, :], cand[:, h - h0, :], work[:, h - h0, :])
                                          for h in range(h0, h0 + LANES)])
                    dve.tensor_tensor(shift[:, t, :, :], best[:, t, :, :],
                                      best[:, t, :, 0:1].broadcast_to([P, PEER_HEADS, 16]),
                                      ALU.subtract).then_inc(shift_ready, 1)
                    pflat = pos[:, :, :].rearrange("p h m -> p (h m)")
                    step(dve.tensor_scalar(row[:, :], pflat, 3, None, ALU.logical_shift_right))
                    step(dve.tensor_copy(posf[:, 0, :], pflat))
                    step.wait()
                    step(dve.tensor_copy(posf[:, 1, :], row[:, :]))
                    step.wait()
                    step(dve.tensor_scalar(ij[:, 0, :], posf[:, 1, :], 1.0, -1.0, ALU.max, ALU.add))
                    step.wait()
                    step(dve.scalar_tensor_tensor(posf[:, 2, :], ij[:, 0, :], 1.0, ij[:, 0, :], ALU.min, ALU.add))
                    step.wait()
                    step(dve.scalar_tensor_tensor(ij[:, 1, :], posf[:, 2, :], -8.0, posf[:, 0, :], ALU.mult, ALU.add))
                    step.wait()
                    for which in range(2):
                        dve.tensor_tensor(hot[:, t, which, :, :],
                                          ij[:, which, :].unsqueeze(2).broadcast_to([P, PAIRS, 16]),
                                          G.iota[:, 0:16].unsqueeze(1).broadcast_to([P, PAIRS, 16]),
                                          ALU.is_equal).then_inc(hot_ready, 1)
                for t in range(PT):
                    dve.wait_ge(exp_ready, t + 1)
                    step(dve.tensor_reduce(sm[:, t, :, 0], ex[:, t, :, :], AX.X, ALU.add))
                    step.wait()
                    step(dve.reciprocal(sm[:, t, :, 1], sm[:, t, :, 0]))
                    step.wait()
                    dve.tensor_tensor(sel[:, t, 2, :].rearrange("p (h m) -> p h m", h=PEER_HEADS), ex[:, t, :, :],
                                      sm[:, t, :, 1:2].broadcast_to([P, PEER_HEADS, 16]), ALU.mult).then_inc(sel_ready, 1)
                    for which in range(2):
                        dve.wait_ge(keyed_ready, 2 * t + which + 1)
                        dve.tensor_reduce(sel[:, t, which, :], hot[:, t, which, :, :], AX.X, ALU.add).then_inc(sel_ready, 1)
                for t in range(PT):
                    dve.wait_ge(sel_turned, t + 1)
                    step(dve.tensor_copy(table[:, :, t * P:(t + 1) * P],
                                         ps[:, t, 0:3 * P].rearrange("p (k c) -> p k c", k=3)))
                step.wait()

            @block.gpsimd
            def _(pool):
                for t in range(PT):
                    for which in range(2):
                        pool.wait_ge(hot_ready, 2 * t + which + 1)
                        k = o = hot[:, t, which, :, :].rearrange("p (h m) c -> p h m c", h=PEER_HEADS)
                        ids = tif[:, t, which::2, :].unsqueeze(2).broadcast_to([P, PEER_HEADS, 16, 16])
                        pool.tensor_tensor(k, o, ids, ALU.mult).then_inc(keyed_ready, 1)

            @block.scalar
            def _(act):
                for t in range(PT):
                    act.wait_ge(shift_ready, t + 1)
                    act.activation(ex[:, t, :, :], shift[:, t, :, :], ACT.Exp).then_inc(exp_ready, 1)

            @block.tensor
            def _(pe):
                for t in range(PT):
                    pe.wait_ge(sel_ready, 3 * (t + 1))
                    for k in range(3):
                        mm = pe.transpose(ps[:, t, k * P:(k + 1) * P], sel[:, t, k, :], G.ident[:, :])
                    mm.then_inc(sel_turned, 1)

            @block.sync
            def _(sp):
                G.ws.run_ahead(sp)


def peer_table(nc, G, table, wt, spill):
    ps = G.ps
    GRP = 2
    BUFS = 4
    BANKS = 4
    TOKS = 2 * GRP
    with scope():
        second = sbuf(nc, "second_weights", [P, N_KEYS - NJ, PT * P], F32)
        hi = sbuf(nc, "hot_i", [P, BUFS, GRP, P], F32)
        hj = sbuf(nc, "hot_j", [P, BUFS, GRP, P], F32)
        steps = PT * P // GRP
        with stage(nc, "i_ready", "j_ready", "weighted", "w_ready", "w_out", "spilled") as (
                block, i_ready, j_ready, weighted, w_ready, w_out, spilled):
            @block.vector
            def _(dve):
                def step(b, base, free):
                    at = ds((base + b) * GRP, GRP)
                    if free:
                        dve.wait_ge(w_ready, base + (b - BUFS + 1))
                    dve.tensor_tensor(hj[:, b, :, :], G.iota[:, :].unsqueeze(1).broadcast_to([P, GRP, P]),
                                      table[:, 1, at].unsqueeze(2).broadcast_to([P, GRP, P]),
                                      ALU.is_equal).then_inc(j_ready, 1)
                    dve.tensor_tensor(hi[:, b, :, :], G.iota[:, :].unsqueeze(1).broadcast_to([P, GRP, P]),
                                      table[:, 0, at].unsqueeze(2).broadcast_to([P, GRP, P]),
                                      ALU.is_equal).then_inc(i_ready, 1)

                for b in range(BUFS):
                    step(b, 0, False)
                with dve.Fori(1, steps // BUFS) as it:
                    for b in range(BUFS):
                        step(b, it * BUFS, True)

            @block.gpsimd
            def _(pool):
                with pool.Fori(0, steps // BUFS) as it:
                    for b in range(BUFS):
                        pool.wait_ge(j_ready, it * BUFS + (b + 1))
                        at = ds(it * (BUFS * GRP) + b * GRP, GRP)
                        pool.tensor_tensor(hj[:, b, :, :], hj[:, b, :, :],
                                           table[:, 2, at].unsqueeze(2).broadcast_to([P, GRP, P]),
                                           ALU.mult).then_inc(weighted, 1)

            @block.tensor
            def _(pe):
                def step(s, base, free):
                    b, bank, half = s % BUFS, s // 2, s % 2
                    pe.wait_ge(i_ready, base + (s + 1))
                    pe.wait_ge(weighted, base + (s + 1))
                    if half == 0 and free is not None:
                        pe.wait_ge(w_out, free + (bank - BANKS + 1))
                    for k in range(GRP):
                        at = (half * GRP + k) * P
                        mm = pe.matmul(ps[:, bank, at:at + P], hi[:, b, k, :], hj[:, b, k, :], start=True, stop=True)
                    mm.then_inc(w_ready, 1)

                for s in range(2 * BANKS):
                    step(s, 0, None)
                with pe.Fori(1, steps // (2 * BANKS)) as it:
                    for s in range(2 * BANKS):
                        step(s, it * (2 * BANKS), it * BANKS)

            @block.scalar
            def _(act):
                with act.Fori(0, steps // (2 * BANKS)) as it:
                    for g in range(BANKS):
                        act.wait_ge(w_ready, it * (2 * BANKS) + 2 * (g + 1))
                        w = ps[:, g, :].rearrange("p (t j) -> p j t", t=TOKS)
                        at = ds(it * (BANKS * TOKS) + g * TOKS, TOKS)
                        act.activation(wt[:, :, at], w[:, 0:NJ, :], ACT.Identity)
                        act.activation(second[:, :, at], w[:, NJ:, :], ACT.Identity).then_inc(w_out, 1)

            @block.sync
            def _(sp):
                G.ws.run_ahead(sp)
                for t in range(PT):
                    sp.wait_ge(w_out, (t + 1) * P // TOKS)
                    sp.dma_start(spill[:, :, t * P:(t + 1) * P], second[:, :, t * P:(t + 1) * P]).then_inc(spilled, 16)
                sp.wait_ge(spilled, 16 * PT)


def peer_experts(nc, G, u0, hs, wt, spill):
    ps, ws = G.ps, G.ws
    SKEW = 2
    W = PT * P
    hT_h, hT_l = hs
    with scope():
        uh = sbuf(nc, "u_high", [P, 2, D], F32R)
        ul = sbuf(nc, "u_low", [P, 2, D], F32R)
        vh = sbuf(nc, "v_high", [P, 2, D], F32R)
        vl = sbuf(nc, "v_low", [P, 2, D], F32R)
        ge = sbuf(nc, "activated", [P, 2, W], F32)
        aw = sbuf(nc, "weighted", [P, W], F32)
        ah = sbuf(nc, "weighted_high", [P, 2, W], F32R)
        al = sbuf(nc, "weighted_low", [P, 2, W], F32R)
        zz = sbuf(nc, "zeros", [P, P], F32)
        with stage(nc, "zeros_set", "u_high_done", "u_split", "v_high_done", "v_split", "scored", "gelu_done", "aw_done",
                   "aw_high_done", "aw_split", "pv_done", "w_landed") as (
                block, zeros_set, uh_done, u_split, vh_done, v_split, scored, gelu_done, aw_done, ah_done, aw_split,
                pv_done, w_landed):
            def u_of(r):
                return ws.slot(u0 + r // UJ)[:, (r % UJ) * D:(r % UJ + 1) * D]

            def v_of(r):
                return ws.slot(u0 + r // UJ)[:, (UJ + r % UJ) * D:(UJ + r % UJ + 1) * D]

            def turns(eng, body):
                for r in range(BODY):
                    body(r, 0, True, False)
                with eng.Fori(1, TURNS) as it:
                    for r in range(BODY):
                        body(r, it * BODY, False, False)
                for r in range(REST):
                    body(r, TURNS * BODY, False, True)

            @block.tensor
            def _(pe):
                def scores(r, base, early):
                    pe.wait_ge(u_split, base + (r + 1))
                    if not (early and r < 3):
                        pe.wait_ge(gelu_done, base + (r - 2))
                    b, o = r % 2, ps[:, r % 3, 0:W]
                    for c in range(DC):
                        s = slice(c * P, (c + 1) * P)
                        pe.matmul(o, uh[:, b, s], hT_h[:, c, :], start=(c == 0), stop=False)
                        pe.matmul(o, uh[:, b, s], hT_l[:, c, :], start=False, stop=False)
                        mm = pe.matmul(o, ul[:, b, s], hT_h[:, c, :], start=False, stop=(c == DC - 1))
                    mm.then_inc(scored, 1)

                def products(r, base):
                    pe.wait_ge(aw_split, base + (r + 1))
                    pe.wait_ge(v_split, base + (r + 1))
                    b = r % 2
                    for t in range(PT):
                        for x, y in ((ah, vh), (ah, vl), (al, vh)):
                            for h in range(2):
                                mm = pe.matmul(ps[:, 4 + 2 * t + h, :], x[:, b, t * P:(t + 1) * P],
                                               y[:, b, h * 512:(h + 1) * 512], start=False, stop=False,
                                               skip_group_check=True)
                    mm.then_inc(pv_done, 1)

                def body(r, base, early, late):
                    if not (late and r + SKEW >= REST):
                        scores(r + SKEW, base, early)
                    products(r, base)

                pe.wait_ge(zeros_set, 1)
                for b in range(4):
                    pe.matmul(ps[:, 4 + b, :], zz[:, :], wt[:, 0:2, :].rearrange("p j t -> p (j t)"), start=True,
                              stop=False, skip_group_check=True)
                for r in range(SKEW):
                    scores(r, 0, True)
                turns(pe, body)
            for n in range(N_KEYS // UJ):
                ws.done(u0 + n, v_split, (n + 1) * UJ)

            @block.scalar
            def _(act):
                def u_high(r, base, early):
                    if r % UJ == 0:
                        n = u0 + r // UJ
                        act.wait_ge(ws.landed[n % SLOTS], landed(n, base))
                    if not (early and r < 2):
                        act.wait_ge(scored, base + (r - 1))
                    act.activation(uh[:, r % 2, :], u_of(r), ACT.Identity).then_inc(uh_done, 1)

                def landed(n, base):
                    value = 16 * (n // SLOTS + 1)
                    if isinstance(base, int):
                        return value + base // BODY * 16
                    return base // BODY * 16 + value

                def body(r, base, early, late):
                    act.wait_ge(scored, base + (r + 1))
                    if not (early and r < 2):
                        act.wait_ge(aw_done, base + (r - 1))
                    act.activation(ge[:, r % 2, :], ps[:, r % 3, 0:W], ACT.Gelu).then_inc(gelu_done, 1)
                    if not (late and r + SKEW >= REST):
                        u_high(r + SKEW, base, early)
                    if not (early and r < 2):
                        act.wait_ge(pv_done, base + (r - 1))
                    act.activation(vh[:, r % 2, :], v_of(r), ACT.Identity).then_inc(vh_done, 1)

                for r in range(SKEW):
                    u_high(r, 0, True)
                turns(act, body)

            @block.vector
            def _(dve):
                def u_low(r, base, early):
                    dve.wait_ge(uh_done, base + (r + 1))
                    if not (early and r < 2):
                        dve.wait_ge(scored, base + (r - 1))
                    dve.tensor_tensor(ul[:, r % 2, :], u_of(r), uh[:, r % 2, :].bitcast(F32),
                                      ALU.subtract).then_inc(u_split, 1)

                def body(r, base, early, late, place=0, landed=None):
                    j = place + r
                    w = wt[:, j, :] if isinstance(j, int) else wt[:, ds(j, 1), :].squeeze(1)
                    if landed is not None:
                        dve.wait_ge(w_landed, landed)
                    b = r % 2
                    dve.wait_ge(gelu_done, base + (r + 1))
                    if not (early and r < 1):
                        dve.wait_ge(aw_split, base + r)
                    dve.tensor_tensor(aw[:, :], ge[:, b, :], w, ALU.mult).then_inc(aw_done, 1)
                    if not (late and r + SKEW >= REST):
                        u_low(r + SKEW, base, early)
                    dve.wait_ge(aw_done, base + (r + 1))
                    if not (early and r < 2):
                        dve.wait_ge(pv_done, base + (r - 1))
                    dve.tensor_copy(ah[:, b, :], aw[:, :]).then_inc(ah_done, 1)
                    dve.wait_ge(ah_done, base + (r + 1))
                    dve.tensor_tensor(al[:, b, :], aw[:, :], ah[:, b, :].bitcast(F32), ALU.subtract).then_inc(aw_split, 1)
                    dve.wait_ge(vh_done, base + (r + 1))
                    dve.tensor_tensor(vl[:, b, :], v_of(r), vh[:, b, :].bitcast(F32), ALU.subtract).then_inc(v_split, 1)

                dve.memset(zz[:, :], 0.0).then_inc(zeros_set, 1)
                for r in range(SKEW):
                    u_low(r, 0, True)
                for r in range(BODY):
                    body(r, 0, True, False)
                with dve.Fori(1, FIRST_TURNS) as it:
                    for r in range(BODY):
                        body(r, it * BODY, False, False, it * BODY)
                with dve.Fori(FIRST_TURNS, TURNS) as it:
                    for r in range(BODY):
                        body(r, it * BODY, False, False, it * BODY - NJ, it * 16 - (FIRST_TURNS - 1) * 16)
                for r in range(REST):
                    body(r, TURNS * BODY, False, True, TURNS * BODY - NJ, (TURNS - FIRST_TURNS + 1) * 16)

            @block.sync
            def _(sp):
                assert ws.issued - u0 == SLOTS
                rounds = (N_KEYS // UJ - SLOTS) // SLOTS
                second_turns = TURNS - FIRST_TURNS
                src = G.d[f"peer_uv{G.layer}"]

                def turn(it):
                    for r in range(SLOTS):
                        n = u0 + SLOTS + r
                        sp.wait_ge(v_split, it * BODY + (r + 1) * UJ)
                        sp.dma_start(ws.slot(n), src[ds(it * SLOTS + (SLOTS + r), 1)].squeeze(0)).then_inc(
                            ws.landed[n % SLOTS], 16)

                with sp.Fori(0, second_turns) as it:
                    turn(it)
                    sp.wait_ge(aw_done, it * BODY + BODY)
                    at = ds(it * BODY, BODY)
                    sp.dma_start(wt[:, at, :], spill[:, at, :]).then_inc(w_landed, 16)
                at = second_turns * BODY
                sp.wait_ge(aw_done, at + REST)
                sp.dma_start(wt[:, at:at + REST, :], spill[:, at:at + REST, :]).then_inc(w_landed, 16)
                with sp.Fori(second_turns, rounds) as it:
                    turn(it)
                ws.issued += rounds * SLOTS
                ws.run_ahead(sp)
    ws.stage_over()


def peer(nc, G, layer, col, tiles, beside=lambda: None):
    ws = G.ws
    G.layer = layer
    key = f"peer{layer}{col}"
    u0 = ws.first[key]
    spill = nc.dram_tensor(f"spill_{key}", [P, N_KEYS - NJ, PT * P], F32).ap()

    def modulated(hs, loads=()):
        transpose_in(nc, G, "h2", lambda t, c: G.x[:, t, c * P:(c + 1) * P], tiles, hs,
                     scale=lambda c, _: G.mod[:, 4 * DC + c, col:col + 1], shift=lambda c, _: G.mod[:, 3 * DC + c, col:col + 1],
                     loads=loads)

    with scope():
        table = sbuf(nc, "pair_table", [P, 3, PT * P], F32)
        with scope():
            scores = sbuf(nc, "key_scores", [P, PT, 2 * PEER_HEADS, N_KEYS], F32)
            with scope():
                hs = two_parts(nc, "peer_hT", PT * P)
                keysT = sbuf(nc, "keysT", [P, 2 * PEER_HEADS, N_KEYS], F32)
                pq = sbuf(nc, "peer_q", [P, 2 * PEER_HEADS, PT * P], F32)
                modulated(hs, [(keysT[:, :, :], G.d["peer_keysT"][layer])])
                ws.make_high(nc)
                jobs = []
                for n in range(2 * PEER_HEADS):
                    w = [a.rearrange("p (c n) -> p c n", c=DC) for a in ws.parts(u0 + n // 4)]
                    jobs.append(Job(u0 + n // 4, DC, lambda c, x, w=w, n=n: w[x][:, c, (n % 4) * P:(n % 4 + 1) * P],
                                    lambda c, x: hs[x][:, c, :], P, PT * P, "vs"[n % 2], pq[:, n, :]))
                project(nc, G, "peer_q", jobs)
                jobs = []
                for t in range(PT):
                    for n in range(2 * PEER_HEADS):
                        jobs.append(Job(None, 1, lambda c, t=t, n=n: pq[:, n, t * P:(t + 1) * P],
                                        lambda c, n=n: keysT[:, n, :], P, N_KEYS, "vs"[n % 2], scores[:, t, n, :]))
                project(nc, G, "peer_s", jobs)
            with scope():
                peer_select(nc, G, layer, scores, table, beside())
        with scope():
            wt = sbuf(nc, "expert_weights", [P, NJ, PT * P], F32)
            peer_table(nc, G, table, wt, spill)
            hs = two_parts(nc, "peer_hT", PT * P)
            modulated(hs)
            peer_experts(nc, G, ws.first[f"experts{layer}{col}"], hs, wt, spill)
    with scope():
        grow = sbuf(nc, "gate_row", [P, 2, D], F32)
        gate_rows(nc, G, 5, [col], grow, banks=4)
        with_rows(nc, G, layer, 1, tiles, None, grow, banks=lambda n: 4 + 2 * n)




def chain_order(d):
    order = [(t, n) for t in range(2) for n in range(2)]
    return order if d == 0 else order[::-1]


def linear_prepare(nc, G, d, units, heads, la, qT, kT, kn, mask, qz, at, kd, etot):
    ps = G.ps
    W = units * P
    dk = P // heads
    work = [(t, u) for t in range(2) for u in range(units)]
    with scope():
        ex = sbuf(nc, "decays", [P, 2, 3 * P], F32)
        ea = sbuf(nc, "decay_after", [P, 2, W], F32)
        qr = sbuf(nc, "q_rel", [P, 2, P], F32)
        kr = sbuf(nc, "k_rel", [P, 2, P], F32)
        with stage(nc, "zeroed", "cum_ready", "after_ready", "ex_ready", "ea_ready", "rel_ready", "qz_ready", "at_ready",
                   "at_out", "kd_ready") as (
                block, zeroed, cum_ready, after_ready, ex_ready, ea_ready, rel_ready, qz_ready, at_ready, at_out, kd_ready):
            @block.tensor
            def _(pe):
                for t in range(2):
                    pe.matmul(ps[:, 2 + t, 0:W], mask[:, 2, :], la[:, t, :], start=True, stop=True).then_inc(after_ready, 1)

                def own(i):
                    pe.wait_ge(rel_ready, 2 * (i + 1))
                    if i >= 2:
                        pe.wait_ge(at_out, i - 1)
                    for a in range(heads):
                        mm = pe.matmul(ps[:, 4 + 2 * (i % 2) + a, 0:P], kr[a * dk:(a + 1) * dk, i % 2, :],
                                       qr[a * dk:(a + 1) * dk, i % 2, :], start=True, stop=True)
                    mm.then_inc(at_ready, 1)

                for i, (t, u) in enumerate(work):
                    if i >= 2:
                        pe.wait_ge(ex_ready, 2 * (i - 1))
                    pe.matmul(ps[:, i % 2, 0:2 * P], la[:, t, u * P:(u + 1) * P],
                              mask[:, 0:2, :].rearrange("p a b -> p (a b)"), start=True, stop=True).then_inc(cum_ready, 1)
                    if i >= 1:
                        own(i - 1)
                own(len(work) - 1)

            @block.scalar
            def _(act):
                for t in range(2):
                    act.wait_ge(after_ready, t + 1)
                    act.activation(ea[:, t, :], ps[:, 2 + t, 0:W], ACT.Exp).then_inc(ea_ready, 1)
                for i, (t, u) in enumerate(work):
                    act.wait_ge(cum_ready, i + 1)
                    if i >= 2:
                        act.wait_ge(qz_ready, i - 1)
                    act.activation(ex[:, i % 2, 0:2 * P], ps[:, i % 2, 0:2 * P], ACT.Exp).then_inc(ex_ready, 1)
                    act.activation(ex[:, i % 2, 2 * P:3 * P], ps[:, i % 2, P:2 * P], ACT.Exp, scale=-1.0).then_inc(ex_ready, 1)

            @block.gpsimd
            def _(pool):
                pool.memset(qz[:, :, :, :, :], 0.0).then_inc(zeroed, 1)

            @block.vector
            def _(dve):
                for t in range(2):
                    dve.wait_ge(ea_ready, t + 1)
                    dve.tensor_tensor(kd[:, t, :], kn[:, t, :], ea[:, t, :], ALU.mult).then_inc(kd_ready, 1)
                dve.wait_ge(zeroed, 1)

                def weights_out(i):
                    t, u = work[i]
                    dve.wait_ge(at_ready, i + 1)
                    for a in range(heads):
                        last = dve.tensor_tensor(at[:, t, u, a, :], ps[:, 4 + 2 * (i % 2) + a, 0:P], mask[:, 3, :], ALU.mult)
                    last.then_inc(at_out, 1)

                for i, (t, u) in enumerate(work):
                    e = ex[:, i % 2, :]
                    cols = slice(t * P, (t + 1) * P)
                    dve.wait_ge(ex_ready, 2 * (i + 1))
                    if i >= 2:
                        dve.wait_ge(at_ready, i - 1)
                    dve.tensor_tensor(qr[:, i % 2, :], qT[:, u, cols], e[:, P:2 * P], ALU.mult).then_inc(rel_ready, 1)
                    dve.tensor_tensor(kr[:, i % 2, :], kT[:, u, cols], e[:, 2 * P:3 * P], ALU.mult).then_inc(rel_ready, 1)
                    for n in range(2):
                        own = slice(n * CHUNK, (n + 1) * CHUNK)
                        dve.tensor_tensor(qz[:, t, u, n, own], qT[:, u, t * P + n * CHUNK:t * P + (n + 1) * CHUNK],
                                          e[:, own], ALU.mult)
                    end = CHUNK - 1 if d == 0 else 0
                    dve.tensor_copy(etot[:, t, u, :], e[:, end:P:CHUNK]).then_inc(qz_ready, 1)
                    if i >= 1:
                        weights_out(i - 1)
                weights_out(len(work) - 1)

            @block.sync
            def _(sp):
                G.ws.run_ahead(sp)


def linear_scan(nc, G, d, units, heads, dv, v, qz, at, kd, etot, state, pair_mask, out, add):
    ps = G.ps
    order = chain_order(d)
    work = [(t, u) for t in range(2) for u in range(units)]
    hv = dv // heads
    with scope():
        up = sbuf(nc, "update", [P, 2, dv], F32)
        with stage(nc, "update_ready", "update_masked", "state_ready", "o_ready", "o_out") as (
                block, update_ready, update_masked, state_ready, o_ready, o_out):
            @block.tensor
            def _(pe):
                k = 0
                for n, (t, c) in enumerate(order[:3]):
                    rows = slice(c * CHUNK, (c + 1) * CHUNK)
                    for u in range(units):
                        if k >= 4:
                            pe.wait_ge(update_masked if heads == 2 else state_ready, k - 3)
                        pe.matmul(ps[:, k % 4, 0:dv], kd[rows, t, u * P:(u + 1) * P], v[rows, t, u * dv:(u + 1) * dv],
                                  start=True, stop=True).then_inc(update_ready, 1)
                        k += 1
                pe.wait_ge(state_ready, 3 * units)
                for i, (t, u) in enumerate(work):
                    if i >= 4:
                        pe.wait_ge(o_out, i - 3)
                    o = ps[:, 4 + i % 4, 0:dv]
                    for c in range(2):
                        pe.matmul(o, qz[:, t, u, c, :], state[:, order.index((t, c)), u, :], start=(c == 0), stop=False,
                                  skip_group_check=True)
                    for a in range(heads):
                        mm = pe.matmul(o[:, a * hv:(a + 1) * hv], at[:, t, u, a, :],
                                       v[:, t, u * dv + a * hv:u * dv + (a + 1) * hv], start=False, stop=True,
                                       skip_group_check=True)
                    mm.then_inc(o_ready, 1)

            @block.vector
            def _(dve):
                k = 0
                for n, (t, c) in enumerate(order[:3]):
                    for u in range(units):
                        dve.wait_ge(update_ready, k + 1)
                        upd = ps[:, k % 4, 0:dv]
                        if heads == 2:
                            if k >= 2:
                                dve.wait_ge(state_ready, k - 1)
                            dve.tensor_tensor(up[:, k % 2, :], upd, pair_mask, ALU.mult).then_inc(update_masked, 1)
                            dve.wait_ge(update_masked, k + 1)
                            upd = up[:, k % 2, :]
                        if n >= 1:
                            dve.wait_ge(state_ready, k - units + 1)
                        dve.scalar_tensor_tensor(state[:, n + 1, u, :], state[:, n, u, :], etot[:, t, u, c:c + 1], upd,
                                                 ALU.mult, ALU.add).then_inc(state_ready, 1)
                        k += 1
                for i, (t, u) in enumerate(work):
                    dve.wait_ge(o_ready, i + 1)
                    o, src = out[:, t, u * dv:(u + 1) * dv], ps[:, 4 + i % 4, 0:dv]
                    if add:
                        dve.tensor_tensor(o, src, o, ALU.add).then_inc(o_out, 1)
                    else:
                        dve.tensor_copy(o, src).then_inc(o_out, 1)

            @block.sync
            def _(sp):
                G.ws.run_ahead(sp)


def log_sigmoid(nc, G, z, parts):
    N = len(parts)
    with scope():
        w = sbuf(nc, "ls_work", [P, N, 512], F32)
        with stage(nc, "abs_ready", "e_ready", "ln_ready", "ls_out") as (block, abs_ready, e_ready, ln_ready, ls_out):
            @block.vector
            def _(dve):
                for i, p in enumerate(parts):
                    dve.scalar_tensor_tensor(w[:, i, :], p, -1.0, p, ALU.mult, ALU.max).then_inc(abs_ready, 1)
                for i, p in enumerate(parts):
                    dve.wait_ge(ln_ready, i + 1)
                    dve.scalar_tensor_tensor(p, p, 0.0, w[:, i, :], ALU.min, ALU.subtract).then_inc(ls_out, 1)

            @block.scalar
            def _(act):
                for i in range(N):
                    act.wait_ge(abs_ready, i + 1)
                    act.activation(w[:, i, :], w[:, i, :], ACT.Exp, scale=-1.0).then_inc(e_ready, 1)
                for i in range(N):
                    act.wait_ge(e_ready, i + 1)
                    act.activation(w[:, i, :], w[:, i, :], ACT.Ln, bias=1.0).then_inc(ln_ready, 1)

            @block.sync
            def _(sp):
                G.ws.run_ahead(sp)


def context_state(nc, G, d, la, kn, v, mask, state):
    ps = G.ps
    with scope():
        e = sbuf(nc, "ctx_decay", [P, 2, 512], F32)
        with stage(nc, "after_ready", "e_ready", "kd_ready", "s_ready", "s_out") as (
                block, after_ready, e_ready, kd_ready, s_ready, s_out):
            @block.tensor
            def _(pe):
                for t in range(2):
                    later = 1 - t if (t == 0) == (d == 0) else None
                    mm = pe.matmul(ps[:, t, :], mask[:, 0, :], la[:, t, :], start=True, stop=later is None)
                    if later is not None:
                        mm = pe.matmul(ps[:, t, :], mask[:, 1, :], la[:, later, :], start=False, stop=True)
                    mm.then_inc(after_ready, 1)
                pe.wait_ge(kd_ready, 2)
                for h in range(H_C):
                    for t in range(2):
                        mm = pe.matmul(ps[:, 4 + h, 0:DV_C], e[:, t, h * P:(h + 1) * P], v[:, t, h * DV_C:(h + 1) * DV_C],
                                       start=(t == 0), stop=(t == 1))
                    mm.then_inc(s_ready, 1)

            @block.scalar
            def _(act):
                for t in range(2):
                    act.wait_ge(after_ready, t + 1)
                    act.activation(e[:, t, :], ps[:, t, :], ACT.Exp).then_inc(e_ready, 1)

            @block.vector
            def _(dve):
                for t in range(2):
                    dve.wait_ge(e_ready, t + 1)
                    dve.tensor_tensor(e[:, t, :], e[:, t, :], kn[:, t, :], ALU.mult).then_inc(kd_ready, 1)
                for h in range(H_C):
                    dve.wait_ge(s_ready, h + 1)
                    dve.tensor_copy(state[:, 0, h, :], ps[:, 4 + h, 0:DV_C]).then_inc(s_out, 1)

            @block.sync
            def _(sp):
                G.ws.run_ahead(sp)


def mixer_c(nc, G):
    ws = G.ws
    u0 = ws.first["gla_in"]
    with scope():
        o = sbuf(nc, "gla_o", [P, 2, 1024], F32)
        sg = sbuf(nc, "silu_g", [P, 2, 1024], F32)
        with scope():
            la = sbuf(nc, "log_a", [P, 2, 4, 512], F32)
            qT = sbuf(nc, "gla_qT", [P, H_C, SEQ], F32)
            kT = sbuf(nc, "gla_kT", [P, H_C, SEQ], F32)
            kn = sbuf(nc, "gla_k", [P, 4, 512], F32)
            v = sbuf(nc, "gla_v", [P, 4, 1024], F32)
            with scope():
                hT = two_parts(nc, "hT", TOK)
                low = sbuf(nc, "lowT", [GATE_RANK + 1, 2, TOK], F32)
                up = sbuf(nc, "gate_up", [GATE_RANK + 1, 2, 512], F32)
                with stage(nc, "low_set", "up_landed") as (block, low_set, up_landed):
                    @block.gpsimd
                    def _(pool):
                        pool.memset(low[:, :, :], 1.0).then_inc(low_set, 1)
                        pool.wait_ge(low_set, 1)

                    @block.sync
                    def _(sp):
                        sp.dma_start(up[:, :, :], G.d["gla_gate"]).then_inc(up_landed, 16)
                        sp.wait_ge(up_landed, 16)
                transpose_in(nc, G, "h1", lambda t, c: G.x[:, t, c * P:(c + 1) * P], [0, 1, 2, 3], hT,
                             scale=lambda c, q: G.mod[:, DC + c, q:q + 1], shift=lambda c, q: G.mod[:, c, q:q + 1])

                ws.make_high(nc)

                def unit(k, n=512):
                    return [w[:, 0:DC * n].rearrange("p (c n) -> p c n", c=DC) for w in ws.parts(u0 + k)]

                def cols(k, off, m, eng, dst, tok, n=512, scale=1.0):
                    return Job(u0 + k, DC, lambda c, x: unit(k, n)[x][:, c, off:off + m], lambda c, x: hT[x][:, c, 0:tok], m, tok, eng,
                               dst, scale=scale)

                def rows(k, t, eng, dst, func=None):
                    return Job(u0 + k, DC, lambda c, x: hT[x][:, c, t * P:(t + 1) * P], lambda c, x: unit(k)[x][:, c, :], P, 512, eng,
                               dst, func=func)
                jobs = [cols(0, h * P, P, "vs"[h % 2], qT[:, h, :], SEQ, scale=DK_C ** -0.5) for h in range(H_C)]
                jobs += [cols(1, h * P, P, "vs"[h % 2], kT[:, h, :], SEQ) for h in range(H_C)]
                jobs += [rows(1, t, "vs"[t % 2], kn[:, t, :]) for t in range(4)]
                for half in range(2):
                    jobs += [rows(2 + half, t, "vs"[t % 2], v[:, t, half * 512:(half + 1) * 512]) for t in range(4)]
                for half in range(2):
                    jobs += [rows(4 + half, t, "s", sg[:, t, half * 512:(half + 1) * 512], func=ACT.Silu) for t in range(2)]
                jobs += [cols(6, dr * 16, 16, "vs"[dr], low[0:16, dr, :], TOK, n=32) for dr in range(2)]
                project(nc, G, "gla_in", jobs)
                jobs = [Job(None, 1, lambda c, t=t, dr=dr: low[:, dr, t * P:(t + 1) * P], lambda c, dr=dr: up[:, dr, :], P,
                            512, "vs"[t % 2], la[:, dr, t, :]) for dr in range(2) for t in range(4)]
                project(nc, G, "gla_gates", jobs)
            log_sigmoid(nc, G, la, [la[:, dr, t, :] for dr in range(2) for t in range(4)])
            with scope():
                mask = sbuf(nc, "chunk_masks", [P, 2, 6, P], F32)
                qz = sbuf(nc, "qz", [P, 2, H_C, 2, P], F32)
                at = sbuf(nc, "at", [P, 2, H_C, 1, P], F32)
                kd = sbuf(nc, "kd", [P, 2, 512], F32)
                etot = sbuf(nc, "etot", [P, 2, H_C, 2], F32)
                state = sbuf(nc, "state", [P, 4, H_C, DV_C], F32)
                with stage(nc, "masks_landed") as (block, masks_landed):
                    @block.sync
                    def _(sp):
                        sp.dma_start(mask[:, :, :, :], G.d["gla_masks"]).then_inc(masks_landed, 16)
                        sp.wait_ge(masks_landed, 16)
                for dr in range(2):
                    context_state(nc, G, dr, la[:, dr, 2:4, :], kn[:, 2:4, :], v[:, 2:4, :], mask[:, dr, 4:6, :], state)
                    linear_prepare(nc, G, dr, H_C, 1, la[:, dr, 0:2, :], qT, kT, kn, mask[:, dr, 0:4, :], qz, at, kd, etot)
                    linear_scan(nc, G, dr, H_C, 1, DV_C, v, qz, at, kd, etot, state, None, o, dr == 1)
        with scope():
            catT = two_parts(nc, "catT", SEQ)
            grow = sbuf(nc, "gate_row", [P, 2, D], F32)

            def by_head(a):
                return lambda n: a[:, n, :].rearrange("p (h c) -> p h c", h=H_C)
            head_norm(nc, G, "gla", by_head(o), 2, H_C, DV_C, G.d["gla_norm_w"], by_head(sg), by_head(o), LN_EPS)
            transpose_in(nc, G, "cat", lambda t, c: o[:, t, c * P:(c + 1) * P], [0, 1], catT)
            gate_rows(nc, G, 2, [0], grow)
            ws.make_high(nc)
            with_rows(nc, G, 1, 0, [0, 1], out_project(G, ws.first["gla_out"], [0, 1], catT), grow,
                      units=[ws.first["gla_out"] + h for h in range(2)])



def rms_in(nc, G, dst, loads):
    x = G.x
    with scope():
        sq = sbuf(nc, "rms_sq", [P, 2, D], F32)
        ms = sbuf(nc, "rms_ms", [P, 2, 2], F32)
        with stage(nc, "squared", "rms_step", "ms_ready", "rms_ready", "scale_ready", "scaled",
                   loads=loads) as (
                block, squared, step_sem, ms_ready, rms_ready, scale_ready, scaled):
            @block.vector
            def _(dve):
                step = Steps(dve, step_sem)
                dve.wait_ge(squared, 2)
                dve.tensor_scalar(ms[:, :, 0], ms[:, :, 0], 1.0 / D, RMS_EPS, ALU.mult, ALU.add).then_inc(ms_ready, 1)
                dve.wait_ge(rms_ready, 1)
                dve.reciprocal(ms[:, :, 0], ms[:, :, 1]).then_inc(scale_ready, 1)
                dve.wait_ge(scale_ready, 1)
                step(dve.tensor_scalar(dst[:, 1, :], x[:, 1, :], ms[:, 1, 0:1], None, ALU.mult))
                step.wait()

            @block.scalar
            def _(act):
                for t in range(2):
                    act.activation(sq[:, t, :], x[:, t, :], ACT.Square, accum_out=ms[:, t, 0:1]).then_inc(squared, 1)
                act.wait_ge(ms_ready, 1)
                act.activation(ms[:, :, 1], ms[:, :, 0], ACT.Sqrt).then_inc(rms_ready, 1)
                act.wait_ge(scale_ready, 1)
                act.activation(dst[:, 0, :], x[:, 0, :], ACT.Identity, scale=ms[:, 0, 0:1]).then_inc(scaled, 1)

            @block.sync
            def _(sp):
                G.ws.run_ahead(sp)


def normed_T(nc, G, key, hT, loads=()):
    with scope():
        xn = sbuf(nc, "x_normed", [P, 2, D], F32)
        g = sbuf(nc, "norm_cols", [P, DC], F32)
        rms_in(nc, G, xn, [(g[:, :], G.d[key]), *loads])
        transpose_in(nc, G, "hn", lambda t, c: xn[:, t, c * P:(c + 1) * P], [0, 1], hT, scale=lambda c, q: g[:, c:c + 1])


def turn(nc, G, moves):
    ps = G.ps
    groups = [moves[i:i + 4] for i in range(0, len(moves), 4)]
    with stage(nc, "turned", "out_v", "out_s") as (block, turned, out_v, out_s):
        outs = (out_v, out_s)

        @block.tensor
        def _(pe):
            for n, g in enumerate(groups):
                if n >= 8:
                    pe.wait_ge(outs[n % 2], (n - 8) // 2 + 1)
                for k, (src, _) in enumerate(g):
                    mm = pe.transpose(ps[:, n % 8, k * P:(k + 1) * P], src, G.ident[:, :])
                mm.then_inc(turned, 1)

        @block.vector
        def _(dve):
            for n in range(0, len(groups), 2):
                dve.wait_ge(turned, n + 1)
                for k, (_, dst) in enumerate(groups[n]):
                    last = dve.tensor_copy(dst, ps[:, n % 8, k * P:(k + 1) * P])
                last.then_inc(out_v, 1)

        @block.scalar
        def _(act):
            for n in range(1, len(groups), 2):
                act.wait_ge(turned, n + 1)
                for k, (_, dst) in enumerate(groups[n]):
                    last = act.activation(dst, ps[:, n % 8, k * P:(k + 1) * P], ACT.Identity)
                last.then_inc(out_s, 1)

        @block.sync
        def _(sp):
            G.ws.run_ahead(sp)


UNITS = 2 * DN_HEADS


def conv_silu(nc, G, layer, raw, cv):
    with scope():
        cw = sbuf(nc, "conv_w", [P, 12, DN_CONV], F32)
        HALF = 6
        TAPS = DN_CONV - 1
        with stage(nc, "cw_landed", "tap0", "conv_step", "silu_out") as (block, cw_landed, tap0, conv_step, silu_out):
            @block.sync
            def _(sp):
                sp.dma_start(cw[:, :, :], G.d[f"dn_conv{layer}"]).then_inc(cw_landed, 16)
                G.ws.run_ahead(sp)

            @block.vector
            def _(dve):
                for h in range(12 // HALF):
                    for j in range(1, DN_CONV):
                        for k in range(HALF):
                            n = h * HALF + k
                            o, i, w = cv[:, n, :], raw[:, n, j:j + SEQ], cw[:, n, j:j + 1]
                            if j == 1:
                                dve.wait_ge(tap0, n + 1)
                            else:
                                dve.wait_ge(conv_step, h * HALF * TAPS + HALF * (j - 2) + k + 1)
                            dve.scalar_tensor_tensor(o, i, w, o, ALU.mult, ALU.add).then_inc(conv_step, 1)

            @block.scalar
            def _(act):
                act.wait_ge(cw_landed, 16)
                for n in range(12):
                    act.activation(cv[:, n, :], raw[:, n, 0:SEQ], ACT.Identity, scale=cw[:, n, 0:1]).then_inc(tap0, 1)
                for n in range(12):
                    h, k = n // HALF, n % HALF
                    act.wait_ge(conv_step, h * HALF * TAPS + HALF * (TAPS - 1) + k + 1)
                    act.activation(cv[:, n, :], cv[:, n, :], ACT.Silu).then_inc(silu_out, 1)


def delta_gates(nc, G, layer, nat, small, rhs, m, qkd, qd, kdec, qkT):
    ps = G.ps
    with scope():
        sq = sbuf(nc, "dn_sq", [P, 2, 8, P], F32)
        ms = sbuf(nc, "dn_ms", [P, 2, 8, 2], F32)
        row = sbuf(nc, "dn_rows", [P, 2, DN_HEADS], F32)
        dm = sbuf(nc, "dn_masks", [P, 4, P], F32)
        ba = sbuf(nc, "dn_beta", [P, 2, DN_HEADS], F32)
        z = sbuf(nc, "dn_z", [P, 2, DN_HEADS], F32)
        g = sbuf(nc, "dn_g", [P, 2, DN_HEADS], F32)
        w = sbuf(nc, "dn_w", [P, 2, DN_HEADS], F32)
        ea = sbuf(nc, "dn_ea", [P, DN_HEADS], F32)
        gb = sbuf(nc, "dn_gb", [P, UNITS, P], F32)
        gc = sbuf(nc, "dn_gc", [P, 5, UNITS], F32)
        with stage(nc, "rows_landed", "dn_step", "ms_ready", "rms_ready", "z_ready", "ln_ready", "act_step", "g_ready",
                   "gc_ready", "gc_out", "eg_ready", "nat_ready") as (
                block, rows_landed, step_sem, ms_ready, rms_ready, z_ready, ln_ready, act_step, g_ready, gc_ready,
                gc_out, eg_ready, nat_ready):
            @block.sync
            def _(sp):
                sp.dma_start(row[:, 0, :], G.d["dn_a_log"][layer].partition_broadcast(P)).then_inc(rows_landed, 16)
                sp.dma_start(row[:, 1, :], G.d["dn_dt_bias"][layer].partition_broadcast(P)).then_inc(rows_landed, 16)
                sp.dma_start(dm[:, :, :], G.d["dn_masks"]).then_inc(rows_landed, 16)
                G.ws.run_ahead(sp)

            @block.scalar
            def _(act):
                act.wait_ge(rows_landed, 48)
                act.activation(ea[:, :], row[:, 0, :], ACT.Exp).then_inc(act_step, 1)
                act.activation(ba[:, :, :], small[:, :, 64:68], ACT.Sigmoid).then_inc(act_step, 1)
                act.wait_ge(z_ready, 1)
                act.activation(w[:, :, :], w[:, :, :], ACT.Exp, scale=-1.0).then_inc(act_step, 1)
                act.wait_ge(act_step, 3)
                act.activation(w[:, :, :], w[:, :, :], ACT.Ln, bias=1.0).then_inc(ln_ready, 1)
                act.wait_ge(ms_ready, 1)
                act.activation(ms[:, :, :, 1], ms[:, :, :, 0], ACT.Sqrt).then_inc(rms_ready, 1)
                act.wait_ge(gc_out, 1)
                act.activation(gc[:, 1, :], gc[:, 0, :], ACT.Exp).then_inc(eg_ready, 1)
                act.activation(gc[:, 4, :], gc[:, 3, :], ACT.Exp).then_inc(eg_ready, 1)

            @block.tensor
            def _(pe):
                pe.wait_ge(rows_landed, 48)
                pe.wait_ge(g_ready, 1)
                gf = g[:, :, :].rearrange("p t h -> p (t h)")
                pe.matmul(ps[:, 0, 0:UNITS], dm[:, 0, :], gf, start=True, stop=True)
                pe.matmul(ps[:, 1, 0:UNITS], G.ones[:, :], gf, start=True, stop=True).then_inc(gc_ready, 1)

            @block.vector
            def _(dve):
                step = Steps(dve, step_sem)
                dve.wait_ge(rows_landed, 48)
                step(dve.tensor_tensor(z[:, :, :], small[:, :, 68:72], row[:, 1:2, :].broadcast_to([P, 2, DN_HEADS]), ALU.add))
                step.wait()
                dve.scalar_tensor_tensor(w[:, :, :], z[:, :, :], -1.0, z[:, :, :], ALU.mult, ALU.max).then_inc(z_ready, 1)
                step(dve.tensor_tensor(sq[:, :, :, :], nat[:, :, 0:8, :], nat[:, :, 0:8, :], ALU.mult))
                dve.wait_ge(ln_ready, 1)
                step(dve.scalar_tensor_tensor(z[:, :, :], z[:, :, :], 0.0, w[:, :, :], ALU.max, ALU.add))
                step.wait()
                dve.wait_ge(act_step, 1)
                dve.scalar_tensor_tensor(g[:, :, :], z[:, :, :], -1.0, ea[:, :].unsqueeze(1).broadcast_to([P, 2, DN_HEADS]),
                                         ALU.mult, ALU.mult).then_inc(g_ready, 1)
                step(dve.tensor_reduce(ms[:, :, :, 0], sq[:, :, :, :], AX.X, ALU.add))
                step.wait()
                dve.tensor_scalar(ms[:, :, :, 0], ms[:, :, :, 0], 1e-6, None, ALU.add).then_inc(ms_ready, 1)
                dve.wait_ge(gc_ready, 1)
                step(dve.tensor_copy(gc[:, 0, :], ps[:, 0, 0:UNITS]))
                step.wait()
                dve.tensor_tensor(gc[:, 3, :], ps[:, 1, 0:UNITS], gc[:, 0, :], ALU.subtract).then_inc(gc_out, 1)
                dve.wait_ge(rms_ready, 1)
                step(dve.reciprocal(ms[:, :, :, 0], ms[:, :, :, 1]))
                step.wait()
                step(dve.tensor_scalar(ms[:, :, 0:4, 0], ms[:, :, 0:4, 0], DN_DHEAD ** -0.5, None, ALU.mult))
                step.wait()
                for t in range(2):
                    dve.tensor_tensor(nat[:, t, 0:8, :], nat[:, t, 0:8, :], ms[:, t, :, 0:1].broadcast_to([P, 8, P]),
                                      ALU.mult).then_inc(nat_ready, 1)
                dve.wait_ge(nat_ready, 2)
                dve.wait_ge(eg_ready, 2)
                dve.wait_ge(act_step, 2)
                step(dve.tensor_tensor(gc[:, 2, :], gc[:, 1, :], ba[:, :, :].rearrange("p t h -> p (t h)"), ALU.mult))
                step.wait()

                def col(k, t):
                    return gc[:, k, t * 4:(t + 1) * 4].unsqueeze(2).broadcast_to([P, 4, P])
                for t in range(2):
                    units = slice(t * 4, (t + 1) * 4)
                    step(dve.tensor_tensor(rhs[:, units, 0:P], nat[:, t, 8:12, :],
                                           ba[:, t, :].unsqueeze(2).broadcast_to([P, 4, P]), ALU.mult))
                    step(dve.tensor_tensor(rhs[:, units, P:2 * P], nat[:, t, 4:8, :], col(2, t), ALU.mult))
                    step(dve.tensor_tensor(qd[:, units, :], nat[:, t, 0:4, :], col(1, t), ALU.mult))
                    step(dve.tensor_tensor(kdec[:, units, :], nat[:, t, 4:8, :], col(4, t), ALU.mult))
                    step(dve.tensor_copy(gb[:, units, :], g[:, t, :].unsqueeze(2).broadcast_to([P, 4, P])))
                step.wait()
        turn(nc, G, [(nat[:, t, 4 * w_ + h, :], qkT[:, w_, h, t * P:(t + 1) * P])
                     for w_ in range(2) for h in range(4) for t in range(2)])
        with scope():
            dd = sbuf(nc, "dn_dist", [P, 2, 2 * P], F32)
            with stage(nc, "gb_ready", "kk_ready", "dist_ready", "decay_ready", "m_out") as (
                    block, gb_ready, kk_ready, dist_ready, decay_ready, m_out):
                @block.tensor
                def _(pe):
                    for i in range(UNITS):
                        t, h = divmod(i, 4)
                        q, k = (qkT[:, a, h, t * P:(t + 1) * P] for a in range(2))
                        if i >= 2:
                            pe.wait_ge(dist_ready, 2 * (i - 1))
                        pe.matmul(ps[:, i % 2, 0:P], gb[:, i, :], dm[:, 0, :], start=True, stop=True).then_inc(gb_ready, 1)
                        if i >= 2:
                            pe.wait_ge(m_out, 2 * (i - 1))
                        pe.matmul(ps[:, 2 + i % 2, 0:P], k, k, start=True, stop=True)
                        pe.matmul(ps[:, 2 + i % 2, P:2 * P], k, q, start=True, stop=True).then_inc(kk_ready, 1)

                @block.vector
                def _(dve):
                    for i in range(UNITS + 1):
                        if i < UNITS:
                            b = i % 2
                            dve.wait_ge(gb_ready, i + 1)
                            if i >= 2:
                                dve.wait_ge(m_out, 2 * (i - 1))
                            dve.scalar_tensor_tensor(dd[:, b, 0:P], ps[:, b, 0:P], gc[:, 0, i:i + 1], dm[:, 1, :],
                                                     ALU.subtract, ALU.max).then_inc(dist_ready, 1)
                            dve.scalar_tensor_tensor(dd[:, b, P:2 * P], ps[:, b, 0:P], gc[:, 0, i:i + 1], dm[:, 2, :],
                                                     ALU.subtract, ALU.min).then_inc(dist_ready, 1)
                        if i >= 1:
                            n = i - 1
                            b = n % 2
                            t, h = divmod(n, 4)
                            dve.wait_ge(decay_ready, 2 * (n + 1))
                            dve.wait_ge(kk_ready, n + 1)
                            dve.scalar_tensor_tensor(m[:, n, :], ps[:, 2 + b, 0:P], ba[:, t, h:h + 1], dd[:, b, 0:P],
                                                     ALU.mult, ALU.mult).then_inc(m_out, 1)
                            dve.tensor_tensor(qkd[:, n, :], ps[:, 2 + b, P:2 * P], dd[:, b, P:2 * P], ALU.mult).then_inc(m_out, 1)

                @block.scalar
                def _(act):
                    for i in range(UNITS):
                        b = i % 2
                        act.wait_ge(dist_ready, 2 * (i + 1))
                        act.activation(dd[:, b, 0:P], dd[:, b, 0:P], ACT.Exp, scale=-1.0).then_inc(decay_ready, 1)
                        act.activation(dd[:, b, P:2 * P], dd[:, b, P:2 * P], ACT.Exp).then_inc(decay_ready, 1)

                @block.sync
                def _(sp):
                    G.ws.run_ahead(sp)


def delta_solve(nc, G, m, blocks, rhs):
    ps = G.ps
    with scope():
        a = sbuf(nc, "solve_a", [P, UNITS, 2 * P], F32)
        b = sbuf(nc, "solve_b", [P, UNITS, 2 * P], F32)
        c = sbuf(nc, "solve_c", [P, UNITS, 2 * P], F32)
        last = sbuf(nc, "solve_last", [P, UNITS, P], F32)
        GROUPS, GU = 2, UNITS // 2
        with stage(nc, "d_set", "pe_done_0", "pe_done_1", "dve_done_0", "dve_done_1") as (block, d_set, *sems):
            pe_done, dve_done = sems[0:GROUPS], sems[GROUPS:]
            def halves(x):
                return x[:, :, 0:P], x[:, :, P:2 * P]
            (d1, d1T), (d2, d2T), (d4, d4T) = halves(a), halves(b), halves(c)
            x1 = rhs[:, :, 2 * P:3 * P]
            _, x1T = halves(a)
            x2, x2T = halves(b)

            @block.tensor
            def _(pe):
                done = [0]

                def step(*products):
                    done[0] += 1
                    for g in range(GROUPS):
                        pe.wait_ge(dve_done[g], done[0])
                        for u in range(g * GU, (g + 1) * GU):
                            for lhsT, r, col in products:
                                if lhsT is None:
                                    mm = pe.transpose(ps[:, u, col:col + P], r[:, u, :], G.ident[:, :])
                                else:
                                    w = r.shape[2]
                                    mm = pe.matmul(ps[:, u, col:col + w], lhsT[:, u, :], r[:, u, :], start=True, stop=True)
                        mm.then_inc(pe_done[g], 1)
                both, cols = rhs[:, :, 0:3 * P], rhs[:, :, 0:2 * P]
                step((None, d1, 0))
                step((d1T, d1, 0), (d1, d1T, P))
                step((d2T, d2, 0), (d2, d2T, P))
                step((d4, d4T, 0))
                for t in (last, d4T, d2T, d1T):
                    step((t, both, 0))
                step((None, x1, 0))
                step((x1T, x1, 0), (x1, x1T, P))
                step((x2, x2T, 0))
                for t in (last, x2T, x1T):
                    step((t, cols, 0))

            @block.vector
            def _(dve):
                n = [0]

                def out(dst, w, op=None):
                    n[0] += 1
                    for g in range(GROUPS):
                        dve.wait_ge(pe_done[g], n[0])
                        own = slice(g * GU, (g + 1) * GU)
                        src = ps[:, own, 0:w]
                        if op is None:
                            ins = dve.tensor_copy(dst[:, own, :], src)
                        else:
                            ins = dve.tensor_tensor(dst[:, own, :], dst[:, own, :], src, op)
                        ins.then_inc(dve_done[g], 1)

                for g in range(GROUPS):
                    own = slice(g * GU, (g + 1) * GU)
                    dve.tensor_tensor(d1[:, own, :], m[:, own, :], blocks.unsqueeze(1).broadcast_to([P, GU, P]),
                                      ALU.mult).then_inc(d_set, 1)
                    dve.wait_ge(d_set, g + 1)
                    dve.tensor_tensor(x1[:, own, :], m[:, own, :], d1[:, own, :], ALU.subtract).then_inc(dve_done[g], 1)
                out(d1T, P)
                out(b[:, :, :], 2 * P)
                out(c[:, :, :], 2 * P)
                out(last[:, :, :], P)
                for op in (ALU.add, ALU.add, ALU.add, ALU.subtract):
                    out(rhs[:, :, :], 3 * P, op)
                out(x1T, P)
                out(b[:, :, :], 2 * P)
                out(last[:, :, :], P)
                for op in (ALU.add, ALU.add, ALU.subtract):
                    out(rhs[:, :, 0:2 * P], 2 * P, op)

            @block.sync
            def _(sp):
                G.ws.run_ahead(sp)


def delta_out(nc, G, rhs, qkd, qdT, wkT, kdec, o):
    ps = G.ps
    H = DN_HEADS
    with scope():
        s = sbuf(nc, "dn_state", [P, H, P], F32)
        u1 = sbuf(nc, "dn_u", [P, H, P], F32)
        with stage(nc, "first_ready", "first_out", "wu_ready", "u_out", "second_ready", "o_out") as (
                block, first_ready, first_out, wu_ready, u_out, second_ready, o_out):
            @block.tensor
            def _(pe):
                for h in range(H):
                    pe.matmul(ps[:, 0, h * P:(h + 1) * P], kdec[:, h, :], rhs[:, h, 0:P], start=True, stop=True)
                for h in range(H):
                    mm = pe.matmul(ps[:, 1, h * P:(h + 1) * P], qkd[:, h, :], rhs[:, h, 0:P], start=True, stop=True)
                mm.then_inc(first_ready, 1)
                pe.wait_ge(first_out, 1)
                for h in range(H):
                    mm = pe.matmul(ps[:, 2, h * P:(h + 1) * P], wkT[:, h, :], s[:, h, :], start=True, stop=True)
                mm.then_inc(wu_ready, 1)
                pe.wait_ge(u_out, 1)
                for h in range(H):
                    pe.matmul(ps[:, 3 + h, 0:P], qdT[:, h, :], s[:, h, :], start=True, stop=False)
                    mm = pe.matmul(ps[:, 3 + h, 0:P], qkd[:, H + h, :], u1[:, h, :], start=False, stop=True)
                mm.then_inc(second_ready, 1)

            @block.vector
            def _(dve):
                dve.wait_ge(first_ready, 1)
                dve.tensor_copy(s[:, :, :], ps[:, 0, :].rearrange("p (h c) -> p h c", h=H)).then_inc(first_out, 1)
                dve.tensor_copy(o[:, 0, :], ps[:, 1, :])
                dve.wait_ge(wu_ready, 1)
                dve.tensor_tensor(u1[:, :, :], rhs[:, H:2 * H, 0:P], ps[:, 2, :].rearrange("p (h c) -> p h c", h=H),
                                  ALU.subtract).then_inc(u_out, 1)
                dve.wait_ge(second_ready, 1)
                dve.tensor_copy(o[:, 1, :].rearrange("p (h c) -> p h c", h=H), ps[:, 3:7, 0:P]).then_inc(o_out, 1)

            @block.sync
            def _(sp):
                G.ws.run_ahead(sp)


def index_select(nc, G, qi, ki, small, amask):
    ps = G.ps
    with scope():
        r = sbuf(nc, "relu", [P, 2, SEQ], F32)
        acc = sbuf(nc, "index_score", [P, 2, SEQ], F32)
        wi = sbuf(nc, "index_w", [P, 2, IDX_HEADS], F32)
        top = sbuf(nc, "index_top", [P, 2, 8], F32)
        work = [(t, h) for t in range(2) for h in range(IDX_HEADS)]
        with stage(nc, "qk_ready", "relu_ready", "idx_step") as (block, qk_ready, relu_ready, step_sem):
            @block.tensor
            def _(pe):
                for i, (t, h) in enumerate(work):
                    o = (h % 2) * 64
                    pe.matmul(ps[:, i, 0:SEQ], qi[o:o + 64, h // 2, t * P:(t + 1) * P], ki[o:o + 64, :], start=True,
                              stop=True).then_inc(qk_ready, 1)

            @block.scalar
            def _(act):
                for i in range(len(work)):
                    act.wait_ge(qk_ready, i + 1)
                    if i >= 2:
                        act.wait_ge(step_sem, i)
                    act.activation(r[:, i % 2, :], ps[:, i, 0:SEQ], ACT.Relu).then_inc(relu_ready, 1)

            @block.vector
            def _(dve):
                step = Steps(dve, step_sem)
                step(dve.tensor_scalar(wi[:, :, :], small[:, :, 72:76], IDX_HEADS ** -0.5 * 64 ** -0.5, None, ALU.mult))
                for i, (t, h) in enumerate(work):
                    dve.wait_ge(relu_ready, i + 1)
                    step.wait()
                    if h == 0:
                        step(dve.tensor_scalar(acc[:, t, :], r[:, i % 2, :], wi[:, t, h:h + 1], None, ALU.mult))
                    else:
                        step(dve.scalar_tensor_tensor(acc[:, t, :], r[:, i % 2, :], wi[:, t, h:h + 1], acc[:, t, :],
                                                      ALU.mult, ALU.add))
                step.wait()
                step(dve.tensor_tensor(acc[:, :, :], acc[:, :, :], amask[:, :, :], ALU.add))
                step.wait()
                for k in range(TOPK // 8):
                    for t in range(2):
                        step(dve.max(top[:, t, :], acc[:, t, :]))
                    step.wait()
                    for t in range(2):
                        step(dve.match_replace(acc[:, t, :], top[:, t, :], acc[:, t, :], TAKEN))
                    step.wait()
                step(dve.tensor_scalar(acc[:, :, :], acc[:, :, :], TAKEN / 2, None, ALU.is_le))
                step.wait()
                step(dve.tensor_scalar(acc[:, :, :], acc[:, :, :], 1.0, -NEG, ALU.subtract, ALU.mult))
                step.wait()
                step(dve.tensor_tensor(amask[:, :, :], amask[:, :, :], acc[:, :, :], ALU.add))
                step.wait()

            @block.sync
            def _(sp):
                G.ws.run_ahead(sp)


def forget_gates(nc, G, layer, f, k):
    with scope():
        lb = sbuf(nc, "hg_lb", [P, DEPTH, SEQ], F32)
        t = sbuf(nc, "hg_t", [P, 3, SEQ], F32)
        with stage(nc, "lb_landed", "hg_step", "max_ready", "lb_exp", "sig_ready", "fg_ready", "ln_ready") as (
                block, lb_landed, step_sem, max_ready, lb_exp, sig_ready, fg_ready, ln_ready):
            @block.sync
            def _(sp):
                for n in range(DEPTH):
                    sp.dma_start(lb[:, n, :], G.d["hg_lb"][n].partition_broadcast(P)).then_inc(lb_landed, 16)
                G.ws.run_ahead(sp)

            @block.scalar
            def _(act):
                act.activation(f[:, :, :], f[:, :, :], ACT.Sigmoid).then_inc(sig_ready, 1)
                act.wait_ge(max_ready, 1)
                act.activation(lb[:, :, :], lb[:, :, :], ACT.Exp).then_inc(lb_exp, 1)
                act.wait_ge(fg_ready, 1)
                act.activation(f[:, :, :], f[:, :, :], ACT.Ln).then_inc(ln_ready, 1)

            @block.vector
            def _(dve):
                step = Steps(dve, step_sem)
                dve.wait_ge(lb_landed, 16 * DEPTH)
                step(dve.tensor_tensor(t[:, 0, :], lb[:, 0, :], lb[:, 1, :], ALU.max))
                step.wait()
                dve.tensor_tensor(lb[:, :, :], lb[:, :, :], t[:, 0:1, :].broadcast_to([P, DEPTH, SEQ]),
                                  ALU.subtract).then_inc(max_ready, 1)
                dve.wait_ge(lb_exp, 1)
                step(dve.tensor_tensor(t[:, 0, :], lb[:, 0, :], lb[:, 1, :], ALU.add))
                step.wait()
                step(dve.reciprocal(t[:, 1, :], t[:, 0, :]))
                step.wait()
                if layer == 0:
                    step(dve.memset(t[:, 0, :], 0.0))
                else:
                    step(dve.tensor_tensor(t[:, 0, :], lb[:, 1, :], t[:, 1, :], ALU.mult))
                step.wait()
                step(dve.tensor_scalar(t[:, 1, :], t[:, 0, :], -1.0, 1.0, ALU.mult, ALU.add))
                dve.wait_ge(sig_ready, 1)
                step.wait()
                step(dve.tensor_tensor(f[:, :, :], f[:, :, :], t[:, 1:2, :].broadcast_to([P, 2, SEQ]), ALU.mult))
                step.wait()
                step(dve.tensor_tensor(f[:, :, :], f[:, :, :], t[:, 0:1, :].broadcast_to([P, 2, SEQ]), ALU.add))
                step.wait()
                dve.tensor_scalar(k[:, :, :], f[:, :, :], -1.0, 1.0, ALU.mult, ALU.add).then_inc(fg_ready, 1)


def load(nc, G, *pairs):
    with stage(nc, "loaded") as (block, loaded):
        @block.sync
        def _(sp):
            for dst, src in pairs:
                sp.dma_start(dst, src).then_inc(loaded, 16)
            sp.wait_ge(loaded, 16 * len(pairs))


def mixer_2(nc, G, layer):
    ws = G.ws
    u0 = ws.first[f"in2_{layer}"]
    with scope():
        cat = sbuf(nc, "cat2", [P, 2, D], F32)
        with scope():
            sz = sbuf(nc, "silu_z", [P, 2, 512], F32)
            qbT = sbuf(nc, "sa_qT", [P, 2, SEQ], F32)
            kbT = sbuf(nc, "sa_kT", [P, SEQ], F32)
            qiT = sbuf(nc, "idx_qT", [P, 2, SEQ], F32)
            kiT = sbuf(nc, "idx_kT", [P, SEQ], F32)
            cqT = sbuf(nc, "hg_qT", [P, 2, SEQ], F32)
            cf = sbuf(nc, "hg_f", [P, 2, SEQ], F32)
            ci = sbuf(nc, "hg_i", [P, 2, SEQ], F32)
            cg = sbuf(nc, "hg_g", [P, 2, SEQ], F32)
            small = sbuf(nc, "small", [P, 2, 76], F32)
            with scope():
                cv = sbuf(nc, "dn_cv", [P, 12, SEQ], F32)
                with scope():
                    raw = sbuf(nc, "dn_raw", [P, 12, SEQ + DN_CONV - 1], F32)
                    hT = two_parts(nc, "hT", SEQ)
                    with stage(nc, "raw_set") as (block, raw_set):
                        @block.gpsimd
                        def _(pool):
                            pool.memset(raw[:, :, 0:DN_CONV - 1], 0.0).then_inc(raw_set, 1)
                            pool.wait_ge(raw_set, 1)
                    normed_T(nc, G, f"g_mix_pre{layer}", hT)

                    ws.make_high(nc)

                    def unit(k, n):
                        return [w[:, 0:DC * n].rearrange("p (c n) -> p c n", c=DC) for w in ws.parts(u0 + k)]

                    def cols(k, off, eng, dst, func=None):
                        w = unit(k, 512)
                        return Job(u0 + k, DC, lambda c, x: w[x][:, c, off:off + P], lambda c, x: hT[x][:, c, :], P, SEQ,
                                   eng, dst, func=func)

                    def rows(k, t, off, m, eng, dst, func=None, n=512):
                        w = unit(k, n)
                        return Job(u0 + k, DC, lambda c, x: hT[x][:, c, t * P:(t + 1) * P],
                                   lambda c, x: w[x][:, c, off:off + m], P, m,
                                   eng, dst, func=func)
                    jobs = []
                    for n in range(12):
                        jobs.append(cols(n // 4, (n % 4) * P, "vs"[n % 2], raw[:, n, DN_CONV - 1:DN_CONV - 1 + SEQ]))
                    jobs += [rows(3, t, 0, 512, "s", sz[:, t, :], func=ACT.Silu) for t in range(2)]
                    jobs += [cols(4, n * P, "vs"[n % 2], (qbT, qiT)[n // 2][:, n % 2, :]) for n in range(4)]
                    jobs += [cols(5, 0, "v", kbT[:, :]), cols(5, P, "v", kiT[:, :])]
                    jobs += [cols(5, (2 + n) * P, "s", cqT[:, n, :], func=ACT.Silu) for n in range(2)]
                    for t in range(2):
                        jobs += [rows(6, t, 0, SEQ, "v", cf[:, t, :]), rows(6, t, SEQ, SEQ, "s", ci[:, t, :])]
                    for t in range(2):
                        jobs += [rows(7, t, 0, SEQ, "s", cg[:, t, :], func=ACT.Silu, n=332),
                                 rows(7, t, SEQ, 76, "v", small[:, t, :], n=332)]
                    project(nc, G, "in2", jobs)
                    conv_silu(nc, G, layer, raw, cv)
                with scope():
                    rhs = sbuf(nc, "dn_rhs", [P, UNITS, 3 * P], F32)
                    m = sbuf(nc, "dn_m", [P, UNITS, P], F32)
                    qkd = sbuf(nc, "dn_qkd", [P, UNITS, P], F32)
                    qd = sbuf(nc, "dn_qd", [P, UNITS, P], F32)
                    kdec = sbuf(nc, "dn_kdec", [P, UNITS, P], F32)
                    with scope():
                        nat = sbuf(nc, "dn_nat", [P, 2, 12, P], F32)
                        qkT = sbuf(nc, "dn_qkT", [P, 2, DN_HEADS, SEQ], F32)
                        turn(nc, G, [(cv[:, n, t * P:(t + 1) * P], nat[:, t, n, :]) for t in range(2) for n in range(12)])
                        delta_gates(nc, G, layer, nat, small, rhs, m, qkd, qd, kdec, qkT)
                    with scope():
                        blocks = sbuf(nc, "dn_blocks", [P, P], F32)
                        load(nc, G, (blocks[:, :], G.d["dn_masks"][:, 3, :]))
                        delta_solve(nc, G, m, blocks[:, :], rhs)
                    with scope():
                        qdT = sbuf(nc, "dn_qdT", [P, DN_HEADS, P], F32)
                        wkT = sbuf(nc, "dn_wkT", [P, DN_HEADS, P], F32)
                        oa = sbuf(nc, "dn_o", [P, 2, 512], F32)
                        turn(nc, G, [(qd[:, 4 + h, :], qdT[:, h, :]) for h in range(4)]
                             + [(rhs[:, 4 + h, P:2 * P], wkT[:, h, :]) for h in range(4)])
                        delta_out(nc, G, rhs, qkd, qdT, wkT, kdec, oa)

                        def by_head(a, lo=0, hi=512, h=4):
                            return lambda n: a[:, n, lo:hi].rearrange("p (h c) -> p h c", h=h)
                        head_norm(nc, G, "dn", by_head(oa), 2, DN_HEADS, DN_DHEAD, G.d["dn_norm"][layer], by_head(sz),
                                  by_head(cat), RMS_EPS)
            with scope():
                amask = sbuf(nc, "key_mask", [P, 2, SEQ], F32)
                load(nc, G, (amask[:, :, :], G.d["admissible"]))
                index_select(nc, G, qiT, kiT, small, amask)
                items = []
                for t in range(2):
                    for h in range(SA_HEADS):
                        o = (h % 2) * 64
                        items.append(Item(qbT[o:o + 64, h // 2, t * P:(t + 1) * P], kbT[o:o + 64, :], SEQ, amask[:, t, :],
                                          None, [small[:, k, 0:64] for k in range(2)],
                                          cat[:, t, 512 + h * 64:512 + (h + 1) * 64]))
                attend(nc, G, items)
            with scope():
                ck = sbuf(nc, "hg_k", [P, 2, SEQ], F32)
                ckT = sbuf(nc, "hg_kT", [P, 2, SEQ], F32)
                mask = sbuf(nc, "hg_masks", [P, 5, P], F32)
                qz = sbuf(nc, "hg_qz", [P, 2, 2, 2, P], F32)
                at = sbuf(nc, "hg_at", [P, 2, 2, 2, P], F32)
                kd = sbuf(nc, "hg_kd", [P, 2, SEQ], F32)
                etot = sbuf(nc, "hg_etot", [P, 2, 2, 2], F32)
                state = sbuf(nc, "hg_state", [P, 4, 2, P], F32)
                oc = sbuf(nc, "hg_o", [P, 2, SEQ], F32)
                forget_gates(nc, G, layer, cf, ck)
                turn(nc, G, [(ck[:, t, n * P:(n + 1) * P], ckT[:, n, t * P:(t + 1) * P]) for n in range(2) for t in range(2)])
                with stage(nc, "state_set", "masks_landed") as (block, state_set, masks_landed):
                    @block.gpsimd
                    def _(pool):
                        pool.memset(state[:, 0, :, :], 0.0).then_inc(state_set, 1)
                        pool.wait_ge(state_set, 1)

                    @block.sync
                    def _(sp):
                        sp.dma_start(mask[:, :, :], G.d["hg_masks"]).then_inc(masks_landed, 16)
                        sp.wait_ge(masks_landed, 16)
                linear_prepare(nc, G, 0, 2, 2, cf, cqT, ckT, ck, mask[:, 0:4, :], qz, at, kd, etot)
                linear_scan(nc, G, 0, 2, 2, P, ci, qz, at, kd, etot, state, mask[:, 4, :], oc, False)
                head_norm(nc, G, "hg", lambda n: oc[:, n, :].rearrange("p (h c) -> p h c", h=4), 2, HG_HEADS, HG_DHEAD,
                          G.d["hg_norm"][layer], lambda n: cg[:, n, :].rearrange("p (h c) -> p h c", h=4),
                          lambda n: cat[:, n, 768:1024].rearrange("p (h c) -> p h c", h=4), RMS_EPS)
        with scope():
            catT = two_parts(nc, "catT", SEQ)
            transpose_in(nc, G, "cat", lambda t, c: cat[:, t, c * P:(c + 1) * P], [0, 1], catT)
            o0 = ws.first[f"out2_{layer}"]
            post_norm(nc, G, f"g_mix_post{layer}", out_project(G, o0, [0, 1], catT), [o0, o0 + 1])


def post_norm(nc, G, key, pre, units):
    with scope():
        row = sbuf(nc, "post_row", [P, D], F32)
        G.ws.make_high(nc)
        residual_norm(nc, G, "post", [0, 1], lambda n: 2 * n, lambda k: row[:, :], None, "rms", pre, units,
                      [(row[:, :], G.d[key].partition_broadcast(P))])


def ffn_2(nc, G, layer):
    ws, ps = G.ws, G.ps
    u0, d0 = ws.first[f"up{layer}"], ws.first[f"down{layer}"]
    with scope():
        aT_high = sbuf(nc, "ffn_act_high", [P, NF, SEQ], F32R)
        aT_low = sbuf(nc, "ffn_act_low", [P, NF, SEQ], F32R)
        BUFS = 12
        with scope():
            hT = two_parts(nc, "hT", SEQ)
            cw = sbuf(nc, "ffn_conv", [P, 2 * NF, FFN_CONV], F32)
            acc = sbuf(nc, "ffn_acc", [P, BUFS, SEQ], F32)
            normed_T(nc, G, f"g_ffn_pre{layer}", hT, [(cw[:, :, :], G.d[f"ffn_conv{layer}"])])
            ws.make_high(nc)
            NU = NF // 2
            with stage(nc, "up_ready", "tap2", "tap1", "tap0", "gelu_ready", "act_out", "act_high", "act_low", "high_done",
                       "low_done") as (
                    block, up_ready, tap2, tap1, tap0, gelu_ready, act_out, act_high, act_low, high_done, low_done):
                def product_of(k):
                    return acc[:, (4 * (k // 2) + k % 2) % BUFS, :]

                @block.tensor
                def _(pe):
                    for u in range(NU):
                        w = [a.rearrange("p (c n) -> p c n", c=DC) for a in ws.parts(u0 + u)]
                        for q in range(4):
                            k = 4 * u + q
                            if k >= 8:
                                pe.wait_ge(tap0, k - 7)
                            for c in range(DC):
                                mm = part_products(pe, ps[:, k % 8, 0:SEQ], low_done, u, c, DC,
                                                   lambda x: w[x][:, c, q * P:(q + 1) * P], lambda x: hT[x][:, c, :],
                                                   c == 0, c == DC - 1, q == 0)
                            mm.then_inc(up_ready, 1)
                        ws.done(u0 + u, up_ready, 4 * (u + 1))

                @block.scalar
                def _(act):
                    def gelu(u):
                        for q in range(2):
                            k = 4 * u + q
                            act.wait_ge(tap0, k + 1)
                            act.activation(acc[:, k % BUFS, :], acc[:, k % BUFS, :], ACT.Gelu_apprx_tanh).then_inc(gelu_ready, 1)
                    def high(u):
                        for k in range(2 * u, 2 * u + 2):
                            act.wait_ge(act_out, k + 1)
                            act.activation(aT_high[:, k, :], product_of(k), ACT.Identity).then_inc(act_high, 1)

                    def split(u):
                        ws.split_high(act, u0 + u, u, ws.release[u0 + u - 2] if u >= 2 else None, high_done)
                    split(0)
                    for u in range(NU):
                        if u + 1 < NU:
                            split(u + 1)
                        for q in range(4):
                            k = 4 * u + q
                            act.wait_ge(up_ready, k + 1)
                            if u >= 3:
                                act.wait_ge(act_low, 2 * (u - 2))
                            act.activation(acc[:, k % BUFS, :], ps[:, k % 8, 0:SEQ], ACT.Identity,
                                           scale=cw[:, k, 2:3]).then_inc(tap2, 1)
                        if u >= 1:
                            gelu(u - 1)
                        if u >= 2:
                            high(u - 2)
                    gelu(NU - 1)
                    high(NU - 2)
                    high(NU - 1)

                @block.vector
                def _(dve):
                    def product(u):
                        for q in range(2):
                            dve.wait_ge(gelu_ready, 2 * u + q + 1)
                            dve.wait_ge(tap0, 4 * u + q + 3)
                            dve.tensor_tensor(product_of(2 * u + q), product_of(2 * u + q),
                                              acc[:, (4 * u + q + 2) % BUFS, :], ALU.mult).then_inc(act_out, 1)

                    def low(u):
                        for k in range(2 * u, 2 * u + 2):
                            dve.wait_ge(act_high, k + 1)
                            dve.tensor_tensor(aT_low[:, k, :], product_of(k), aT_high[:, k, :].bitcast(F32),
                                              ALU.subtract).then_inc(act_low, 1)
                    ws.split_low(dve, u0, 0, high_done, low_done)
                    for u in range(NU):
                        if u + 1 < NU:
                            ws.split_low(dve, u0 + u + 1, u + 1, high_done, low_done)
                        for tap, before, sem in ((1, tap2, tap1), (0, tap1, tap0)):
                            for q in range(4):
                                k = 4 * u + q
                                s = 2 - tap
                                dve.wait_ge(before, k + 1)
                                dve.scalar_tensor_tensor(acc[:, k % BUFS, s:SEQ], ps[:, k % 8, 0:SEQ - s],
                                                         cw[:, k, tap:tap + 1], acc[:, k % BUFS, s:SEQ], ALU.mult,
                                                         ALU.add).then_inc(sem, 1)
                        if u >= 1:
                            product(u - 1)
                        if u >= 2:
                            low(u - 2)
                    product(NU - 1)
                    low(NU - 2)
                    low(NU - 1)

                @block.sync
                def _(sp):
                    ws.run_ahead(sp)
            ws.stage_over()

        def down(pe, y_ready, part_done, low_done):
            for h in range(2):
                for q in range(3):
                    i = 3 * h + q
                    chunks = range(8 * q, min(8 * q + 8, NF))
                    w = [a[:, 0:len(chunks) * 512].rearrange("p (c n) -> p c n", n=512) for a in ws.parts(d0 + i)]
                    for t in range(2):
                        for c in chunks:
                            mm = part_products(pe, ps[:, 2 * t + h, :], low_done, i, c - 8 * q, len(chunks),
                                               lambda x: (aT_high, aT_low)[x][:, c, t * P:(t + 1) * P],
                                               lambda x: w[x][:, c - 8 * q, :], c == 0, c == NF - 1, t == 0)
                        if (h, q) == (1, 2):
                            mm.then_inc(y_ready, 1)
                            ws.done(d0 + i, y_ready, t + 1)
                    if (h, q) != (1, 2):
                        mm.then_inc(part_done, 1)
                        ws.done(d0 + i, part_done, i + 1)
        post_norm(nc, G, f"g_ffn_post{layer}", down, [d0 + i for i in range(6)])



class Shared:
    pass


def make_shared(nc, dram):
    G = Shared()
    G.d = dram
    G.ident = sbuf(nc, "ident", [P, P], F32)
    G.ones = sbuf(nc, "ones", [P, P], F32)
    G.iota = sbuf(nc, "iota", [P, P], F32)
    G.x = sbuf(nc, "x", [P, 4, D], F32)
    G.mod = sbuf(nc, "mod", [P, 6 * DC, 2], F32)
    G.mod_next = sbuf(nc, "mod_next", [P, 6 * DC, 2], F32)
    G.sc = sbuf(nc, "silu_c", [P, DC, PAD], F32)
    G.bias = sbuf(nc, "mod_bias", [P, DEPTH, 6 * DC, 2], F32)
    G.pick = sbuf(nc, "row_picker", [P, 2], F32)
    for b in range(2):
        Sems.sets.append([nc.alloc_semaphore(f"stage_{b}_{n}") for n in range(STAGE_SEMS)])
    G.ps = nc.alloc_psum_tensor("ps", [P, 8, 512], F32)
    G.ws = Weights(nc)
    return G


def load_x(nc, G):
    with scope():
        cc = sbuf(nc, "c_cols", [P, 2, DC], F32)
        bm = sbuf(nc, "b_mod", [P, DEPTH, 6 * DC], F32)
        with stage(nc, "x_landed", "c_landed", "ones_set", "sc_zeroed", "silu_done", "bias_step") as (
                block, x_landed, c_landed, ones_set, sc_zeroed, silu_done, bias_step):
            @block.sync
            def _(sp):
                sp.dma_start(cc[:, 0, :], G.d["c"]).then_inc(c_landed, 16)
                sp.dma_start(cc[:, 1, :], G.d["c_ctx"]).then_inc(c_landed, 16)
                for layer in range(DEPTH):
                    sp.dma_start(bm[:, layer, :], G.d[f"b_mod{layer}"]).then_inc(c_landed, 16)
                sp.dma_start(G.pick[:, :], G.d["pick"]).then_inc(x_landed, 16)
                sp.dma_start(G.ident[:, :], G.d["ident"]).then_inc(x_landed, 16)
                G.ws.run_ahead(sp)
                sp.dma_start(G.iota[:, :], G.d["iota"]).then_inc(x_landed, 16)
                sp.dma_start(G.x[:, 0:2, :], G.d["x"]).then_inc(x_landed, 16)
                sp.dma_start(G.x[:, 2:4, :], G.d["ctx"]).then_inc(x_landed, 16)
                sp.wait_ge(x_landed, 80)

            @block.scalar
            def _(act):
                act.wait_ge(c_landed, 16 * (2 + DEPTH))
                act.wait_ge(sc_zeroed, 1)
                act.activation(G.sc[:, :, 0:2].rearrange("p c k -> p k c"), cc[:, :, :], ACT.Silu).then_inc(silu_done, 1)

            @block.vector
            def _(dve):
                dve.memset(G.ones[:, :], 1.0).then_inc(ones_set, 1)
                dve.memset(G.sc[:, :, :], 0.0).then_inc(sc_zeroed, 1)
                dve.wait_ge(c_landed, 16 * (2 + DEPTH))
                step = Steps(dve, bias_step)
                step(dve.tensor_copy(G.bias[:, :, :, :], bm[:, :, :].unsqueeze(3).broadcast_to([P, DEPTH, 6 * DC, 2])))
                step.wait()
                for part in (1, 4):
                    v = G.bias[:, :, part * DC:(part + 1) * DC, :]
                    step(dve.tensor_scalar(v, v, 1.0, None, ALU.add))
                step.wait()


def plan_weights(G):
    ws, d = G.ws, G.d

    def blocks(name, widths):
        a, out, at = d[name], [], 0
        for w in widths:
            out.append(a[:, at:at + w])
            at += w
        return out

    for layer in range(DEPTH):
        if layer == 0:
            w_mod = blocks("w_mod0", [UNIT] * 12)
            ws.plan("mod_a", w_mod[0:4])
            ws.plan("ab_in", blocks("ab_w_in", [UNIT] * 5 + [DC * 400]))
            ws.plan("mod_b", w_mod[4:8])
            ws.plan("mod_c", w_mod[8:12])
            ws.plan("ab_out", blocks("ab_w_out", [UNIT] * 2))
        else:
            ws.plan("gla_in", blocks("gla_w_in", [UNIT] * 6 + [DC * 32]))
            ws.plan("gla_out", blocks("gla_w_out", [UNIT] * 2))
        for col in range(2 if layer == 0 else 1):
            ws.plan(f"peer{layer}{col}", blocks(f"peer_wq{layer}", [UNIT] * 4))
            if (layer, col) == (0, 1):
                ws.plan("mod_next", blocks("w_mod1", [UNIT] * 12))
            ws.plan(f"experts{layer}{col}", [d[f"peer_uv{layer}"][n] for n in range(N_KEYS // 2)])
    for layer in range(DEPTH):
        ws.plan(f"in2_{layer}", blocks(f"w_in_2{layer}", [UNIT] * 7 + [DC * 332]))
        ws.plan(f"out2_{layer}", blocks(f"w_out_2{layer}", [UNIT] * 2))
        ws.plan(f"up{layer}", blocks(f"ffn_w_up_2{layer}", [UNIT] * 11))
        ws.plan(f"down{layer}", blocks(f"ffn_w_down_2{layer}", [UNIT, UNIT, 6 * 512] * 2))


def program(nc, dram, out):
    with scope():
        G = make_shared(nc, dram)
        plan_weights(G)
        load_x(nc, G)
        with scope():
            with stage(nc, beside=Modulation(nc, G, "mod_a", 0, 0, 4, G.mod)) as (block,):
                @block.sync
                def _(sp):
                    G.ws.run_ahead(sp)
        mixer_ab(nc, G)
        peer(nc, G, 0, 0, [0, 1])
        peer(nc, G, 0, 1, [2, 3], beside=lambda: Modulation(nc, G, "mod_next", 1, 0, 12, G.mod_next))
        G.mod = G.mod_next
        mixer_c(nc, G)
        peer(nc, G, 1, 0, [0, 1])
        for layer in range(DEPTH):
            mixer_2(nc, G, layer)
            ffn_2(nc, G, layer)
        with stage(nc, "out_landed") as (block, out_landed):
            @block.sync
            def _(sp):
                sp.dma_start(out.rearrange("a (t p) d -> p (a t) d", p=P), G.x[:, 0:2, :]).then_inc(out_landed, 16)
                sp.wait_ge(out_landed, 16)



def tri(keep):
    s, t = np.arange(P)[:, None], np.arange(P)[None, :]
    return np.where(keep(s, t), 0.0, NEG).astype(np.float32)


def constants():
    f = np.float32
    c = {"ident": np.eye(P, dtype=f), "pick": np.tile(np.eye(PAD, dtype=f)[:, 0:2], (P // PAD, 1)), "iota": np.tile(np.arange(P, dtype=f), (P, 1))}
    m = np.full((P, 2, QK_WIDTH), NEG, f)
    s = np.arange(P)[:, None]
    for tile, q0, nq, at in QK_PARTS:
        pos_s = (tile % 2) * P + s
        q = np.arange(q0, q0 + nq)[None, :]
        for dr in range(2):
            if tile < 2:
                ok = pos_s <= q if dr == 0 else pos_s >= q
            else:
                own = (q - SEQ >= pos_s) if dr == 0 else (q - SEQ <= pos_s)
                ok = np.where(q < SEQ, True, own)
            m[:, dr, at:at + nq] = np.where(ok, 0.0, NEG)
    c["scan_mask"] = m
    c["row_select"] = np.ascontiguousarray(np.repeat(np.eye(H_M, dtype=f)[:, :, None], P, 2))
    wm = np.zeros((P, 2, TOK), f)
    for t in range(2):
        i, j = t * P + s, np.arange(SEQ)[None, :]
        wm[:, t, 0:SEQ] = np.where(np.abs(i - j) <= WINDOW, 0.0, NEG)
    c["window_mask"] = wm
    rows = SEQ // 64
    row = np.repeat(np.arange(rows), 64).astype(f)
    col = np.tile(np.arange(64), rows).astype(f)
    n_freq = DH_A // 4
    inv = (f(10000.0) ** (-np.arange(n_freq, dtype=f) / f(n_freq))).astype(f)
    ang = np.concatenate([row[:, None] * inv, col[:, None] * inv], -1)
    at = (np.arange(P) % DH_A) // 2
    c["rope_cos"] = np.ascontiguousarray(np.cos(ang).astype(f).T[at])
    c["rope_sin"] = np.ascontiguousarray(np.sin(ang).astype(f).T[at])
    sw = np.zeros((P, P), f)
    for i in range(0, P, 2):
        sw[i + 1, i], sw[i, i + 1] = -1.0, 1.0
    c["rope_swap"] = sw
    c["gla_masks"] = np.stack([chunk_masks(dr, 1 / GATE_TAU) for dr in range(2)], 1)
    hg = chunk_masks(0, 1.0)[:, 0:5]
    hg[:, 4] = s // HG_DHEAD == s.T // HG_DHEAD
    c["hg_masks"] = hg
    t = s.T
    c["dn_masks"] = np.stack([s <= t, np.where(t < s, 0.0, -NEG), np.where(s <= t, 0.0, NEG), s // 16 == t // 16],
                             1).astype(f)
    q = np.arange(SEQ)
    ok = q[None, :] // CHUNK <= q[:, None] // CHUNK
    c["admissible"] = np.where(ok, 0.0, NEG).astype(f).reshape(2, P, SEQ).transpose(1, 0, 2)
    return c


def chunk_masks(d, unit):
    s, t = np.arange(P)[:, None], np.arange(P)[None, :]
    if d == 1:
        s, t = P - 1 - s, P - 1 - t
    same = s // CHUNK == t // CHUNK
    mid = t // CHUNK * CHUNK + CHUNK // 2 - 1
    cum = same & (s <= t)
    rel = (same & (s > mid) & (s <= t)) * 1.0 - (same & (s <= mid) & (s > t)) * 1.0
    return np.stack([cum * unit, rel * unit, (same & (s > t)) * unit, cum * 1.0, (s > t) * unit,
                     np.full((P, P), unit)], 1).astype(np.float32)


def pack_columns(w, blocks):
    k = w.shape[0] // P
    w3 = w.reshape(k, P, w.shape[1])
    return np.ascontiguousarray(np.concatenate([w3[:, :, b].transpose(1, 0, 2).reshape(P, -1) for b in blocks], 1))


def spans(n, width=512, start=0):
    return [np.arange(a, min(a + width, start + n)) for a in range(start, start + n, width)]


def layouts(i):
    g = {k: np.asarray(v) for k, v in i.items()}
    a = {"x": g["x"][0].reshape(2, P, D).transpose(1, 0, 2), "ctx": g["ctx"][0].reshape(2, P, D).transpose(1, 0, 2),
         "c": g["c"].reshape(DC, P).T, "c_ctx": g["c_ctx"].reshape(DC, P).T,
         "ln_w": g["ln_w"].reshape(2 * DEPTH, D), "ln_b": g["ln_b"].reshape(2 * DEPTH, D)}
    for n in range(DEPTH):
        a[f"w_mod{n}"] = pack_columns(g["w_mod"][n], spans(6 * D))
        a[f"b_mod{n}"] = g["b_mod"][n].reshape(6 * DC, P).T
        a[f"peer_wq{n}"] = pack_columns(g["peer_wq"][n], spans(2048))
        u = g["peer_u"][n].reshape(N_KEYS, N_KEYS // 2, 2, DC, P).transpose(1, 4, 2, 3, 0)
        v = g["peer_v"][n].reshape(N_KEYS, N_KEYS // 2, 2, D).transpose(1, 0, 2, 3)
        a[f"peer_uv{n}"] = np.concatenate([u.reshape(N_KEYS // 2, P, 2 * D), v.reshape(N_KEYS // 2, P, 2 * D)], 2)
    a["peer_keysT"] = g["peer_keys"].reshape(DEPTH, 2 * PEER_HEADS, N_KEYS, P).transpose(0, 3, 1, 2)
    w = g["ab_w_in"][0]
    base = 2064
    ka = [np.arange(2576 + h * DH_A, 2576 + (h + 1) * DH_A) for h in (0, 0, 1, 1)]
    gates = [2048 + dr * 8 + kind * 4 + np.arange(4) for kind in range(2) for dr in range(2)]
    last = np.concatenate(ka + [np.arange(2704, 2832)] + gates)
    a["ab_w_in"] = pack_columns(w, spans(2048) + [np.arange(base, base + 512), last])
    a["ab_gate_b"] = g["ab_gate_b"][0].transpose(1, 0, 2).reshape(4, H_M).T
    a["ab_norm_w"] = g["ab_norm_w"][0]
    a["ab_sink"] = g["ab_sink"][0]
    a["ab_w_out"] = pack_columns(g["ab_w_out"][0], spans(D))
    layouts_rest(g, a)
    return a



def layouts_rest(g, a):
    a["gla_w_in"] = pack_columns(g["gla_w_in"][0], spans(3072) + [np.arange(3072, 3104)])
    up = np.concatenate([g["gla_gate_up"][0], g["gla_gate_b"][0][:, None, :]], 1)
    a["gla_gate"] = up.transpose(1, 0, 2)
    a["gla_norm_w"] = g["gla_norm_w"][0]
    a["gla_w_out"] = pack_columns(g["gla_w_out"][0], spans(D))
    r = np.arange
    k, ki = r(2312, 2376), r(2696, 2760)
    cols = [r(0, 512), r(512, 1024), r(1024, 1536), r(1536, 2048),
            np.concatenate([r(2056, 2312), r(2440, 2696)]), np.concatenate([k, k, ki, ki, r(2764, 3020)]),
            r(3020, 3532), np.concatenate([r(3532, 3788), r(2376, 2440), r(2048, 2056), r(2760, 2764)])]
    for n in range(DEPTH):
        a[f"w_in_2{n}"] = pack_columns(g["w_in_2"][n], cols)
        a[f"dn_conv{n}"] = g["dn_conv_2"][n].reshape(DN_CONV, 12, P).transpose(2, 1, 0)
        a[f"w_out_2{n}"] = pack_columns(g["w_out_2"][n], spans(D))
        for name in ("g_mix_pre", "g_ffn_pre"):
            a[f"{name}{n}"] = g[f"{name}_2"][n].reshape(DC, P).T
        for name in ("g_mix_post", "g_ffn_post"):
            a[f"{name}{n}"] = g[f"{name}_2"][n]
        tiles = [r(b + (2 * u) * P, b + (2 * u + 2) * P) for u in range(NF // 2) for b in (0, D_FF)]
        units = [np.concatenate(tiles[2 * u:2 * u + 2]) for u in range(NF // 2)]
        a[f"ffn_w_up_2{n}"] = pack_columns(g["ffn_w_up_2"][n], units)
        fc = g["ffn_conv_2"][n][:, np.concatenate(units)]
        a[f"ffn_conv{n}"] = fc.reshape(FFN_CONV, 2 * NF, P).transpose(2, 1, 0)
        w3 = g["ffn_w_down_2"][n].reshape(NF, P, 2, 512)
        a[f"ffn_w_down_2{n}"] = np.concatenate(
            [w3[q:min(q + 8, NF), :, h].transpose(1, 0, 2).reshape(P, -1) for h in range(2) for q in (0, 8, 16)], 1)
    a["dn_a_log"], a["dn_dt_bias"] = g["dn_a_log_2"], g["dn_dt_bias_2"]
    a["dn_norm"] = np.tile(g["dn_norm_2"], (1, DN_HEADS))
    a["hg_lb"] = g["hg_lb_2"]
    a["hg_norm"] = np.tile(g["hg_norm_2"], (1, HG_HEADS))

_OUTS = [((1, SEQ, D), "float32")]


def kernel(**inputs):
    import concourse.bacc as _bacc
    from concourse.bass_utils import run_bass_kernel_spmd as _run

    nc = _bacc.Bacc("TRN2", target_bir_lowering=False, num_devices=1)
    arrays, dram = {}, {}
    for name, a in {**layouts(inputs), **constants()}.items():
        a = np.ascontiguousarray(a)
        arrays[f"in_{name}"] = a
        dram[name] = nc.dram_tensor(f"in_{name}", a.shape, mybir.dt.from_np(a.dtype), kind="ExternalInput").ap()
    out = nc.dram_tensor("out_0", _OUTS[0][0], F32, kind="ExternalOutput").ap()
    program(nc, dram, out)
    r = _run(nc, [arrays], core_ids=[0])
    return r.results[0]["out_0"]
```
